# Optimizing a Trainium2 kernel written in Bass

```python
import jax, jax.numpy as jnp
from jax import lax
import numpy as np
import math

D_MODEL = 1024
BATCH = 1
SEQ = 512
DEPTH = 1

CHUNK = 64
D_SHORT = D_MODEL
D_CONF = D_MODEL
SHORT_K = 3
CONF_K = 31
D_FF = -(-8 * D_MODEL // (3 * 256)) * 256
N_MOD = 6
EPS = 1e-6
LN_EPS = 1e-5
SPLITS = (D_SHORT, 2 * D_SHORT, 3 * D_SHORT,
          3 * D_SHORT + D_CONF, 3 * D_SHORT + 2 * D_CONF,
          3 * D_SHORT + 2 * D_CONF + D_MODEL)
D_IN = 3 * D_SHORT + 2 * D_CONF + 2 * D_MODEL


def rms_norm(x, g):
    xf = x.astype(jnp.float32)
    y = xf * lax.rsqrt(jnp.mean(xf * xf, axis=-1, keepdims=True) + EPS)
    return (y * g.astype(jnp.float32)).astype(x.dtype)

def layer_norm(x, g, b):
    xf = x.astype(jnp.float32)
    mu = jnp.mean(xf, axis=-1, keepdims=True)
    var = jnp.mean(jnp.square(xf - mu), axis=-1, keepdims=True)
    y = (xf - mu) * lax.rsqrt(var + LN_EPS)
    return (y * g.astype(jnp.float32) + b.astype(jnp.float32)).astype(x.dtype)

def causal_dwconv(u, w):
    k, ch = w.shape
    return lax.conv_general_dilated(
        u, w.astype(u.dtype)[:, None, :], window_strides=(1,), padding=[(k - 1, 0)],
        dimension_numbers=('NWC', 'WIO', 'NWC'), feature_group_count=ch)

def first_inputs(seed: int = 0) -> dict:
    key = jax.random.key(seed)
    ks = jax.random.split(key, 20)
    n = jax.random.normal
    d = D_MODEL
    return {
        'x': n(ks[0], (BATCH, SEQ, d), jnp.float32),
        'c': n(ks[1], (BATCH, d), jnp.float32),
        'w_ada': n(ks[2], (DEPTH, d, N_MOD * d), jnp.float32) * (0.5 * d ** -0.5),
        'b_ada': n(ks[3], (DEPTH, N_MOD * d), jnp.float32) * 0.02,
        'norm_mix_g': 1.0 + 0.05 * n(ks[4], (DEPTH, d), jnp.float32),
        'w_in': n(ks[5], (DEPTH, d, D_IN), jnp.float32) * d ** -0.5,
        'conv_short_w': n(ks[6], (DEPTH, SHORT_K, D_SHORT), jnp.float32) * SHORT_K ** -0.5,
        'w_short_out': n(ks[7], (DEPTH, D_SHORT, d), jnp.float32) * D_SHORT ** -0.5,
        'conv_conf_w': n(ks[8], (DEPTH, CONF_K, D_CONF), jnp.float32) * CONF_K ** -0.5,
        'conv_conf_b': n(ks[9], (DEPTH, D_CONF), jnp.float32) * 0.02,
        'conf_ln_g': 1.0 + 0.05 * n(ks[10], (DEPTH, D_CONF), jnp.float32),
        'conf_ln_b': n(ks[11], (DEPTH, D_CONF), jnp.float32) * 0.02,
        'w_conf_out': n(ks[12], (DEPTH, D_CONF, d), jnp.float32) * D_CONF ** -0.5,
        'w_o': n(ks[13], (DEPTH, d, d), jnp.float32) * d ** -0.5,
        'norm_ffn_g': 1.0 + 0.05 * n(ks[14], (DEPTH, d), jnp.float32),
        'w_ffn_in': n(ks[15], (DEPTH, d, 2 * D_FF), jnp.float32) * d ** -0.5,
        'w_ffn_out': n(ks[16], (DEPTH, D_FF, d), jnp.float32) * D_FF ** -0.5,
        'final_norm_g': 1.0 + 0.05 * n(ks[17], (d,), jnp.float32),
    }

def first_block(x, c, w_ada, b_ada, norm_mix_g, w_in, conv_short_w, w_short_out,
              conv_conf_w, conv_conf_b, conf_ln_g, conf_ln_b, w_conf_out, w_o,
              norm_ffn_g, w_ffn_in, w_ffn_out, final_norm_g):
    for l in range(DEPTH):
        mod = jax.nn.silu(c) @ w_ada[l] + b_ada[l]
        sh1, sc1, g1, sh2, sc2, g2 = jnp.split(mod[:, None, :], N_MOD, axis=-1)

        h = rms_norm(x, norm_mix_g[l]) * (1.0 + sc1) + sh1
        proj = jnp.einsum('bsd,de->bse', h, w_in[l])
        b_s, c_s, v_s, v_c, gl_c, gate_br = jnp.split(proj, SPLITS[:-1], axis=-1)

        y_a = b_s * causal_dwconv(c_s * v_s, conv_short_w[l])
        y_a = jnp.einsum('bsc,cd->bsd', y_a, w_short_out[l])

        u = v_c * jax.nn.sigmoid(gl_c)
        u = causal_dwconv(u, conv_conf_w[l]) + conv_conf_b[l]
        u = jax.nn.silu(layer_norm(u, conf_ln_g[l], conf_ln_b[l]))
        y_b = jnp.einsum('bsc,cd->bsd', u, w_conf_out[l])

        g_a, g_b = jnp.split(jax.nn.sigmoid(gate_br), 2, axis=-1)
        mix = jnp.einsum('bsd,de->bse', g_a * y_a + g_b * y_b, w_o[l])
        x = x + g1 * mix

        h2 = rms_norm(x, norm_ffn_g[l]) * (1.0 + sc2) + sh2
        a, bgate = jnp.split(jnp.einsum('bsd,df->bsf', h2, w_ffn_in[l]), 2, axis=-1)
        x = x + g2 * jnp.einsum('bsf,fd->bsd', jax.nn.silu(a) * bgate, w_ffn_out[l])

    return rms_norm(x, final_norm_g)


DEPTH_2 = 2

N_A_LAYERS = DEPTH_2 // 2
N_B_LAYERS = DEPTH_2 - N_A_LAYERS

GDN_HEADS = 8
GDN_DK = 128
GDN_DV = 128
GDN_QK_WIDTH = GDN_HEADS * GDN_DK
GDN_V_WIDTH = GDN_HEADS * GDN_DV
GDN_CONV = 4
GDN_CHUNK = 64
GDN_IN_WIDTH = 2 * GDN_QK_WIDTH + 2 * GDN_V_WIDTH + 2 * GDN_HEADS

FOX_HEADS = 16
FOX_HD = 64
FOX_WIDTH = FOX_HEADS * FOX_HD
FOX_QBLOCK = 128
KV_WIDTH = 2 * FOX_WIDTH + FOX_HEADS

D_FF_2 = int(math.ceil(8 * D_MODEL / 3 / 256) * 256)

RMS_EPS = 1e-6


def rms_norm_2(x, w):
    xf = x.astype(jnp.float32)
    y = xf * lax.rsqrt(jnp.mean(xf * xf, axis=-1, keepdims=True) + RMS_EPS)
    return (y * w.astype(jnp.float32)).astype(x.dtype)

def l2_normalize(x):
    xf = x.astype(jnp.float32)
    return xf * lax.rsqrt(jnp.sum(xf * xf, axis=-1, keepdims=True) + RMS_EPS)

def causal_depthwise_conv_silu(x, w):
    k_width = w.shape[0]
    y = lax.conv_general_dilated(
        x, w[:, None, :].astype(x.dtype), window_strides=(1,), padding=[(k_width - 1, 0)],
        dimension_numbers=("NWC", "WIO", "NWC"), feature_group_count=x.shape[-1])
    return jax.nn.silu(y)

def gated_delta_rule_chunked(q, k, v, g, beta):
    b_sz, t_len, n_h, d_k = q.shape
    d_v = v.shape[-1]
    c = GDN_CHUNK
    n_c = t_len // c

    def to_chunks(a):
        return a.reshape(b_sz, n_c, c, n_h, *a.shape[3:]).swapaxes(2, 3)

    qc, kc, vc, gc, bc = map(to_chunks, (q, k, v, g, beta))
    G = jnp.cumsum(gc, axis=-1)
    causal = jnp.tril(jnp.ones((c, c), dtype=bool))
    strict = jnp.tril(jnp.ones((c, c), dtype=bool), -1)
    diff = G[..., :, None] - G[..., None, :]
    decay_mat = jnp.where(causal, jnp.exp(jnp.where(causal, diff, 0.0)), 0.0)

    kk = jnp.einsum("bnhcd,bnhsd->bnhcs", kc, kc)
    a_strict = jnp.where(strict, bc[..., :, None] * kk * decay_mat, 0.0)
    rhs = jnp.concatenate([bc[..., None] * kc * jnp.exp(G)[..., None], bc[..., None] * vc], axis=-1)
    sol = lax.linalg.triangular_solve(a_strict, rhs, left_side=True, lower=True, unit_diagonal=True)
    w_c, u_c = sol[..., :d_k], sol[..., d_k:]

    a_qk = jnp.einsum("bnhcd,bnhsd->bnhcs", qc, kc) * decay_mat
    g_last = G[..., -1]
    q_dec = qc * jnp.exp(G)[..., None]
    k_dec = kc * jnp.exp(g_last[..., None] - G)[..., None]

    xs = tuple(jnp.moveaxis(a, 1, 0) for a in (q_dec, k_dec, u_c, w_c, a_qk, jnp.exp(g_last)))

    def step(state, inp):
        qg, kd, u_i, w_i, a_i, gl = inp
        v_new = u_i - jnp.einsum("bhcd,bhde->bhce", w_i, state)
        o = jnp.einsum("bhcd,bhde->bhce", qg, state) + jnp.einsum("bhcs,bhse->bhce", a_i, v_new)
        state = state * gl[..., None, None] + jnp.einsum("bhcd,bhce->bhde", kd, v_new)
        return state, o

    s0 = jnp.zeros((b_sz, n_h, d_k, d_v), jnp.float32)
    _, o = lax.scan(step, s0, xs)
    return o.transpose(1, 0, 3, 2, 4).reshape(b_sz, t_len, n_h, d_v)

def gated_deltanet_mixer(h, w_in, conv_w, a_log, dt_bias, out_norm, w_out):
    b_sz, t_len, _ = h.shape
    proj = h @ w_in
    o1 = 2 * GDN_QK_WIDTH + GDN_V_WIDTH
    o2 = o1 + GDN_V_WIDTH
    qkv = causal_depthwise_conv_silu(proj[..., :o1], conv_w)
    z = proj[..., o1:o2].reshape(b_sz, t_len, GDN_HEADS, GDN_DV)
    b_logit = proj[..., o2:o2 + GDN_HEADS]
    a_in = proj[..., o2 + GDN_HEADS:]
    q = qkv[..., :GDN_QK_WIDTH].reshape(b_sz, t_len, GDN_HEADS, GDN_DK)
    k = qkv[..., GDN_QK_WIDTH:2 * GDN_QK_WIDTH].reshape(b_sz, t_len, GDN_HEADS, GDN_DK)
    v = qkv[..., 2 * GDN_QK_WIDTH:].reshape(b_sz, t_len, GDN_HEADS, GDN_DV).astype(jnp.float32)
    q = l2_normalize(q) * (GDN_DK ** -0.5)
    k = l2_normalize(k)
    beta = jax.nn.sigmoid(b_logit.astype(jnp.float32))
    g = -jnp.exp(a_log.astype(jnp.float32)) * jax.nn.softplus(
        a_in.astype(jnp.float32) + dt_bias.astype(jnp.float32))
    o = gated_delta_rule_chunked(q, k, v, g, beta).astype(h.dtype)
    o = rms_norm_2(o, out_norm) * jax.nn.silu(z)
    return o.reshape(b_sz, t_len, GDN_V_WIDTH) @ w_out

def shared_kv(x, kv_norm, w_kv, b_forget):
    b_sz, t_len, _ = x.shape
    kvf = rms_norm_2(x, kv_norm) @ w_kv
    k = kvf[..., :FOX_WIDTH].reshape(b_sz, t_len, FOX_HEADS, FOX_HD).transpose(0, 2, 1, 3)
    v = kvf[..., FOX_WIDTH:2 * FOX_WIDTH].reshape(b_sz, t_len, FOX_HEADS, FOX_HD).transpose(0, 2, 1, 3)
    f_logit = (kvf[..., 2 * FOX_WIDTH:] + b_forget).astype(jnp.float32)
    log_f_cum = jnp.cumsum(jax.nn.log_sigmoid(f_logit), axis=1).transpose(0, 2, 1)
    return k, v, log_f_cum

def forgetting_attention_mixer(h, w_q, w_o, k, v, log_f_cum):
    b_sz, t_len, _ = h.shape
    q = (h @ w_q).reshape(b_sz, t_len, FOX_HEADS, FOX_HD).transpose(0, 2, 1, 3)
    scale = FOX_HD ** -0.5
    outs = []
    for blk in range(t_len // FOX_QBLOCK):
        s0 = blk * FOX_QBLOCK
        e = s0 + FOX_QBLOCK
        s = jnp.einsum("bhqd,bhkd->bhqk", q[:, :, s0:e], k[:, :, :e]).astype(jnp.float32) * scale
        s = s + log_f_cum[:, :, s0:e, None] - log_f_cum[:, :, None, :e]
        mask = (s0 + jnp.arange(FOX_QBLOCK))[:, None] >= jnp.arange(e)[None, :]
        p = jax.nn.softmax(jnp.where(mask, s, -jnp.inf), axis=-1)
        outs.append(jnp.einsum("bhqk,bhkd->bhqd", p.astype(v.dtype), v[:, :, :e]))
    o = jnp.concatenate(outs, axis=2)
    return o.transpose(0, 2, 1, 3).reshape(b_sz, t_len, FOX_WIDTH) @ w_o

def swiglu(h, w_in, w_out):
    gu = h @ w_in
    return (jax.nn.silu(gu[..., :D_FF_2]) * gu[..., D_FF_2:]) @ w_out

def second_inputs(seed: int = 0) -> dict:
    key = jax.random.key(seed)
    ks = jax.random.split(key, 20)
    f32 = jnp.float32

    def w(k, shape, fan_in):
        return jax.random.normal(k, shape, f32) * (fan_in ** -0.5)

    def gain(k, shape):
        return 1.0 + 0.1 * jax.random.normal(k, shape, f32)

    x = jax.random.normal(ks[0], (BATCH, SEQ, D_MODEL), f32)
    a_init = jax.random.uniform(ks[9], (N_A_LAYERS, GDN_HEADS), f32, 1.0, 16.0)
    dt = jnp.exp(jax.random.uniform(ks[10], (N_A_LAYERS, GDN_HEADS), f32, math.log(1e-3), math.log(0.1)))
    return {
        "x": x,
        "pre_mix_norm": gain(ks[1], (DEPTH_2, D_MODEL)),
        "post_mix_norm": gain(ks[2], (DEPTH_2, D_MODEL)),
        "pre_ffn_norm": gain(ks[3], (DEPTH_2, D_MODEL)),
        "post_ffn_norm": gain(ks[4], (DEPTH_2, D_MODEL)),
        "w_ffn_in": w(ks[5], (DEPTH_2, D_MODEL, 2 * D_FF_2), D_MODEL),
        "w_ffn_out": w(ks[6], (DEPTH_2, D_FF_2, D_MODEL), D_FF_2),
        "gdn_w_in": w(ks[7], (N_A_LAYERS, D_MODEL, GDN_IN_WIDTH), D_MODEL),
        "gdn_conv": w(ks[8], (N_A_LAYERS, GDN_CONV, 2 * GDN_QK_WIDTH + GDN_V_WIDTH), GDN_CONV),
        "gdn_a_log": jnp.log(a_init),
        "gdn_dt_bias": dt + jnp.log(-jnp.expm1(-dt)),
        "gdn_out_norm": gain(ks[11], (N_A_LAYERS, GDN_DV)),
        "gdn_w_out": w(ks[12], (N_A_LAYERS, GDN_V_WIDTH, D_MODEL), GDN_V_WIDTH),
        "kv_norm": gain(ks[13], (D_MODEL,)),
        "w_kv": w(ks[14], (D_MODEL, KV_WIDTH), D_MODEL),
        "b_forget": 2.0 + 0.5 * jax.random.normal(ks[15], (FOX_HEADS,), f32),
        "fox_w_q": w(ks[16], (N_B_LAYERS, D_MODEL, FOX_WIDTH), D_MODEL),
        "fox_w_o": w(ks[17], (N_B_LAYERS, FOX_WIDTH, D_MODEL), FOX_WIDTH),
    }

def second_block(x, pre_mix_norm, post_mix_norm, pre_ffn_norm, post_ffn_norm, w_ffn_in, w_ffn_out,
              gdn_w_in, gdn_conv, gdn_a_log, gdn_dt_bias, gdn_out_norm, gdn_w_out,
              kv_norm, w_kv, b_forget, fox_w_q, fox_w_o):
    k_sh = v_sh = c_sh = None
    for layer in range(DEPTH_2):
        h = rms_norm_2(x, pre_mix_norm[layer])
        if layer < N_A_LAYERS:
            i = layer
            mix = gated_deltanet_mixer(h, gdn_w_in[i], gdn_conv[i], gdn_a_log[i], gdn_dt_bias[i],
                                       gdn_out_norm[i], gdn_w_out[i])
        else:
            i = layer - N_A_LAYERS
            if i == 0:
                k_sh, v_sh, c_sh = shared_kv(x, kv_norm, w_kv, b_forget)
            mix = forgetting_attention_mixer(h, fox_w_q[i], fox_w_o[i], k_sh, v_sh, c_sh)
        x = x + rms_norm_2(mix, post_mix_norm[layer])
        f = swiglu(rms_norm_2(x, pre_ffn_norm[layer]), w_ffn_in[layer], w_ffn_out[layer])
        x = x + rms_norm_2(f, post_ffn_norm[layer])
    return x


def setup_inputs(seed=0):
    out = dict(first_inputs(seed))
    for name, value in second_inputs(seed + 1).items():
        if name != "x":
            out[name + "_2"] = value
    return out


def reference(
    x, c, w_ada, b_ada, norm_mix_g, w_in, conv_short_w, w_short_out, conv_conf_w, conv_conf_b,
    conf_ln_g, conf_ln_b, w_conf_out, w_o, norm_ffn_g, w_ffn_in, w_ffn_out, final_norm_g,
    pre_mix_norm_2, post_mix_norm_2, pre_ffn_norm_2, post_ffn_norm_2, w_ffn_in_2, w_ffn_out_2,
    gdn_w_in_2, gdn_conv_2, gdn_a_log_2, gdn_dt_bias_2, gdn_out_norm_2, gdn_w_out_2, kv_norm_2,
    w_kv_2, b_forget_2, fox_w_q_2, fox_w_o_2,
):
    x = first_block(
        x, c, w_ada, b_ada, norm_mix_g, w_in, conv_short_w, w_short_out, conv_conf_w,
        conv_conf_b, conf_ln_g, conf_ln_b, w_conf_out, w_o, norm_ffn_g, w_ffn_in, w_ffn_out,
        final_norm_g,
    )
    return second_block(
        x, pre_mix_norm_2, post_mix_norm_2, pre_ffn_norm_2, post_ffn_norm_2, w_ffn_in_2,
        w_ffn_out_2, gdn_w_in_2, gdn_conv_2, gdn_a_log_2, gdn_dt_bias_2, gdn_out_norm_2,
        gdn_w_out_2, kv_norm_2, w_kv_2, b_forget_2, fox_w_q_2, fox_w_o_2,
    )


_drawn_inputs = setup_inputs


def setup_inputs(seed=0):
    import zlib

    import numpy as np

    out = dict(_drawn_inputs(seed))
    spreads = {}
    factors = {'conv_conf_b': 6.405, 'conf_ln_g': 4.876, 'conf_ln_b': 8.0}
    for name, (base, spread) in spreads.items():
        noise = np.random.default_rng([zlib.crc32(name.encode()), seed]).standard_normal(out[name].shape)
        drawn = base * np.exp(spread * noise) if base else spread * noise
        out[name] = __import__('jax').numpy.asarray(drawn.astype(out[name].dtype))
    for name, factor in factors.items():
        out[name] = (out[name] * factor).astype(out[name].dtype)
    return out
```

```python
from contextlib import ExitStack, contextmanager

import concourse.bass as bass
import numpy as np
from concourse import mybir

F32 = mybir.dt.float32
F32R = mybir.dt.float32r
BF16 = mybir.dt.bfloat16
ACT = mybir.ActivationFunctionType
ALU = mybir.AluOpType

P = 128
D = 1024
T = 512
KT = D // P
DFF = 2816
FT = DFF // P
RING = 4
AHEAD = 3
UNIT = 8 * P
SHORT_K, CONF_K = 3, 31
ADA_COLS = 256
ADA_BUFS = 3
ADA_CHUNKS = 6 * D // ADA_COLS
ADA_FIRST = 2 * D // ADA_COLS

PARAMS = [("norm_mix_g", 8), ("norm_ffn_g", 8), ("final_norm_g", 8), ("conv_conf_b", 8), ("conf_ln_g", 8),
          ("conf_ln_b", 8), ("c", 8), ("b_ada", 48), ("conv_short_w", 8 * SHORT_K), ("conv_conf_w", 8 * CONF_K),
          ("pre_mix_norm_2", 16), ("post_mix_norm_2", 16), ("pre_ffn_norm_2", 16), ("post_ffn_norm_2", 16),
          ("kv_norm_2", 8), ("gdn_conv_2", 24 * 4), ("gdn_out_norm_2", 1)]
PCOL, _n = {}, 0
for _name, _w in PARAMS:
    PCOL[_name] = _n
    _n += _w
NPARAM = _n

PHASES = [("conf_in", 16), ("short_in", 24), ("mix_a", 16), ("gate_b", 8), ("conf_out", 8), ("w_o", 8),
          ("ffn_in", 2 * FT), ("ffn_out", FT),
          ("gdn_qkv", 24), ("gdn_z", 8), ("gdn_out", 8), ("ffn_in_a", 2 * FT), ("ffn_out_a", FT),
          ("fox_k", 8), ("fox_v", 8), ("fox_q", 8), ("fox_o", 8), ("ffn_in_b", 2 * FT), ("ffn_out_b", FT)]
FIRST, _n = {}, 0
for _name, _w in PHASES:
    FIRST[_name] = _n
    _n += _w
UNITS = _n
COUNT = dict(PHASES)

INPUTS = [("h1", 8), ("short", 8), ("conf", 8), ("mixed", 8), ("ffn_x", 8), ("ffn_h", FT),
          ("gdn_x", 8), ("gdn_o", 8), ("ffn_x_a", 8), ("ffn_h_a", FT),
          ("kv_x", 8), ("q_x", 8), ("fox_o", 8), ("ffn_x_b", 8), ("ffn_h_b", FT)]
XR, _n = {}, 0
for _name, _w in INPUTS:
    XR[_name] = _n
    _n += _w

HEADS, DH = 8, 128
CH = 128
NCH = T // CH
LEVELS = 7
FOX_HEADS, FOX_D = 16, 64
QB = T // P
NCONST = 2 + 3 + LEVELS


BIG_BYTES = 91072


class Steps:

    def __init__(self, eng, sem):
        self.eng, self.sem, self.n, self.i, self.per = eng, sem, 0, None, 0

    @contextmanager
    def loop(self, count, per):
        start = self.n
        with self.eng.Fori(0, count) as i:
            self.i, self.per = i, per
            yield i
            assert self.n - start == per, (self.n - start, per)
        self.i, self.n = None, start + count * per

    def value(self):
        return self.n if self.i is None else self.n + self.i * self.per

    def step(self, ins):
        ins.then_inc(self.sem, 1)
        self.n += 1
        return ins

    def wait(self):
        self.eng.wait_ge(self.sem, self.value())

    def seq(self, ins):
        self.step(ins)
        self.wait()


def program(nc, xT, params, weights, ada, small_w, rows, consts, out):
    ctx = ExitStack()
    with ctx:
        def at(name, where, shape, dt=F32):
            return nc.alloc_sbuf_tensor_at(name, shape, dt, offset=where)

        place = [-(-nc.sbuf_base // 32) * 32]

        def sb(name, shape, dt=F32):
            t = at(name, place[0], shape, dt)
            place[0] += -(-int(np.prod(shape[1:])) * 4 // 32) * 32
            return t

        raw = sb("raw", [P, RING, UNIT])
        w_hi = sb("w_hi", [P, RING, UNIT], F32R)
        w_lo = sb("w_lo", [P, RING, UNIT], F32R)
        X = sb("X", [P, KT, T])
        XB = place[0]
        x_hi = sb("x_hi", [P, KT, T], F32R)
        x_lo = sb("x_lo", [P, KT, T], F32R)
        par = sb("par", [P, NPARAM])
        mod = sb("mod", [P, 48])
        gain = sb("gain", [P, 2, KT])
        silu_c = sb("silu_c", [P, KT])
        ones = sb("ones", [P, P])
        eps6 = sb("eps6", [P, 1])
        eps5 = sb("eps5", [P, 1])
        total = sb("total", [P, T])
        square = sb("square", [P, T])
        rstd = sb("rstd", [P, T])
        act_out = sb("act_out", [P, 2, T])
        tmp = sb("tmp", [P, T])
        prod_pad = sb("prod_pad", [P, 3 + T])
        ada_acc = sb("ada_acc", [P, ADA_COLS])
        tri = at("tri", place[0] - 4 * ADA_COLS, [P, 2, P])
        small_raw = at("small_raw", place[0] - 4 * ADA_COLS, [P, 2 * KT * 16])
        small_hi = sb("small_hi", [P, 2, KT, 16], F32R)
        small_lo = sb("small_lo", [P, 2, KT, 16], F32R)
        row = sb("row", [P, 32])
        tok = sb("tok", [P, 16, NCH * HEADS])
        BIG = place[0]
        assert BIG + BIG_BYTES <= nc.sbuf_usable_end, (BIG, nc.sbuf_usable_end)
        f_hi = at("f_hi", BIG, [P, FT, T], F32R)
        f_lo = at("f_lo", BIG + FT * T * 4, [P, FT, T], F32R)
        U = at("U", BIG, [P, KT, CONF_K - 1 + T])
        UC = at("UC", BIG + 17344, [P, KT, T])
        y_hi = at("y_hi", BIG + 33728, [P, KT, T], F32R)
        y_lo = at("y_lo", BIG + 50112, [P, KT, T], F32R)
        ada_w = at("ada_w", BIG + 66496, [P, ADA_BUFS, KT, ADA_COLS])
        gate = at("gate", BIG + 66496, [P, KT, T])
        mixed = U[:, :, 0:T]
        qkv = at("qkv", BIG, [P, 3 * HEADS, T])
        z_gate = at("z_gate", BIG + 49152, [P, HEADS, T])
        og_hi = at("og_hi", BIG, [P, KT, T], F32R)
        og_lo = at("og_lo", BIG + 16384, [P, KT, T], F32R)
        inv_t = [at(f"inv_t{n}", BIG + 65536 + 2048 * n, [P, NCH, CH]) for n in range(4)]
        attn = [at(f"attn{n}", BIG + 73728 + 2048 * n, [P, NCH, CH]) for n in range(4)]
        beta_v = [at(f"beta_v{n}", BIG + 81920 + 2048 * n, [P, NCH, DH]) for n in range(4)]
        inv = [at(f"inv{n}", XB + 2048 * n, [P, NCH, CH]) for n in range(2)]
        half = [at(f"half{n}", XB + 4096 + 2048 * n, [P, NCH, CH]) for n in range(2)]
        level_a = [[at(f"level_a{n}{b}", XB + 8192 + 4096 * n + 2048 * b, [P, NCH, CH]) for b in range(2)]
                   for n in range(2)]
        lower_t = [at(f"lower_t{n}", XB + 16384 + 2048 * n, [P, NCH, CH]) for n in range(2)]
        state = at("state", XB + 20480, [P, 2, DH])
        masks = at("masks", XB + 21504, [P, NCONST - 2, P], BF16)
        masks_raw = at("masks_raw", XB + 8192, [P, NCONST - 2, P])
        key_dec = [at(f"key_dec{n}", XB + 24576 + 2048 * n, [P, NCH, DH]) for n in range(4)]
        new_v_sb = [tmp[:, n * P:(n + 1) * P] for n in range(2)]
        rest_sb = [tmp[:, (2 + n) * P:(3 + n) * P] for n in range(2)]
        mix = at("mix", XB, [P, KT, T])
        kf = at("kf", BIG, [P, KT, T])
        vt = at("vt", BIG + 16384, [P, QB, D])
        qf = at("qf", BIG + 32768, [P, KT, T])
        q_hi = at("q_hi", BIG + 49152, [P, KT, T], F32R)
        q_lo = at("q_lo", BIG + 65536, [P, KT, T], F32R)
        score = [at(f"score{n}", XB + 2048 * n, [P, T]) for n in range(2)]
        prob = [at(f"prob{n}", XB + 4096 + 2048 * n, [P, T]) for n in range(2)]
        prob_t = [at(f"prob_t{n}", XB + 8192 + 2048 * n, [P, QB, P]) for n in range(2)]
        forget = [at(f"forget{n}", XB + 12288 + 2048 * n, [P, T]) for n in range(2)]
        forget_sum = at("forget_sum", XB + 16384, [16, T])
        softmax = at("softmax", XB + 18432, [P, 4, 4])

        def pcol(name, j):
            return par[:, PCOL[name] + j:PCOL[name] + j + 1]

        bank = [ctx.enter_context(nc.psum_tensor(f"bank{b}", [P, T], F32)) for b in range(8)]
        stat = bank[7]
        ada_ps = bank[6]

        def sem(name):
            return ctx.enter_context(nc.semaphore(name))

        raw_landed = [sem(f"raw_landed{s}") for s in range(RING)]
        w_rounded = sem("w_rounded")
        w_split = sem("w_split")
        w_used = sem("w_used")
        bank_free = sem("bank_free")
        x_ready = sem("x_ready")
        gated = sem("gated")
        inputs_landed = sem("inputs_landed")
        consts_ready = sem("consts_ready")
        sum_ready = sem("sum_ready")
        stat_ready = sem("stat_ready")
        rstd_ready = sem("rstd_ready")
        silu_c_ready = sem("silu_c_ready")
        ada_landed = [sem(f"ada_landed{s}") for s in range(ADA_BUFS)]
        ada_used = sem("ada_used")
        ada_sum_ready = sem("ada_sum_ready")
        ada_ps_ready = sem("ada_ps_ready")
        gain_ready = sem("gain_ready")
        ln_scaled = sem("ln_scaled")
        ln_silu = sem("ln_silu")
        act_steps = sem("act_steps")
        dve_steps = sem("dve_steps")
        silu_in = sem("silu_in")
        silu_out = sem("silu_out")
        sq_ready = sem("sq_ready")
        sq_summed = sem("sq_summed")
        head_rstd = sem("head_rstd")
        head_rstd_used = sem("head_rstd_used")
        tok_pe = sem("tok_pe")
        tok_act = sem("tok_act")
        tok_dve = sem("tok_dve")
        masks_landed = sem("masks_landed")
        masks_ready = sem("masks_ready")
        z_ready = sem("z_ready")
        head_products = sem("head_products")
        decay_row = sem("decay_row")
        diff_ready = sem("diff_ready")
        decay_ready = sem("decay_ready")
        head_taken = sem("head_taken")
        turned = sem("turned")
        turned_used = sem("turned_used")
        level_ready = sem("level_ready")
        first_half = sem("first_half")
        first_copied = sem("first_copied")
        second_half = sem("second_half")
        inverse_ready = sem("inverse_ready")
        ks_ready = sem("ks_ready")
        rest_ready = sem("rest_ready")
        new_v = sem("new_v")
        new_v_copied = sem("new_v_copied")
        chunk_done = sem("chunk_done")
        state_ready = sem("state_ready")
        o_copied = sem("o_copied")
        forget_row = sem("forget_row")
        forget_copied = sem("forget_copied")
        scores_done = sem("scores_done")
        scores_taken = sem("scores_taken")
        exp_done = sem("exp_done")
        prob_ready = sem("prob_ready")
        prob_turned = sem("prob_turned")
        prob_copied = sem("prob_copied")
        pv_done = sem("pv_done")
        v_free = sem("v_free")
        out_ready = sem("out_ready")
        out_stored = sem("out_stored")

        block = ctx.enter_context(nc.Block())

        @block.sync
        def _(sp):
            def load(s, u, wait):
                if wait is not None:
                    sp.wait_ge(w_split, wait)
                sp.dma_start(raw[:, s, :], weights[bass.ds(u, 1), :, :].rearrange("a p n -> (a p) n")
                             ).then_inc(raw_landed[s], 16)

            sp.dma_start(X[:], xT.rearrange("(k p) t -> p k t", p=P)).then_inc(inputs_landed, 16)
            sp.dma_start(par[:], params).then_inc(inputs_landed, 16)
            for s in range(RING):
                load(s, s, None)
            with sp.Fori(0, UNITS // RING - 1) as i:
                for s in range(RING):
                    load(s, i * RING + (RING + s), i * RING + (s + 1))
            for u in range(UNITS // RING * RING, UNITS):
                load(u % RING, u, u - RING + 1)
            sp.wait_ge(out_ready, KT)
            sp.dma_start(out.rearrange("(k p) t -> p k t", p=P), X[:]).then_inc(out_stored, 16)
            sp.wait_ge(out_stored, 16)

        @block.gpsimd
        def _(pool):
            def low(s, u1):
                pool.wait_ge(w_rounded, u1)
                nc.gpsimd.tensor_tensor(w_lo[:, s, :], raw[:, s, :], w_hi[:, s, :].bitcast(F32),
                                        ALU.subtract).then_inc(w_split, 1)

            with pool.Fori(0, UNITS // RING) as i:
                for s in range(RING):
                    low(s, i * RING + (s + 1))
            for u in range(UNITS // RING * RING, UNITS):
                low(u % RING, u + 1)

        @block.scalar
        def _(act):
            st = Steps(act, act_steps)

            def round_unit(u, i=None, per=0):
                if u + (0 if i is None else per) >= UNITS + per * (i is not None):
                    return
                s = u % RING
                if i is None:
                    landed, free = 16 * (u // RING + 1), u - RING + 1
                else:
                    landed, free = i * (16 * per // RING) + 16 * (u // RING + 1), i * per + (u - RING + 1)
                act.wait_ge(raw_landed[s], landed)
                if u >= RING or i is not None:
                    act.wait_ge(w_used, free)
                nc.scalar.activation(w_hi[:, s, :], raw[:, s, :], ACT.Copy).then_inc(w_rounded, 1)

            def rstd_of(n, scale, eps):
                act.wait_ge(stat_ready, n)
                st.seq(nc.scalar.activation(rstd[:], stat[:], ACT.Ln, bias=eps[:], scale=scale))
                nc.scalar.activation(rstd[:], rstd[:], ACT.Exp, scale=-0.5).then_inc(rstd_ready, 1)

            def gate_pairs(phase, func, which):
                u0 = FIRST[phase]
                with act.Fori(0, COUNT[phase] // 4) as i:
                    for j in range(4):
                        round_unit(u0 + j + AHEAD, i, 4)
                        if j % 2 == which:
                            act.wait_ge(w_used, i * 4 + (u0 + j + 1))
                            act.wait_ge(bank_free, i * 4 + (u0 + j // 2 * 2 + 2))
                            nc.scalar.activation(act_out[:, j // 2, :], bank[(u0 + j) % RING][:], func
                                                 ).then_inc(gated, 1)

            def round_units(phase):
                u0 = FIRST[phase]
                n = min(COUNT[phase], UNITS - AHEAD - u0)
                with act.Fori(0, n // RING) as i:
                    for j in range(RING):
                        round_unit(u0 + j + AHEAD, i, RING)
                for u in range(u0 + n // RING * RING, u0 + n):
                    round_unit(u + AHEAD)

            for n in range(AHEAD):
                round_unit(n)
            act.wait_ge(inputs_landed, 32)
            nc.scalar.activation(silu_c[:], par[:, PCOL["c"]:PCOL["c"] + 8], ACT.Silu).then_inc(silu_c_ready, 1)

            def load_ada(k):
                if k >= ADA_BUFS:
                    act.wait_ge(ada_used, k - ADA_BUFS + 1)
                act.dma_start(ada_w[:, k % ADA_BUFS, :, :], ada[k]).then_inc(ada_landed[k % ADA_BUFS], 16)

            for k in range(ADA_FIRST):
                load_ada(k)
            act.wait_ge(consts_ready, 1)
            rstd_of(1, 1.0 / D, eps6)
            gate_pairs("conf_in", ACT.Sigmoid, 1)
            u0 = FIRST["short_in"]
            with act.Fori(0, 2) as i:
                for j in range(12):
                    round_unit(u0 + j + AHEAD, i, 12)
                    if j % 3 == 0:
                        act.wait_ge(w_used, i * 12 + (u0 + j + 1))
                        act.wait_ge(bank_free, i * 12 + (u0 + j + 2))
                        nc.scalar.activation(act_out[:, (j // 3) % 2, :], bank[(u0 + j) % RING][:], ACT.Copy
                                             ).then_inc(gated, 1)
            u0 = FIRST["mix_a"]
            for j in range(16):
                round_unit(u0 + j + AHEAD)
                load_ada(ADA_FIRST + j)
                if j % 2 == 1:
                    act.wait_ge(w_used, u0 + j + 1)
                    act.wait_ge(bank_free, u0 + j // 2 * 2 + 2)
                    nc.scalar.activation(act_out[:, (j // 2) % 2, :], bank[(u0 + j) % RING][:], ACT.Sigmoid
                                         ).then_inc(gated, 1)
            round_units("gate_b")
            act.wait_ge(bank_free, FIRST["gate_b"] + 8 + RING)
            nc.scalar.activation(gate[:], gate[:], ACT.Sigmoid).then_inc(gated, 1)
            rstd_of(3, 1.0 / D, eps5)
            for m in range(KT):
                act.wait_ge(ln_scaled, m + 1)
                nc.scalar.activation(UC[:, m, :], UC[:, m, :], ACT.Silu, scale=pcol("conf_ln_g", m),
                                     bias=pcol("conf_ln_b", m)).then_inc(ln_silu, 1)
            round_units("conf_out")
            round_units("w_o")
            rstd_of(4, 1.0 / D, eps6)
            gate_pairs("ffn_in", ACT.Silu, 0)
            round_units("ffn_out")
            rstd_of(5, 1.0 / D, eps6)
            act.dma_start(small_raw[:], small_w).then_inc(inputs_landed, 16)
            act.dma_start(row[:], rows.partition_broadcast(P).rearrange("p a b -> p (a b)")).then_inc(inputs_landed, 16)
            rstd_of(6, 1.0 / D, eps6)
            u0 = FIRST["gdn_qkv"]
            with act.Fori(0, 6) as i:
                for j in range(4):
                    round_unit(u0 + j + AHEAD, i, 4)
                    act.wait_ge(silu_in, i * 4 + (j + 1))
                    t = qkv[:, bass.ds(i * 4 + j, 1), :].rearrange("p a t -> p (a t)")
                    nc.scalar.activation(t, t, ACT.Silu).then_inc(silu_out, 1)

            def head_rstd_of(r, scale):
                act.wait_ge(sq_summed, r + 1)
                if r >= 2:
                    act.wait_ge(head_rstd_used, r - 1)
                b = act_out[:, r % 2, :]
                st.seq(nc.scalar.activation(b, bank[4 + r % 2][:], ACT.Ln, bias=eps6[:], scale=scale))
                nc.scalar.activation(b, b, ACT.Exp, scale=-0.5).then_inc(head_rstd, 1)

            u0 = FIRST["gdn_z"]
            act.wait_ge(tok_dve, 1)
            act.dma_start(tri[:], consts[:, 0:2, :]).then_inc(masks_landed, 16)
            for j in range(8):
                round_unit(u0 + j + AHEAD)
                if j == 0:
                    act.wait_ge(tok_dve, 2)
                    nc.scalar.activation(tok[:, 0, :], tok[:, 0, :], ACT.Exp, scale=-1.0)
                    st.seq(nc.scalar.activation(tok[:, 2, :], tok[:, 2, :], ACT.Exp, scale=-1.0))
                    nc.scalar.activation(tok[:, 2, :], tok[:, 2, :], ACT.Ln, bias=ones[:, 0:1])
                    nc.scalar.activation(tok[:, 3, 0:8], row[:, 0:8], ACT.Exp).then_inc(tok_act, 1)
                if j == 2:
                    act.wait_ge(tok_pe, 2)
                    nc.scalar.activation(tok[:, 5, :], bank[6][:, 64:96], ACT.Exp)
                    nc.scalar.activation(tok[:, 6, :], bank[6][:, 96:128], ACT.Exp).then_inc(tok_act, 1)
                if j == 4:
                    act.wait_ge(tok_dve, 4)
                    nc.scalar.activation(tok[:, 7, :], tok[:, 7, :], ACT.Exp).then_inc(tok_act, 1)
                head_rstd_of(2 * j, 1.0)
                head_rstd_of(2 * j + 1, 1.0)
            act.wait_ge(w_used, FIRST["gdn_out"])
            act.dma_start(masks_raw[:], consts[:, 2:, :]).then_inc(masks_landed, 16)
            act.wait_ge(bank_free, FIRST["gdn_out"] + RING)
            nc.scalar.activation(z_gate[:], z_gate[:], ACT.Silu).then_inc(z_ready, 1)

            def chunk_copies(p, c, part):
                for n in range(2):
                    k = p * 8 + c * 2 + n
                    if part == 0:
                        act.wait_ge(new_v, k + 1)
                        nc.scalar.activation(new_v_sb[n], bank[n][:, P:2 * P], ACT.Copy).then_inc(new_v_copied, 1)
                    else:
                        act.wait_ge(chunk_done, k + 1)
                        nc.scalar.activation(qkv[:, 16 + 2 * p + n, c * CH:(c + 1) * CH], bank[n][:, 2 * P:3 * P],
                                             ACT.Copy).then_inc(o_copied, 1)

            for p in range(HEADS // 2 + 1):
                if p < HEADS // 2:
                    for h in (2 * p, 2 * p + 1):
                        act.wait_ge(head_products, 4 * h + 1)
                        if h:
                            act.wait_ge(head_taken, h)
                        nc.scalar.activation(rstd[:], bank[0][:], ACT.Exp).then_inc(decay_row, 1)
                        act.wait_ge(diff_ready, h + 1)
                        nc.scalar.activation(act_out[:, h % 2, :], square[:], ACT.Exp).then_inc(decay_ready, 1)
                for lv in range(LEVELS):
                    if p < HEADS // 2 and lv >= 1:
                        for n in range(2):
                            act.wait_ge(first_half, p * 14 + lv * 2 + n + 1)
                            if lv >= 2 or p >= 1:
                                act.wait_ge(second_half, p * 12 + (lv - 1) * 2 + n - 1)
                            nc.scalar.activation(half[n][:], bank[4 + 2 * n][:], ACT.Copy).then_inc(first_copied, 1)
                    if p >= 1 and lv < NCH:
                        chunk_copies(p - 1, lv, 0)
                        chunk_copies(p - 1, lv, 1)
            for h in range(HEADS):
                head_rstd_of(16 + h, 1.0 / DH)
            round_units("gdn_out")
            rstd_of(7, 1.0 / D, eps6)
            rstd_of(8, 1.0 / D, eps6)
            gate_pairs("ffn_in_a", ACT.Silu, 0)
            round_units("ffn_out_a")
            rstd_of(9, 1.0 / D, eps6)
            rstd_of(10, 1.0 / D, eps6)
            round_units("fox_k")
            round_units("fox_v")
            act.wait_ge(tok_dve, 5)
            st.seq(nc.scalar.activation(tok[:, 10:12, :], tok[:, 10:12, :], ACT.Exp, scale=-1.0))
            nc.scalar.activation(tok[:, 10:12, :], tok[:, 10:12, :], ACT.Ln, bias=ones[:, 0:1]).then_inc(tok_act, 1)
            act.wait_ge(w_used, FIRST["fox_q"])
            act.wait_ge(tok_pe, 3)
            act.dma_start(masks_raw[:], consts[:, 2:, :]).then_inc(masks_landed, 16)
            round_units("fox_q")

            def copy_prob(s):
                b = s % QB
                act.wait_ge(prob_turned, s + 1)
                if s >= 2:
                    act.wait_ge(pv_done, s - 1)
                nc.scalar.activation(prob_t[s % 2][:, 0:b + 1, :], bank[3 + s % 2][:, 0:(b + 1) * P], ACT.Copy
                                     ).then_inc(prob_copied, 1)

            STEPS = FOX_HEADS * QB
            for s in range(STEPS + 2):
                h, b = s // QB, s % QB
                if s < STEPS:
                    act.wait_ge(scores_taken, s + 1)
                    if s >= 2:
                        act.wait_ge(prob_turned, s - 1)
                    q = softmax[:, s % 2, :]
                    nc.scalar.activation(prob[s % 2][:, 0:(b + 1) * P], score[s % 2][:, 0:(b + 1) * P], ACT.Exp,
                                         scale=-1.0, bias=q[:, 0:1], accum_out=q[:, 1:2]).then_inc(exp_done, 1)
                if s >= 2:
                    copy_prob(s - 2)
            round_units("fox_o")
            rstd_of(11, 1.0 / D, eps6)
            rstd_of(12, 1.0 / D, eps6)
            gate_pairs("ffn_in_b", ACT.Silu, 0)
            round_units("ffn_out_b")
            rstd_of(13, 1.0 / D, eps6)

        @block.tensor
        def _(pe):
            def product(acc, s, t, hi, lo, k, start, stop):
                w = bass.ts(t, P)
                nc.tensor.matmul(acc, w_hi[:, s, w], hi[:, k, :], start=start, stop=False)
                nc.tensor.matmul(acc, w_hi[:, s, w], lo[:, k, :], start=False, stop=False)
                return nc.tensor.matmul(acc, w_lo[:, s, w], hi[:, k, :], start=False, stop=stop)

            def unit(u, hi, lo, ready, i=None, per=0):
                s = u % RING
                moved = 0 if i is None else i * per
                pe.wait_ge(w_split, moved + (u + 1))
                pe.wait_ge(bank_free, moved + (u + 1))
                for k in range(KT):
                    if ready is not None:
                        pe.wait_ge(x_ready, ready + k + 1)
                    last = product(bank[s][:], s, k, hi, lo, k, k == 0, k == KT - 1)
                last.then_inc(w_used, 1)

            def units(phase, hi, lo, ready):
                u0 = FIRST[phase]
                with pe.Fori(0, COUNT[phase] // RING) as i:
                    for j in range(RING):
                        unit(u0 + j, hi, lo, ready if j == 0 else None, i, RING)

            def small(which, ready):
                for c in range(NCH):
                    for k in range(KT):
                        if c == 0:
                            pe.wait_ge(x_ready, ready + k + 1)
                        for t, (x, w) in enumerate(((x_hi, small_hi), (x_hi, small_lo), (x_lo, small_hi))):
                            last = nc.tensor.matmul(bank[6][:, c * 16:(c + 1) * 16], x[:, k, bass.ts(c, P)],
                                                    w[:, which, k, :], start=k == 0 and t == 0,
                                                    stop=k == KT - 1 and t == 2)
                return last

            def ffn_out(phase, ready):
                u0 = FIRST[phase]
                for half in range(2):
                    for k2 in range(FT // 2):
                        u = u0 + half * (FT // 2) + k2
                        s = u % RING
                        pe.wait_ge(w_split, u + 1)
                        if k2 == 0:
                            pe.wait_ge(bank_free, u0 + RING)
                        if half == 0:
                            pe.wait_ge(x_ready, ready + 2 * k2 + 2)
                        for m in range(4):
                            for kk in range(2):
                                k = 2 * k2 + kk
                                last = product(bank[4 * half + m][:], s, kk * 4 + m, f_hi, f_lo, k,
                                               k == 0, k == FT - 1)
                        last.then_inc(w_used, 1)

            def sum_over_partitions(n):
                pe.wait_ge(sum_ready, n)
                nc.tensor.matmul(stat[:], ones[:], total[:], start=True, stop=True).then_inc(stat_ready, 1)

            def ada_columns(k):
                pe.wait_ge(ada_sum_ready, k + 1)
                for b in range(ADA_COLS // P):
                    last = nc.tensor.matmul(ada_ps[:, 2 * k + b:2 * k + b + 1], ada_acc[:, bass.ts(b, P)],
                                            ones[:, 0:1], start=True, stop=True)
                last.then_inc(ada_ps_ready, 1)

            pe.wait_ge(consts_ready, 1)
            sum_over_partitions(1)
            for k in range(ADA_FIRST):
                ada_columns(k)
            units("conf_in", x_hi, x_lo, 0)
            units("short_in", x_hi, x_lo, None)
            u0 = FIRST["mix_a"]
            for j in range(16):
                if j % 2 == 0:
                    unit(u0 + j, y_hi, y_lo, 8 if j == 0 else None)
                else:
                    unit(u0 + j, x_hi, x_lo, None)
                if j == 5:
                    sum_over_partitions(2)
                if j == 9:
                    sum_over_partitions(3)
                if j >= 1:
                    ada_columns(ADA_FIRST + j - 1)
            ada_columns(ADA_CHUNKS - 1)
            units("gate_b", x_hi, x_lo, None)
            units("conf_out", y_hi, y_lo, 16)
            units("w_o", x_hi, x_lo, 24)
            sum_over_partitions(4)
            units("ffn_in", x_hi, x_lo, 32)
            ffn_out("ffn_out", XR["ffn_h"])
            sum_over_partitions(5)
            sum_over_partitions(6)
            units("gdn_qkv", x_hi, x_lo, XR["gdn_x"])
            u0 = FIRST["gdn_z"]
            pe.wait_ge(tok_dve, 1)
            small(0, XR["gdn_x"]).then_inc(tok_pe, 1)

            def sum_head(r):
                pe.wait_ge(sq_ready, r + 1)
                if r >= 2:
                    pe.wait_ge(head_rstd, r - 1)
                nc.tensor.matmul(bank[4 + r % 2][:], ones[:], (square, total)[r % 2][:], start=True, stop=True
                                 ).then_inc(sq_summed, 1)

            beta, decay, upper, ident = tok[:, 0, :], tok[:, 4, :], tri[:, 0, :], tri[:, 1, :]
            for j in range(8):
                if j == 2:
                    pe.wait_ge(tok_dve, 3)
                    pe.wait_ge(masks_landed, 16)
                    nc.tensor.matmul(bank[6][:, 64:96], upper, decay, start=True, stop=True)
                    nc.tensor.matmul(bank[6][:, 96:128], ones[:], decay, start=True, stop=True
                                     ).then_inc(tok_pe, 1)
                unit(u0 + j, x_hi, x_lo, None)
                sum_head(2 * j)
                sum_head(2 * j + 1)

            def chunk_part(p, c, part):
                for n in range(2):
                    h, k = 2 * p + n, p * 8 + c * 2 + n
                    slot, cols, b = (p % 2) * 2 + n, slice(c * CH, (c + 1) * CH), bank[n]
                    if part == 0:
                        pe.wait_ge(state_ready, p * 10 + c * 2 + n + 1)
                        nc.tensor.matmul(b[:, 0:P], qkv[:, 8 + h, cols], state[:, n, :], start=True, stop=True
                                         ).then_inc(ks_ready, 1)
                    elif part == 1:
                        pe.wait_ge(rest_ready, k + 1)
                        nc.tensor.matmul(b[:, P:2 * P], inv_t[slot][:, c, :], rest_sb[n], start=True, stop=True
                                         ).then_inc(new_v, 1)
                    else:
                        pe.wait_ge(new_v_copied, k + 1)
                        if k >= 2:
                            pe.wait_ge(o_copied, k - 1)
                        nc.tensor.matmul(b[:, 2 * P:3 * P], state[:, n, :], qkv[:, h, cols], start=True, stop=False)
                        nc.tensor.matmul(b[:, 2 * P:3 * P], new_v_sb[n], attn[slot][:, c, :], start=False, stop=True)
                        nc.tensor.matmul(b[:, 3 * P:4 * P], key_dec[slot][:, c, :], new_v_sb[n], start=True,
                                         stop=True).then_inc(chunk_done, 1)

            for p in range(HEADS // 2 + 1):
                if p < HEADS // 2:
                    for h in (2 * p, 2 * p + 1):
                        if h == 0:
                            pe.wait_ge(bank_free, FIRST["gdn_out"] + RING)
                            pe.wait_ge(tok_dve, 4)
                            pe.wait_ge(head_rstd_used, 16)
                        else:
                            pe.wait_ge(head_taken, h)
                        if h >= 2 and h % 2 == 0:
                            pe.wait_ge(turned_used, 2 * h)
                            pe.wait_ge(o_copied, 0 if p < 2 else 8 * (p - 1))
                            pe.wait_ge(state_ready, 0 if p < 2 else 10 * (p - 1))
                        for c in range(NCH):
                            g = decay[:, c * HEADS + h:c * HEADS + h + 1].broadcast_to([P, P])
                            last = nc.tensor.matmul(bank[0][:, bass.ts(c, P)], g, upper, start=True, stop=True)
                        last.then_inc(head_products, 1)
                        for c in range(NCH):
                            g = beta[:, c * HEADS + h:c * HEADS + h + 1].broadcast_to([P, P])
                            last = nc.tensor.matmul(bank[1][:, bass.ts(c, P)], g, ident, start=True, stop=True)
                        last.then_inc(head_products, 1)
                        for c in range(NCH):
                            kc = qkv[:, 8 + h, bass.ts(c, P)]
                            last = nc.tensor.matmul(bank[2][:, bass.ts(c, P)], kc, kc, start=True, stop=True)
                        last.then_inc(head_products, 1)
                        for c in range(NCH):
                            last = nc.tensor.matmul(bank[3][:, bass.ts(c, P)], qkv[:, 8 + h, bass.ts(c, P)],
                                                    qkv[:, h, bass.ts(c, P)], start=True, stop=True)
                        last.then_inc(head_products, 1)
                for lv in range(LEVELS):
                    if p < HEADS // 2:
                        for n in range(2):
                            pe.wait_ge(level_ready, p * 14 + lv * 2 + n + 1)
                            if lv == 0:
                                pe.wait_ge(head_taken, 2 * p + 2)
                            else:
                                pe.wait_ge(inverse_ready, p * 14 + (lv - 1) * 2 + n + 1)
                            for c in range(NCH):
                                r = ident if lv == 0 else inv[n][:, c, :]
                                last = nc.tensor.matmul(bank[4 + 2 * n][:, bass.ts(c, P)],
                                                        level_a[n][lv % 2][:, c, :], r, start=True, stop=True)
                            last.then_inc(first_half, 1)
                    if p >= 1 and lv < NCH:
                        chunk_part(p - 1, lv, 0)
                    if p < HEADS // 2 and lv in (0, 1):
                        h = 2 * p + lv
                        for w in range(2):
                            if h >= 1:
                                pe.wait_ge(turned_used, 2 * h - 1 + w)
                            for c in range(NCH):
                                last = nc.tensor.transpose(bank[2 + w][:, bass.ts(c, P)],
                                                           qkv[:, 16 - 8 * w + h, bass.ts(c, P)], ident)
                            last.then_inc(turned, 1)
                    if p >= 1 and lv < NCH:
                        chunk_part(p - 1, lv, 1)
                    if p < HEADS // 2 and lv >= 1:
                        slot = (p % 2) * 2
                        for n in range(2):
                            pe.wait_ge(first_copied, p * 12 + (lv - 1) * 2 + n + 1)
                            if lv < LEVELS - 1:
                                for c in range(NCH):
                                    nc.tensor.matmul(bank[4 + 2 * n][:, bass.ts(c, P)], inv_t[slot + n][:, c, :],
                                                     half[n][:, c, :], start=True, stop=True)
                            for c in range(NCH):
                                last = nc.tensor.matmul(bank[5 + 2 * n][:, bass.ts(c, P)], half[n][:, c, :],
                                                        inv_t[slot + n][:, c, :], start=True, stop=True)
                            last.then_inc(second_half, 1)
                    if p >= 1 and lv < NCH:
                        chunk_part(p - 1, lv, 2)
            for r in range(16, 24):
                sum_head(r)
            units("gdn_out", og_hi, og_lo, XR["gdn_o"])
            sum_over_partitions(7)
            sum_over_partitions(8)
            units("ffn_in_a", x_hi, x_lo, XR["ffn_x_a"])
            ffn_out("ffn_out_a", XR["ffn_h_a"])
            sum_over_partitions(9)
            sum_over_partitions(10)
            units("fox_k", x_hi, x_lo, XR["kv_x"])
            small(1, XR["kv_x"]).then_inc(tok_pe, 1)
            u0 = FIRST["fox_v"]
            for hv in range(2):
                for k2 in range(KT // 2):
                    u = u0 + hv * (KT // 2) + k2
                    s = u % RING
                    pe.wait_ge(w_split, u + 1)
                    if k2 == 0:
                        pe.wait_ge(bank_free, u0 + RING)
                    for t in range(QB):
                        b = bank[4 * hv + t] if 4 * hv + t != 6 else bank[6]
                        if hv == 1 and k2 == 0 and t == 2:
                            pe.wait_ge(tok_dve, 5)
                        for kk in range(2):
                            k = 2 * k2 + kk
                            for i, (x, w) in enumerate(((x_hi, w_hi), (x_hi, w_lo), (x_lo, w_hi))):
                                last = nc.tensor.matmul(b[:], x[:, k, bass.ts(t, P)], w[:, s, bass.ts(kk, T)],
                                                        start=k == 0 and i == 0, stop=k == KT - 1 and i == 2)
                    last.then_inc(w_used, 1)
            units("fox_q", q_hi, q_lo, XR["q_x"])
            pe.wait_ge(tok_dve, 6)
            pe.wait_ge(v_free, 8)
            for c in range(NCH):
                last = nc.tensor.matmul(bank[7][0:16, bass.ts(c, P)], tok[:, 8:10, :].rearrange(
                    "p a b -> p (a b)")[:, c * 16:(c + 1) * 16], ident, start=True, stop=True)
            last.then_inc(tok_pe, 1)
            pe.wait_ge(masks_ready, 2)
            pe.wait_ge(bank_free, FIRST["fox_o"] + RING)
            STEPS = FOX_HEADS * QB

            def forget_on_partitions(h):
                pe.wait_ge(tok_dve, 7) if h == 0 else pe.wait_ge(forget_copied, h)
                pick = tri[0:16, 1, h:h + 1].broadcast_to([16, P])
                nc.tensor.matmul(bank[7][:], pick, forget_sum[:], start=True, stop=True).then_inc(forget_row, 1)

            forget_on_partitions(0)
            for s in range(STEPS + 3):
                if s < STEPS:
                    h, b = s // QB, s % QB
                    rows_ = slice(h % 2 * FOX_D, (h % 2 + 1) * FOX_D)
                    if s >= 3:
                        pe.wait_ge(scores_taken, s - 2)
                    acc = bank[s % 3]
                    nc.tensor.matmul(acc[:, 0:(b + 1) * P], qf[rows_, h // 2, bass.ts(b, P)],
                                     kf[rows_, h // 2, 0:(b + 1) * P], start=True, stop=False)
                    nc.tensor.matmul(acc[:, bass.ts(b, P)], masks[:, 8, :], masks[:, 9, :], start=False, stop=True
                                     ).then_inc(scores_done, 1)
                    if b == 1 and h + 1 < FOX_HEADS:
                        forget_on_partitions(h + 1)
                if 2 <= s < STEPS + 2:
                    s2 = s - 2
                    pe.wait_ge(prob_ready, s2 + 1)
                    if s2 >= 2:
                        pe.wait_ge(prob_copied, s2 - 1)
                    for kb in range(s2 % QB + 1):
                        last = nc.tensor.transpose(bank[3 + s2 % 2][:, bass.ts(kb, P)],
                                                   prob[s2 % 2][:, bass.ts(kb, P)], ident)
                    last.then_inc(prob_turned, 1)
                if s >= 3:
                    s3 = s - 3
                    h, b = s3 // QB, s3 % QB
                    rows_ = slice(h % 2 * FOX_D, (h % 2 + 1) * FOX_D)
                    pe.wait_ge(prob_copied, s3 + 1)
                    if b == 0 and h % 2 == 0 and h >= 4:
                        pe.wait_ge(x_ready, XR["fox_o"] + h // 2 - 1)
                    for kb in range(b + 1):
                        last = nc.tensor.matmul(bank[5 + h // 2 % 2][rows_, bass.ts(b, P)],
                                                vt[:, kb, h * FOX_D:(h + 1) * FOX_D], prob_t[s3 % 2][:, kb, :],
                                                start=kb == 0, stop=kb == b)
                    last.then_inc(pv_done, 1)
            units("fox_o", q_hi, q_lo, XR["fox_o"])
            sum_over_partitions(11)
            sum_over_partitions(12)
            units("ffn_in_b", x_hi, x_lo, XR["ffn_x_b"])
            ffn_out("ffn_out_b", XR["ffn_h_b"])
            sum_over_partitions(13)

        @block.vector
        def _(dve):
            st = Steps(dve, dve_steps)
            V = nc.vector

            def split(src, hi, lo):
                st.seq(V.tensor_copy(hi, src))
                V.tensor_tensor(lo, src, hi.bitcast(F32), ALU.subtract).then_inc(x_ready, 1)

            def add_square(src, first):
                if first:
                    st.seq(V.tensor_tensor(total[:], src, src, ALU.mult))
                else:
                    st.seq(V.tensor_tensor(square[:], src, src, ALU.mult))
                    st.seq(V.tensor_tensor(total[:], total[:], square[:], ALU.add))

            def tile(t, m):
                return t[:, bass.ds(m, 1), :].rearrange("p a t -> p (a t)") if not isinstance(m, int) else t[:, m, :]

            def conv_taps(src, dst, name, m, taps, bias=None):
                w = par[:, PCOL[name]:PCOL[name] + 8 * taps].rearrange("p (m k) -> p m k", k=taps)

                def weight(k):
                    return w[:, m, k:k + 1] if isinstance(m, int) else \
                        w[:, bass.ds(m, 1), k:k + 1].rearrange("p a b -> p (a b)")
                if bias is None:
                    st.seq(V.tensor_scalar(dst, src[:, 0:T], weight(0), None, ALU.mult))
                else:
                    b = par[:, bass.ds(m + PCOL[bias], 1)]
                    st.seq(V.tensor_scalar(dst, src[:, 0:T], weight(0), b, ALU.mult, ALU.add))
                for k in range(1, taps):
                    st.seq(V.scalar_tensor_tensor(dst, src[:, k:k + T], weight(k), dst, ALU.mult, ALU.add))

            V.memset(eps6[:], 1e-6)
            V.memset(eps5[:], 1e-5)
            V.memset(U[:, :, 0:CONF_K - 1], 0.0)
            V.memset(prod_pad[:, 0:3], 0.0)
            V.memset(ones[:], 1.0).then_inc(consts_ready, 1)
            V.memset(tmp[:, 0:1], 0.0).then_inc(bank_free, RING)
            dve.wait_ge(consts_ready, 1)

            dve.wait_ge(inputs_landed, 32)
            for m in range(KT):
                if m == 0:
                    st.seq(V.tensor_tensor(total[:], X[:, m, :], X[:, m, :], ALU.mult))
                else:
                    st.seq(V.tensor_tensor(square[:], X[:, m, :], X[:, m, :], ALU.mult))
                    ins = V.tensor_tensor(total[:], total[:], square[:], ALU.add)
                    if m < KT - 1:
                        st.seq(ins)
                    else:
                        ins.then_inc(sum_ready, 1)

            def ada_chunk(k):
                b = k % ADA_BUFS
                dve.wait_ge(ada_landed[b], 16 * (k // ADA_BUFS + 1))
                if k >= 1:
                    dve.wait_ge(ada_ps_ready, k)
                st.seq(V.tensor_scalar(ada_acc[:], ada_w[:, b, 0, :], silu_c[:, 0:1], None, ALU.mult))
                for j in range(1, KT - 1):
                    st.seq(V.scalar_tensor_tensor(ada_acc[:], ada_w[:, b, j, :], silu_c[:, j:j + 1], ada_acc[:],
                                                  ALU.mult, ALU.add))
                V.scalar_tensor_tensor(ada_acc[:], ada_w[:, b, KT - 1, :], silu_c[:, KT - 1:KT], ada_acc[:],
                                       ALU.mult, ALU.add).then_inc(ada_sum_ready, 1)
                dve.wait_ge(ada_sum_ready, k + 1)
                V.memset(tmp[:, 0:1], 0.0).then_inc(ada_used, 1)

            dve.wait_ge(silu_c_ready, 1)
            for k in range(ADA_FIRST):
                ada_chunk(k)
            b_ada = par[:, PCOL["b_ada"]:PCOL["b_ada"] + 48]
            dve.wait_ge(ada_ps_ready, ADA_FIRST)
            st.seq(V.tensor_tensor(mod[:, 0:16], ada_ps[:, 0:16], b_ada[:, 0:16], ALU.add))
            g = par[:, PCOL["norm_mix_g"]:PCOL["norm_mix_g"] + 8]
            st.seq(V.scalar_tensor_tensor(gain[:, 0, :], mod[:, 8:16], 1.0, g, ALU.add, ALU.mult))

            def modulated_input(n, which, shift):
                dve.wait_ge(rstd_ready, n)
                for m in range(KT):
                    st.seq(V.scalar_tensor_tensor(tmp[:], X[:, m, :], gain[:, which, m:m + 1], rstd[:],
                                                  ALU.mult, ALU.mult))
                    st.seq(V.tensor_scalar(tmp[:], tmp[:], mod[:, shift + m:shift + m + 1], None, ALU.add))
                    split(tmp[:], x_hi[:, m, :], x_lo[:, m, :])
                    dve.wait_ge(x_ready, XSET[which] + m + 1)

            XSET = [0, 32]
            modulated_input(1, 0, 0)

            u0 = FIRST["conf_in"]
            with st.loop(4, CONF_K) as i:
                for j in range(2):
                    dve.wait_ge(gated, i * 2 + (j + 1))
                    V.tensor_tensor(tile(U, i * 2 + j)[:, CONF_K - 1:], bank[(u0 + 2 * j) % RING][:],
                                    act_out[:, j, :], ALU.mult).then_inc(bank_free, 2)
                dve.wait_ge(bank_free, i * 4 + (u0 + 4 + RING))
                conv_taps(tile(U, i), tile(UC, i), "conv_conf_w", i, CONF_K, "conv_conf_b")
            u0 = FIRST["short_in"]
            with st.loop(2, 4 * (SHORT_K + 1) + 2 * CONF_K) as i:
                for r in range(4):
                    m = i * 4 + r
                    cu = u0 + 3 * r
                    dve.wait_ge(gated, i * 4 + (8 + r + 1))
                    dve.wait_ge(w_used, i * 12 + (cu + 2))
                    V.tensor_tensor(prod_pad[:, 3:], bank[(cu + 1) % RING][:], act_out[:, r % 2, :],
                                    ALU.mult).then_inc(bank_free, 2)
                    dve.wait_ge(bank_free, i * 12 + (cu + 2 + RING))
                    conv_taps(prod_pad[:, 4 - SHORT_K:], tmp[:], "conv_short_w", m, SHORT_K)
                    dve.wait_ge(w_used, i * 12 + (cu + 3))
                    V.tensor_tensor(tmp[:], tmp[:], bank[(cu + 2) % RING][:], ALU.mult).then_inc(bank_free, 1)
                    dve.wait_ge(bank_free, i * 12 + (cu + 3 + RING))
                    st.seq(V.tensor_copy(tile(y_hi, m), tmp[:]))
                    V.tensor_tensor(tile(y_lo, m), tmp[:], tile(y_hi, m).bitcast(F32), ALU.subtract
                                    ).then_inc(x_ready, 1)
                    dve.wait_ge(x_ready, i * 4 + (8 + r + 1))
                    if r % 2 == 1:
                        c = i * 2 + (4 + r // 2)
                        conv_taps(tile(U, c), tile(UC, c), "conv_conf_w", c, CONF_K, "conv_conf_b")
            u0 = FIRST["mix_a"]
            for j in range(8):
                dve.wait_ge(gated, 16 + j + 1)
                V.tensor_tensor(mixed[:, j, :], bank[(u0 + 2 * j) % RING][:], act_out[:, j % 2, :], ALU.mult
                                ).then_inc(bank_free, 2)
                ada_chunk(ADA_FIRST + 2 * j)
                ada_chunk(ADA_FIRST + 2 * j + 1)
                if j == 1:
                    st.seq(V.tensor_tensor(total[:], UC[:, 0, :], UC[:, 1, :], ALU.add))
                    for m in range(2, KT):
                        ins = V.tensor_tensor(total[:], total[:], UC[:, m, :], ALU.add)
                        st.seq(ins) if m < KT - 1 else ins.then_inc(sum_ready, 1)
                if j == 3:
                    dve.wait_ge(stat_ready, 2)
                    st.seq(V.tensor_scalar(rstd[:], stat[:], 1.0 / D, None, ALU.mult))
                    for m in range(KT):
                        st.seq(V.tensor_tensor(UC[:, m, :], UC[:, m, :], rstd[:], ALU.subtract))
                        if m < KT - 1:
                            add_square(UC[:, m, :], m == 0)
                    st.seq(V.tensor_tensor(square[:], UC[:, KT - 1, :], UC[:, KT - 1, :], ALU.mult))
                    V.tensor_tensor(total[:], total[:], square[:], ALU.add).then_inc(sum_ready, 1)
            dve.wait_ge(ada_ps_ready, ADA_CHUNKS)
            st.seq(V.tensor_tensor(mod[:, 16:48], ada_ps[:, 16:48], b_ada[:, 16:48], ALU.add))
            g = par[:, PCOL["norm_ffn_g"]:PCOL["norm_ffn_g"] + 8]
            st.seq(V.scalar_tensor_tensor(gain[:, 1, :], mod[:, 32:40], 1.0, g, ALU.add, ALU.mult))
            u0 = FIRST["gate_b"]
            for j in range(8):
                dve.wait_ge(w_used, u0 + j + 1)
                V.tensor_copy(gate[:, j, :], bank[(u0 + j) % RING][:]).then_inc(bank_free, 1)
            dve.wait_ge(rstd_ready, 2)
            for m in range(KT):
                V.tensor_tensor(UC[:, m, :], UC[:, m, :], rstd[:], ALU.mult).then_inc(ln_scaled, 1)
            for m in range(KT):
                dve.wait_ge(ln_silu, m + 1)
                split(UC[:, m, :], y_hi[:, m, :], y_lo[:, m, :])
            u0 = FIRST["conf_out"]
            dve.wait_ge(gated, 25)
            for j in range(8):
                dve.wait_ge(w_used, u0 + j + 1)
                V.tensor_tensor(tmp[:], bank[(u0 + j) % RING][:], gate[:, j, :], ALU.mult).then_inc(bank_free, 1)
                dve.wait_ge(bank_free, u0 + j + 1 + RING)
                st.seq(V.tensor_tensor(tmp[:], tmp[:], mixed[:, j, :], ALU.add))
                split(tmp[:], x_hi[:, j, :], x_lo[:, j, :])
                dve.wait_ge(x_ready, 24 + j + 1)

            def add_to_residual(banks, when, scale, freed):
                for j in range(KT):
                    dve.wait_ge(w_used, when(j))
                    ins = V.scalar_tensor_tensor(X[:, j, :], banks[j][:], mod[:, scale + j:scale + j + 1],
                                                 X[:, j, :], ALU.mult, ALU.add)
                    if freed(j):
                        ins.then_inc(bank_free, freed(j)[0])
                        dve.wait_ge(bank_free, freed(j)[1])
                    else:
                        st.seq(ins)
                    if j == 0:
                        st.seq(V.tensor_tensor(total[:], X[:, j, :], X[:, j, :], ALU.mult))
                    else:
                        st.seq(V.tensor_tensor(square[:], X[:, j, :], X[:, j, :], ALU.mult))
                        ins = V.tensor_tensor(total[:], total[:], square[:], ALU.add)
                        st.seq(ins) if j < KT - 1 else ins.then_inc(sum_ready, 1)

            u0 = FIRST["w_o"]
            add_to_residual([bank[(u0 + j) % RING] for j in range(8)], lambda j: u0 + j + 1, 16,
                            lambda j: (1, u0 + j + 1 + RING))
            modulated_input(3, 1, 24)
            def ffn_in(phase, gated0, ready):
                u1 = FIRST[phase]
                with st.loop(FT // 2, 2) as i:
                    for j in range(2):
                        dve.wait_ge(gated, i * 2 + (gated0 + j + 1))
                        dve.wait_ge(w_used, i * 4 + (u1 + 2 * j + 2))
                        V.tensor_tensor(tmp[:], bank[(u1 + 2 * j + 1) % RING][:], act_out[:, j, :], ALU.mult
                                        ).then_inc(bank_free, 2)
                        dve.wait_ge(bank_free, i * 4 + (u1 + 2 * j + 2 + RING))
                        m = i * 2 + j
                        st.seq(V.tensor_copy(tile(f_hi, m), tmp[:]))
                        V.tensor_tensor(tile(f_lo, m), tmp[:], tile(f_hi, m).bitcast(F32), ALU.subtract
                                        ).then_inc(x_ready, 1)
                        dve.wait_ge(x_ready, i * 2 + (ready + j + 1))

            def sum_squares(src, j):
                if j == 0:
                    st.seq(V.tensor_tensor(total[:], src, src, ALU.mult))
                else:
                    st.seq(V.tensor_tensor(square[:], src, src, ALU.mult))
                    ins = V.tensor_tensor(total[:], total[:], square[:], ALU.add)
                    st.seq(ins) if j < KT - 1 else ins.then_inc(sum_ready, 1)

            ffn_in("ffn_in", 25, XR["ffn_h"])
            u2 = FIRST["ffn_out"]
            add_to_residual(bank, lambda j: u2 + (FT // 2) * (1 + j // 4), 40,
                            lambda j: (FT, u2 + FT + RING) if j == KT - 1 else None)

            def post_norm(n, name, j0, src):
                dve.wait_ge(rstd_ready, n)
                for m in range(KT):
                    if src is X:
                        st.seq(V.scalar_tensor_tensor(X[:, m, :], X[:, m, :], pcol(name, j0 + m), rstd[:],
                                                      ALU.mult, ALU.mult))
                    else:
                        st.seq(V.scalar_tensor_tensor(tmp[:], src[:, m, :], pcol(name, j0 + m), rstd[:],
                                                      ALU.mult, ALU.mult))
                        ins = V.tensor_tensor(X[:, m, :], X[:, m, :], tmp[:], ALU.add)
                        if name == "post_ffn_norm_2" and j0 == 8:
                            ins.then_inc(out_ready, 1)
                            dve.wait_ge(out_ready, m + 1)
                            continue
                        st.seq(ins)
                    sum_squares(X[:, m, :], m)

            def norm_input(n, name, j0, hi, lo, ready):
                dve.wait_ge(rstd_ready, n)
                for m in range(KT):
                    st.seq(V.scalar_tensor_tensor(tmp[:], X[:, m, :], pcol(name, j0 + m), rstd[:],
                                                  ALU.mult, ALU.mult))
                    split(tmp[:], hi[:, m, :], lo[:, m, :])
                    dve.wait_ge(x_ready, ready + m + 1)

            def take_mix(banks, when, freed):
                for j in range(KT):
                    dve.wait_ge(w_used, when(j))
                    ins = V.tensor_copy(mix[:, j, :], banks[j][:])
                    if freed(j):
                        ins.then_inc(bank_free, freed(j)[0])
                        dve.wait_ge(bank_free, freed(j)[1])
                    else:
                        st.seq(ins)
                    sum_squares(mix[:, j, :], j)

            def take_mix_units(phase):
                u0 = FIRST[phase]
                take_mix([bank[(u0 + j) % RING] for j in range(8)], lambda j: u0 + j + 1,
                         lambda j: (1, u0 + j + 1 + RING))

            def take_mix_ffn(phase):
                u2 = FIRST[phase]
                take_mix(bank, lambda j: u2 + (FT // 2) * (1 + j // 4),
                         lambda j: (FT, u2 + FT + RING) if j == KT - 1 else None)

            post_norm(4, "final_norm_g", 0, X)
            norm_input(5, "pre_mix_norm_2", 0, x_hi, x_lo, XR["gdn_x"])
            dve.wait_ge(inputs_landed, 64)
            sh = small_hi[:].rearrange("p a k n -> p (a k n)")
            st.seq(V.tensor_copy(sh, small_raw[:]))
            V.tensor_tensor(small_lo[:].rearrange("p a k n -> p (a k n)"), small_raw[:], sh.bitcast(F32),
                            ALU.subtract).then_inc(tok_dve, 1)
            u0 = FIRST["gdn_qkv"]
            with st.loop(6, 4 * 3) as i:
                for j in range(4):
                    m = i * 4 + j
                    dve.wait_ge(w_used, i * 4 + (u0 + j + 1))
                    dve.wait_ge(silu_in, i * 4 + j)
                    V.tensor_copy(prod_pad[:, 3:], bank[(u0 + j) % RING][:]).then_inc(bank_free, 1)
                    dve.wait_ge(bank_free, i * 4 + (u0 + j + 1 + RING))
                    w = par[:, PCOL["gdn_conv_2"]:PCOL["gdn_conv_2"] + 96].rearrange("p (m k) -> p m k", k=4)
                    w = [w[:, bass.ds(m, 1), k:k + 1].rearrange("p a b -> p (a b)") for k in range(4)]
                    d = tile(qkv, m)
                    st.seq(V.tensor_scalar(d, prod_pad[:, 0:T], w[0], None, ALU.mult))
                    for k in (1, 2):
                        st.seq(V.scalar_tensor_tensor(d, prod_pad[:, k:k + T], w[k], d, ALU.mult, ALU.add))
                    V.scalar_tensor_tensor(d, prod_pad[:, 3:3 + T], w[3], d, ALU.mult, ALU.add).then_inc(silu_in, 1)

            def square_head(r, src):
                if r >= 2:
                    dve.wait_ge(sq_summed, r - 1)
                V.tensor_tensor((square, total)[r % 2][:], src, src, ALU.mult).then_inc(sq_ready, 1)

            u0 = FIRST["gdn_z"]
            dt = row[:, 8:16].unsqueeze(1).broadcast_to([P, NCH, HEADS])

            def byhead(n):
                return tok[:, n, :].rearrange("p (c h) -> p c h", h=HEADS)
            dve.wait_ge(silu_out, 24)
            square_head(0, qkv[:, 0, :])
            for j in range(8):
                if j == 0:
                    dve.wait_ge(tok_pe, 1)
                    ba = bank[6][:, 0:64].rearrange("p (c n) -> p c n", n=16)
                    st.seq(V.tensor_copy(byhead(0), ba[:, :, 0:8]))
                    st.seq(V.tensor_tensor(byhead(1), ba[:, :, 8:16], dt, ALU.add))
                    V.scalar_tensor_tensor(tok[:, 2, :], tok[:, 1, :], -1.0, tok[:, 1, :], ALU.mult, ALU.max).then_inc(tok_dve, 1)
                if j == 1:
                    dve.wait_ge(tok_act, 1)
                    st.seq(V.tensor_scalar(tok[:, 0, :], tok[:, 0, :], 1.0, None, ALU.add))
                    st.seq(V.reciprocal(tok[:, 0, :], tok[:, 0, :]))
                    st.seq(V.scalar_tensor_tensor(tok[:, 1, :], tok[:, 1, :], 0.0, tok[:, 2, :], ALU.max, ALU.add))
                    ea = tok[:, 3, 0:8].unsqueeze(1).broadcast_to([P, NCH, HEADS])
                    V.scalar_tensor_tensor(byhead(4), byhead(1), -1.0, ea, ALU.mult, ALU.mult).then_inc(tok_dve, 1)
                if j == 3:
                    dve.wait_ge(tok_act, 2)
                    st.seq(V.tensor_copy(tok[:, 8, :], bank[6][:, 64:96]))
                    st.seq(V.scalar_tensor_tensor(tok[:, 9, :], tok[:, 0, :], -1.0, tok[:, 5, :], ALU.mult, ALU.mult))
                    V.tensor_tensor(tok[:, 7, :], bank[6][:, 96:128], tok[:, 8, :], ALU.subtract
                                    ).then_inc(tok_dve, 1)
                dve.wait_ge(w_used, u0 + j + 1)
                V.tensor_copy(z_gate[:, j, :], bank[(u0 + j) % RING][:]).then_inc(bank_free, 1)
                for r in (2 * j, 2 * j + 1):
                    if r < 15:
                        square_head(r + 1, qkv[:, r + 1, :])
                    dve.wait_ge(head_rstd, r + 1)
                    V.scalar_tensor_tensor(qkv[:, r, :], qkv[:, r, :], DH ** -0.5 if r < HEADS else 1.0,
                                           act_out[:, r % 2, :], ALU.mult, ALU.mult).then_inc(head_rstd_used, 1)
            dve.wait_ge(masks_landed, 32)
            V.tensor_copy(masks[:], masks_raw[:]).then_inc(masks_ready, 1)
            dve.wait_ge(masks_ready, 1)
            dve.wait_ge(tok_act, 3)

            def perhead(n, h):
                return byhead(n)[:, :, h:h + 1].broadcast_to([P, NCH, P])

            def four(b):
                return b[:].rearrange("p (c n) -> p c n", c=NCH)

            def mask4(n):
                return masks[:, n, :].unsqueeze(1).broadcast_to([P, NCH, P])
            ident4 = tri[:, 1, :].unsqueeze(1).broadcast_to([P, NCH, P])

            def chunk_rest(p, c):
                for n in range(2):
                    h, k = 2 * p + n, p * 8 + c * 2 + n
                    dve.wait_ge(ks_ready, k + 1)
                    V.scalar_tensor_tensor(rest_sb[n], bank[n][:, 0:P], tok[:, 9, c * 8 + h:c * 8 + h + 1],
                                           beta_v[(p % 2) * 2 + n][:, c, :], ALU.mult, ALU.add
                                           ).then_inc(rest_ready, 1)

            def chunk_state(p, c):
                for n in range(2):
                    h, k = 2 * p + n, p * 8 + c * 2 + n
                    dve.wait_ge(o_copied, k + 1)
                    V.scalar_tensor_tensor(state[:, n, :], state[:, n, :], tok[:, 6, c * 8 + h:c * 8 + h + 1],
                                           bank[n][:, 3 * P:4 * P], ALU.mult, ALU.add).then_inc(state_ready, 1)

            for p in range(HEADS // 2 + 1):
                if p < HEADS // 2:
                    for n in range(2):
                        h, slot = 2 * p + n, (p % 2) * 2 + n
                        sq4 = square[:].rearrange("p (c n) -> p c n", c=NCH)
                        dec4 = act_out[:, n, :].rearrange("p (c n) -> p c n", c=NCH)
                        dve.wait_ge(decay_row, h + 1)
                        st.seq(V.tensor_tensor(sq4, four(bank[0]), perhead(8, h), ALU.subtract))
                        V.tensor_tensor(sq4, sq4, mask4(0), ALU.add).then_inc(diff_ready, 1)
                        dve.wait_ge(head_products, 4 * h + 4)
                        st.seq(V.tensor_tensor(qkv[:, h, :], qkv[:, h, :], rstd[:], ALU.mult))
                        dve.wait_ge(decay_ready, h + 1)
                        V.tensor_tensor(attn[slot][:], four(bank[3]), dec4, ALU.mult)
                        st.seq(V.tensor_tensor(lower_t[n][:], four(bank[2]), dec4, ALU.mult))
                        V.tensor_tensor(lower_t[n][:], lower_t[n][:], four(bank[1]), ALU.mult).then_inc(head_taken, 1)
                        dve.wait_ge(head_taken, h + 1)
                        V.tensor_tensor(level_a[n][0][:], lower_t[n][:], mask4(1), ALU.mult).then_inc(level_ready, 1)
                if p >= 1:
                    for n in range(2):
                        V.memset(state[:, n, :], 0.0).then_inc(state_ready, 1)
                for lv in range(LEVELS):
                    if p < HEADS // 2 and lv + 1 < LEVELS:
                        for n in range(2):
                            if lv >= 1:
                                dve.wait_ge(first_half, p * 14 + (lv - 1) * 2 + n + 1)
                            V.tensor_tensor(level_a[n][(lv + 1) % 2][:], lower_t[n][:], mask4(2 + lv), ALU.mult
                                            ).then_inc(level_ready, 1)
                    if p >= 1 and lv < NCH:
                        chunk_rest(p - 1, lv)
                    if p < HEADS // 2:
                        for n in range(2):
                            slot = (p % 2) * 2 + n
                            if lv == 0:
                                dve.wait_ge(level_ready, p * 14 + n + 1)
                                st.seq(V.tensor_tensor(inv_t[slot][:], ident4, level_a[n][0][:], ALU.subtract))
                                dve.wait_ge(first_half, p * 14 + n + 1)
                                V.tensor_tensor(inv[n][:], ident4, four(bank[4 + 2 * n]), ALU.subtract
                                                ).then_inc(inverse_ready, 1)
                            else:
                                dve.wait_ge(second_half, p * 12 + (lv - 1) * 2 + n + 1)
                                if lv < LEVELS - 1:
                                    st.seq(V.tensor_tensor(inv[n][:], inv[n][:], four(bank[4 + 2 * n]), ALU.subtract))
                                V.tensor_tensor(inv_t[slot][:], inv_t[slot][:], four(bank[5 + 2 * n]), ALU.subtract
                                                ).then_inc(inverse_ready, 1)
                        if lv in (0, 1):
                            h, slot = 2 * p + lv, (p % 2) * 2 + lv
                            dve.wait_ge(turned, 2 * h + 1)
                            V.tensor_tensor(beta_v[slot][:], four(bank[2]), perhead(0, h), ALU.mult
                                            ).then_inc(turned_used, 1)
                            dve.wait_ge(turned, 2 * h + 2)
                            V.tensor_tensor(key_dec[slot][:], four(bank[3]), perhead(7, h), ALU.mult
                                            ).then_inc(turned_used, 1)
                    if p >= 1 and lv < NCH:
                        chunk_state(p - 1, lv)
            dve.wait_ge(o_copied, 32)
            dve.wait_ge(z_ready, 1)
            square_head(16, qkv[:, 16, :])
            for h in range(HEADS):
                if h + 1 < HEADS:
                    square_head(17 + h, qkv[:, 17 + h, :])
                dve.wait_ge(head_rstd, 17 + h)
                V.scalar_tensor_tensor(tmp[:], qkv[:, 16 + h, :], pcol("gdn_out_norm_2", 0), act_out[:, h % 2, :],
                                       ALU.mult, ALU.mult).then_inc(head_rstd_used, 1)
                dve.wait_ge(head_rstd_used, 17 + h)
                st.seq(V.tensor_tensor(tmp[:], tmp[:], z_gate[:, h, :], ALU.mult))
                split(tmp[:], og_hi[:, h, :], og_lo[:, h, :])
                dve.wait_ge(x_ready, XR["gdn_o"] + h + 1)
            take_mix_units("gdn_out")
            post_norm(6, "post_mix_norm_2", 0, mix)
            norm_input(7, "pre_ffn_norm_2", 0, x_hi, x_lo, XR["ffn_x_a"])
            ffn_in("ffn_in_a", 25 + FT, XR["ffn_h_a"])
            take_mix_ffn("ffn_out_a")
            post_norm(8, "post_ffn_norm_2", 0, mix)
            norm_input(9, "kv_norm_2", 0, x_hi, x_lo, XR["kv_x"])
            norm_input(9, "pre_mix_norm_2", 8, q_hi, q_lo, XR["q_x"])
            u0 = FIRST["fox_k"]
            for j in range(8):
                dve.wait_ge(w_used, u0 + j + 1)
                V.tensor_copy(kf[:, j, :], bank[(u0 + j) % RING][:]).then_inc(bank_free, 1)
            soft, part = (tok[:, n:n + 2, :].rearrange("p a b -> p (a b)") for n in (8, 10))
            bf = row[:, 16:32].unsqueeze(1).broadcast_to([P, NCH, 16])
            dve.wait_ge(tok_pe, 3)
            st.seq(V.tensor_tensor(soft.rearrange("p (c n) -> p c n", n=16),
                                   bank[6][:, 0:64].rearrange("p (c n) -> p c n", n=16), bf, ALU.add))
            V.scalar_tensor_tensor(part, soft, -1.0, soft, ALU.mult, ALU.max).then_inc(tok_dve, 1)
            st.seq(V.tensor_scalar(soft, soft, -1.0, 0.0, ALU.mult, ALU.max))
            dve.wait_ge(tok_act, 4)
            V.tensor_tensor(soft, soft, part, ALU.add).then_inc(tok_dve, 1)
            u0 = FIRST["fox_v"]
            for hv in range(2):
                dve.wait_ge(w_used, u0 + 4 * (hv + 1))
                for t in range(QB):
                    V.tensor_copy(vt[:, t, bass.ts(hv, T)], bank[4 * hv + t][:]).then_inc(v_free, 1)
            dve.wait_ge(v_free, 8)
            V.memset(tmp[:, 0:1], 0.0).then_inc(bank_free, 8)
            u0 = FIRST["fox_q"]
            for j in range(8):
                dve.wait_ge(w_used, u0 + j + 1)
                V.tensor_scalar(qf[:, j, :], bank[(u0 + j) % RING][:], FOX_D ** -0.5, None, ALU.mult
                                ).then_inc(bank_free, 1)
            dve.wait_ge(masks_landed, 48)
            V.tensor_copy(masks[:], masks_raw[:]).then_inc(masks_ready, 1)
            dve.wait_ge(tok_pe, 4)
            st.seq(V.memset(square[0:16, :], 1.0))
            V.tensor_tensor_scan(forget_sum[:], square[0:16, :], bank[7][0:16, :], 0.0, ALU.mult, ALU.add
                                 ).then_inc(tok_dve, 1)
            dve.wait_ge(masks_ready, 2)
            STEPS = FOX_HEADS * QB

            def take_heads(t):
                dve.wait_ge(pv_done, 8 * (t + 1))
                o = bank[5 + t % 2][:]
                st.seq(V.tensor_copy(q_hi[:, t, :], o))
                V.tensor_tensor(q_lo[:, t, :], o, q_hi[:, t, :].bitcast(F32), ALU.subtract).then_inc(x_ready, 1)

            for s in range(STEPS + 1):
                if s < STEPS:
                    h, b = s // QB, s % QB
                    e = (b + 1) * P
                    if b == 0:
                        dve.wait_ge(forget_row, h + 1)
                        V.tensor_copy(forget[h % 2][:], bank[7][:]).then_inc(forget_copied, 1)
                        dve.wait_ge(forget_copied, h + 1)
                    dve.wait_ge(scores_done, s + 1)
                    if s >= 2:
                        dve.wait_ge(exp_done, s - 1)
                    V.tensor_tensor_reduce(out=score[s % 2][:, 0:e], in0=bank[s % 3][:, 0:e],
                                           in1=forget[h % 2][:, 0:e], scale=-1.0, scalar=3e38, op0=ALU.add,
                                           op1=ALU.min, accum_out=softmax[:, s % 2, 0:1]).then_inc(scores_taken, 1)
                if s >= 1:
                    s1 = s - 1
                    h1, e = s1 // QB, (s1 % QB + 1) * P
                    q = softmax[:, s1 % 2, :]
                    dve.wait_ge(exp_done, s1 + 1)
                    st.seq(V.reciprocal(q[:, 2:3], q[:, 1:2]))
                    V.tensor_scalar(prob[s1 % 2][:, 0:e], prob[s1 % 2][:, 0:e], q[:, 2:3], None, ALU.mult
                                    ).then_inc(prob_ready, 1)
                if s >= 12 and (s - 12) % 8 == 0:
                    take_heads((s - 12) // 8)
            take_heads(7)
            take_mix_units("fox_o")
            post_norm(10, "post_mix_norm_2", 8, mix)
            norm_input(11, "pre_ffn_norm_2", 8, x_hi, x_lo, XR["ffn_x_b"])
            ffn_in("ffn_in_b", 25 + 2 * FT, XR["ffn_h_b"])
            take_mix_ffn("ffn_out_b")
            post_norm(12, "post_ffn_norm_2", 8, mix)


def unit_tiles(w):
    return w.reshape(KT, P, -1, P).transpose(2, 1, 0, 3).reshape(-1, P, UNIT)


def ffn_out_units(w):
    return w.reshape(FT // 2, 2, P, 2, 4, P).transpose(3, 0, 2, 1, 4, 5).reshape(-1, P, UNIT)


def paired(*parts):
    return np.stack(parts, axis=1).reshape(-1, P, UNIT)


def columns(v, name):
    v = v.reshape(-1, v.shape[-1] // P, P)
    v = v.transpose(2, 1, 0) if "conv_" in name and not name.endswith("_b") or name == "gdn_conv_2" \
        else v.transpose(2, 0, 1)
    return v.reshape(P, -1)


def constant_tiles():
    a, b = np.arange(P)[:, None], np.arange(P)[None, :]
    tiles = [a <= b, a == b, np.where(a <= b, 0.0, -1e30)]
    for lv in range(LEVELS):
        n = 2 ** lv
        tiles.append((a // (2 * n) == b // (2 * n)) & (a // n % 2 == 0) & (b // n % 2 == 1))
    tiles += [a == b, np.where(a >= b, 0.0, -1e30)]
    return np.ascontiguousarray(np.stack([t.astype(np.float32) for t in tiles]).transpose(1, 0, 2))


def kernel(**inputs):
    import concourse.bacc as _bacc
    from concourse.bass_utils import run_bass_kernel_spmd as _run

    a = {k: np.asarray(v) for k, v in inputs.items()}
    w_in = unit_tiles(a["w_in"][0])
    b_u, c_u, v_u, vc_u, gl_u, ga_u, gb_u = (w_in[8 * n:8 * n + 8] for n in range(7))
    ffn = unit_tiles(a["w_ffn_in"][0])
    gdn = a["gdn_w_in_2"][0]
    ffn_2 = []
    for n in range(2):
        f = unit_tiles(a["w_ffn_in_2"][n])
        ffn_2.append((paired(f[:FT], f[FT:]), ffn_out_units(a["w_ffn_out_2"][n])))
    weights = np.concatenate([
        paired(vc_u, gl_u), paired(c_u, v_u, b_u), paired(unit_tiles(a["w_short_out"][0]), ga_u), gb_u,
        unit_tiles(a["w_conf_out"][0]), unit_tiles(a["w_o"][0]), paired(ffn[:FT], ffn[FT:]),
        ffn_out_units(a["w_ffn_out"][0]),
        unit_tiles(gdn[:, :4096]), unit_tiles(a["gdn_w_out_2"][0]), *ffn_2[0],
        unit_tiles(a["w_kv_2"][:, :1024]),
        a["w_kv_2"][:, 1024:2048].reshape(4, 2, P, 2, T).transpose(3, 0, 2, 1, 4).reshape(-1, P, UNIT),
        unit_tiles(a["fox_w_q_2"][0]), unit_tiles(a["fox_w_o_2"][0]), *ffn_2[1]])
    small = np.stack([gdn[:, 4096:], a["w_kv_2"][:, 2048:]]).reshape(2, KT, P, 16).transpose(2, 0, 1, 3)
    rows = np.concatenate([a["gdn_a_log_2"].ravel(), a["gdn_dt_bias_2"].ravel(), a["b_forget_2"]]).reshape(1, 32)
    params = np.concatenate([columns(a[name], name) for name, _ in PARAMS], axis=1)
    ada = np.ascontiguousarray(a["w_ada"][0].reshape(KT, P, ADA_CHUNKS, ADA_COLS).transpose(2, 1, 0, 3))
    arrays = {"x_t": np.ascontiguousarray(a["x"][0].T), "params": np.ascontiguousarray(params),
              "weights": np.ascontiguousarray(weights), "ada": ada,
              "small_w": np.ascontiguousarray(small.reshape(P, -1)), "rows": rows, "consts": constant_tiles()}
    nc = _bacc.Bacc("TRN2", target_bir_lowering=False, num_devices=1)
    args = [nc.dram_tensor(n, v.shape, F32, kind="ExternalInput").ap() for n, v in arrays.items()]
    out = nc.dram_tensor("out_t", (D, T), F32, kind="ExternalOutput").ap()
    program(nc, *args, out)
    r = _run(nc, [arrays], core_ids=[0])
    return r.results[0]["out_t"].T.reshape(1, T, D)
```

```python
from contextlib import ExitStack, contextmanager

import concourse.bass as bass
import numpy as np
from concourse import mybir

F32 = mybir.dt.float32
F32R = mybir.dt.float32r
BF16 = mybir.dt.bfloat16
ACT = mybir.ActivationFunctionType
ALU = mybir.AluOpType

P = 128
D = 1024
T = 512
KT = D // P
DFF = 2816
FT = DFF // P
RING = 4
AHEAD = RING
UNIT = 8 * P
SHORT_K, CONF_K = 3, 31
POOL_TAPS = 15
ADA_COLS = 256
ADA_BUFS = 3
ADA_CHUNKS = 6 * D // ADA_COLS
ADA_FIRST = 2 * D // ADA_COLS
ADA_ON_PE = (0, 2, 4, 6)
ADA_ON_DVE = [k for k in range(ADA_CHUNKS) if k not in ADA_ON_PE]

PARAMS = [("norm_mix_g", 8), ("norm_ffn_g", 8), ("final_norm_g", 8), ("conv_conf_b", 8), ("conf_ln_g", 8),
          ("conf_ln_b", 8), ("c", 8), ("b_ada", 48), ("conv_short_w", 8 * SHORT_K), ("conv_conf_w", 8 * CONF_K),
          ("pre_mix_norm_2", 16), ("post_mix_norm_2", 16), ("pre_ffn_norm_2", 16), ("post_ffn_norm_2", 16),
          ("kv_norm_2", 8), ("gdn_conv_2", 24 * 4), ("gdn_out_norm_2", 1)]
PCOL, _n = {}, 0
for _name, _w in PARAMS:
    PCOL[_name] = _n
    _n += _w
NPARAM = _n

PHASES = [("conf_in", 16), ("short_in", 24), ("mix_a", 16), ("gate_b", 8), ("conf_out", 8), ("w_o", 8),
          ("ffn_in", 2 * FT), ("ffn_out", FT),
          ("gdn_qkv", 24), ("gdn_z", 8), ("gdn_out", 8), ("ffn_in_a", 2 * FT), ("ffn_out_a", FT),
          ("fox_k", 8), ("fox_v", 8), ("fox_q", 8), ("fox_o", 8), ("ffn_in_b", 2 * FT), ("ffn_out_b", FT)]
FIRST, _n = {}, 0
for _name, _w in PHASES:
    FIRST[_name] = _n
    _n += _w
UNITS = _n
COUNT = dict(PHASES)

INPUTS = [("h1", 8), ("short", 8), ("conf", 8), ("mixed", 8), ("ffn_x", 8), ("ffn_h", FT),
          ("gdn_x", 8), ("gdn_o", 8), ("ffn_x_a", 8), ("ffn_h_a", FT),
          ("kv_x", 8), ("q_x", 8), ("fox_o", 8), ("ffn_x_b", 8), ("ffn_h_b", FT)]
XR, _n = {}, 0
for _name, _w in INPUTS:
    XR[_name] = _n
    _n += _w

HEADS, DH = 8, 128
CH = 128
NCH = T // CH
LEVELS = 7
FOX_HEADS, FOX_D = 16, 64
QB = T // P
NCONST = 2 + 3 + LEVELS


BIG_BYTES = 91072


class Steps:

    def __init__(self, eng, sem):
        self.eng, self.sem, self.n, self.i, self.per = eng, sem, 0, None, 0

    @contextmanager
    def loop(self, count, per):
        start = self.n
        with self.eng.Fori(0, count) as i:
            self.i, self.per = i, per
            yield i
            assert self.n - start == per, (self.n - start, per)
        self.i, self.n = None, start + count * per

    def value(self):
        return self.n if self.i is None else self.n + self.i * self.per

    def step(self, ins):
        ins.then_inc(self.sem, 1)
        self.n += 1
        return self.value()

    def after(self, mark):
        if mark is not None:
            self.eng.wait_ge(self.sem, mark)

    def wait(self):
        self.eng.wait_ge(self.sem, self.value())

    def seq(self, ins):
        self.step(ins)
        self.wait()


def program(nc, xT, params, weights, ada, small_w, rows, consts, out):
    ctx = ExitStack()
    with ctx:
        def at(name, where, shape, dt=F32):
            return nc.alloc_sbuf_tensor_at(name, shape, dt, offset=where)

        place = [-(-nc.sbuf_base // 32) * 32]

        def sb(name, shape, dt=F32):
            t = at(name, place[0], shape, dt)
            place[0] += -(-int(np.prod(shape[1:])) * 4 // 32) * 32
            return t

        raw = sb("raw", [P, RING, UNIT])
        w_hi = sb("w_hi", [P, RING, UNIT], F32R)
        w_lo = sb("w_lo", [P, RING, UNIT], F32R)
        X = sb("X", [P, KT, T])
        XB = place[0]
        x_hi = sb("x_hi", [P, KT, T], F32R)
        x_lo = sb("x_lo", [P, KT, T], F32R)
        par = sb("par", [P, NPARAM])
        mod = sb("mod", [P, 48])
        gain = sb("gain", [P, 2, KT])
        silu_c = sb("silu_c", [P, KT])
        ones = sb("ones", [P, P])
        eps6 = sb("eps6", [P, 1])
        eps5 = sb("eps5", [P, 1])
        spare = sb("spare", [P, 24])
        joint_gain = sb("joint_gain", [P, KT])
        total = sb("total", [P, T])
        square = sb("square", [P, T])
        rstd = sb("rstd", [P, T])
        act_out = sb("act_out", [P, 2, T])
        tmp = sb("tmp", [P, T])
        prod_pad = sb("prod_pad", [P, 3 + T])
        ada_acc = at("ada_acc", place[0], [P, 2, 2 * ADA_COLS])
        place[0] += 4 * ADA_COLS
        tri = at("tri", place[0] - 4 * ADA_COLS, [P, 2, P])
        small_raw = at("small_raw", place[0] - 4 * ADA_COLS, [P, 2 * KT * 16])
        small_hi = sb("small_hi", [P, 2, KT, 16], F32R)
        small_lo = sb("small_lo", [P, 2, KT, 16], F32R)
        row = sb("row", [P, 32])
        tok = sb("tok", [P, 16, NCH * HEADS])
        BIG = place[0]
        assert BIG + BIG_BYTES <= nc.sbuf_usable_end, (BIG, nc.sbuf_usable_end)
        f_hi = at("f_hi", BIG, [P, FT, T], F32R)
        f_lo = at("f_lo", BIG + FT * T * 4, [P, FT, T], F32R)
        U = at("U", BIG, [P, KT, CONF_K - 1 + T])
        UC = at("UC", BIG + 17344, [P, KT, T])
        y_hi = at("y_hi", BIG + 33728, [P, KT, T], F32R)
        y_lo = at("y_lo", BIG + 50112, [P, KT, T], F32R)
        ada_w = at("ada_w", BIG + 66496, [P, ADA_BUFS, KT, ADA_COLS])
        gate = at("gate", BIG + 66496, [P, KT, T])
        mixed = U[:, :, 0:T]
        qkv = at("qkv", BIG, [P, 3 * HEADS, T])
        z_gate = at("z_gate", BIG + 49152, [P, HEADS, T])
        og_hi = at("og_hi", BIG, [P, KT, T], F32R)
        og_lo = at("og_lo", BIG + 16384, [P, KT, T], F32R)
        inv_t = [at(f"inv_t{n}", BIG + 65536 + 2048 * n, [P, NCH, CH]) for n in range(4)]
        attn = [at(f"attn{n}", BIG + 73728 + 2048 * n, [P, NCH, CH]) for n in range(4)]
        beta_v = [at(f"beta_v{n}", BIG + 81920 + 2048 * n, [P, NCH, DH]) for n in range(4)]
        inv = [at(f"inv{n}", XB + 2048 * n, [P, NCH, CH]) for n in range(2)]
        half = [at(f"half{n}", XB + 4096 + 2048 * n, [P, NCH, CH]) for n in range(2)]
        level_a = [[at(f"level_a{n}{b}", XB + 8192 + 4096 * n + 2048 * b, [P, NCH, CH]) for b in range(2)]
                   for n in range(2)]
        lower_t = [at(f"lower_t{n}", XB + 16384 + 2048 * n, [P, NCH, CH]) for n in range(2)]
        state = at("state", XB + 20480, [P, 2, DH])
        masks = at("masks", XB + 21504, [P, NCONST - 2, P], BF16)
        masks_raw = at("masks_raw", XB + 8192, [P, NCONST - 2, P])
        key_dec = [at(f"key_dec{n}", XB + 24576 + 2048 * n, [P, NCH, DH]) for n in range(4)]
        new_v_sb = [tmp[:, n * P:(n + 1) * P] for n in range(2)]
        rest_sb = [tmp[:, (2 + n) * P:(3 + n) * P] for n in range(2)]
        mix = at("mix", XB, [P, KT, T])
        kf = at("kf", BIG, [P, KT, T])
        vt = at("vt", BIG + 16384, [P, QB, D])
        qf = at("qf", BIG + 32768, [P, KT, T])
        q_hi = at("q_hi", BIG + 49152, [P, KT, T], F32R)
        q_lo = at("q_lo", BIG + 65536, [P, KT, T], F32R)
        score = [at(f"score{n}", XB + 2048 * n, [P, T]) for n in range(2)]
        prob = [at(f"prob{n}", XB + 4096 + 2048 * n, [P, T]) for n in range(2)]
        prob_t = [at(f"prob_t{n}", XB + 8192 + 2048 * n, [P, QB, P]) for n in range(2)]
        forget = [at(f"forget{n}", XB + 12288 + 2048 * n, [P, T]) for n in range(2)]
        forget_sum = at("forget_sum", XB + 16384, [16, T])
        softmax = at("softmax", XB + 18432, [P, 4, 4])

        def pcol(name, j):
            return par[:, PCOL[name] + j:PCOL[name] + j + 1]

        bank = [ctx.enter_context(nc.psum_tensor(f"bank{b}", [P, T], F32)) for b in range(8)]
        stat = bank[7]
        ada_ps = bank[6]

        def sem(name):
            return ctx.enter_context(nc.semaphore(name))

        raw_landed = [sem(f"raw_landed{s}") for s in range(RING)]
        w_rounded = sem("w_rounded")
        tap_scaled = sem("tap_scaled")
        tap_added = sem("tap_added")
        w_split = sem("w_split")
        w_used = sem("w_used")
        bank_free = sem("bank_free")
        x_ready = sem("x_ready")
        gated = sem("gated")
        inputs_landed = sem("inputs_landed")
        params_landed = sem("params_landed")
        consts_ready = sem("consts_ready")
        sum_ready = sem("sum_ready")
        stat_ready = sem("stat_ready")
        rstd_ready = sem("rstd_ready")
        silu_c_ready = sem("silu_c_ready")
        ada_landed = [sem(f"ada_landed{s}") for s in range(ADA_BUFS)]
        ada_sum_ready = sem("ada_sum_ready")
        ada_ps_ready = sem("ada_ps_ready")
        gain_ready = sem("gain_ready")
        ln_scaled = sem("ln_scaled")
        ln_silu = sem("ln_silu")
        act_steps = sem("act_steps")
        dve_steps = sem("dve_steps")
        first_squares = sem("first_squares")
        stat_part = sem("stat_part")
        x_new = sem("x_new")
        hi_ready = sem("hi_ready")
        tile_squared = sem("tile_squared")
        squares_added = sem("squares_added")
        rstd_joined = sem("rstd_joined")
        a_scaled = sem("a_scaled")
        silu_in = sem("silu_in")
        silu_out = sem("silu_out")
        sq_ready = sem("sq_ready")
        sq_summed = sem("sq_summed")
        head_rstd = sem("head_rstd")
        head_rstd_used = sem("head_rstd_used")
        tok_pe = sem("tok_pe")
        tok_act = sem("tok_act")
        tok_dve = sem("tok_dve")
        masks_landed = sem("masks_landed")
        masks_ready = sem("masks_ready")
        z_ready = sem("z_ready")
        head_products = sem("head_products")
        decay_row = sem("decay_row")
        diff_ready = sem("diff_ready")
        decay_ready = sem("decay_ready")
        head_taken = sem("head_taken")
        turned = sem("turned")
        turned_used = sem("turned_used")
        level_ready = sem("level_ready")
        first_half = sem("first_half")
        first_copied = sem("first_copied")
        second_half = sem("second_half")
        inverse_ready = sem("inverse_ready")
        ks_ready = sem("ks_ready")
        rest_ready = sem("rest_ready")
        new_v = sem("new_v")
        new_v_copied = sem("new_v_copied")
        chunk_done = sem("chunk_done")
        state_ready = sem("state_ready")
        o_copied = sem("o_copied")
        forget_row = sem("forget_row")
        forget_copied = sem("forget_copied")
        scores_done = sem("scores_done")
        scores_taken = sem("scores_taken")
        exp_done = sem("exp_done")
        prob_ready = sem("prob_ready")
        prob_turned = sem("prob_turned")
        prob_copied = sem("prob_copied")
        pv_done = sem("pv_done")
        v_free = sem("v_free")
        out_ready = sem("out_ready")
        out_stored = sem("out_stored")

        block = ctx.enter_context(nc.Block())

        def ada_chunk_used(eng, k):
            if k in ADA_ON_PE:
                eng.wait_ge(ada_ps_ready, k + 1)
            else:
                eng.wait_ge(ada_sum_ready, ADA_ON_DVE.index(k) + 1)

        def tile(t, m):
            return t[:, bass.ds(m, 1), :].rearrange("p a t -> p (a t)") if not isinstance(m, int) else t[:, m, :]

        def conv_weight(name, taps, m, k):
            w = par[:, PCOL[name]:PCOL[name] + dict(PARAMS)[name]].rearrange("p (m k) -> p m k", k=taps)
            return w[:, bass.ds(m, 1), k:k + 1].rearrange("p a b -> p (a b)")

        def blocks(t, lv, odd):
            return t.rearrange("p c (g two n) -> p (c g) two n", two=2, n=2 ** lv)[:, :, odd, :]

        def taps_beside(j):
            return [n for n in range(POOL_TAPS) if n * 12 // POOL_TAPS == j]

        @block.sync
        def _(sp):
            def load(s, u, wait):
                if wait is not None:
                    sp.wait_ge(w_split, wait)
                sp.dma_start(raw[:, s, :], weights[bass.ds(u, 1), :, :].rearrange("a p n -> (a p) n")
                             ).then_inc(raw_landed[s], 16)

            def load_ada(k):
                if k >= ADA_BUFS:
                    ada_chunk_used(sp, k - ADA_BUFS)
                sp.dma_start(ada_w[:, k % ADA_BUFS, :, :], ada[k]).then_inc(ada_landed[k % ADA_BUFS], 16)

            sp.dma_start(par[:], params).then_inc(params_landed, 16)
            for k in range(2):
                load_ada(k)
            sp.dma_start(X[:], xT.rearrange("(k p) t -> p k t", p=P)).then_inc(inputs_landed, 16)
            for k in range(2, ADA_FIRST):
                load_ada(k)
                if 3 <= k < 3 + RING:
                    load(k - 3, k - 3, None)
            with sp.Fori(0, UNITS // RING - 1) as i:
                for s in range(RING):
                    load(s, i * RING + (RING + s), i * RING + (s + 1))
            for u in range(UNITS // RING * RING, UNITS):
                load(u % RING, u, u - RING + 1)
            for n in range(4):
                sp.wait_ge(out_ready, 2 * n + 2)
                sp.dma_start(out.rearrange("(k p) t -> p k t", p=P)[:, 2 * n:2 * n + 2, :], X[:, 2 * n:2 * n + 2, :]
                             ).then_inc(out_stored, 16)
            sp.wait_ge(out_stored, 64)

        @block.gpsimd
        def _(pool):
            def low(s, u1):
                pool.wait_ge(w_rounded, u1)
                nc.gpsimd.tensor_tensor(w_lo[:, s, :], raw[:, s, :], w_hi[:, s, :].bitcast(F32),
                                        ALU.subtract).then_inc(w_split, 1)

            def lows(start, count):
                with pool.Fori(0, count // RING) as i:
                    for s in range(RING):
                        low((start + s) % RING, i * RING + (start + s + 1))

            nc.gpsimd.memset(spare[:, 23:24], 0.0).then_inc(tap_added, 2)
            start = FIRST["short_in"] + AHEAD
            lows(0, start)
            for i in range(2):
                for j in range(12):
                    u = start + 12 * i + j
                    low(u % RING, u + 1)
                    for n in taps_beside(j):
                        if n:
                            pool.wait_ge(tap_scaled, i * POOL_TAPS + n + 1)
                            pool.wait_ge(tap_added, i * (POOL_TAPS - 1) + n + 1)
                            nc.gpsimd.tensor_tensor(UC[:, 6 + i, :], UC[:, 6 + i, :], ada_acc[:, (n - 1) % 2, :],
                                                    ALU.add).then_inc(tap_added, 1)
            start += 24
            lows(start, UNITS - start)
            for u in range(start + (UNITS - start) // RING * RING, UNITS):
                low(u % RING, u + 1)

        @block.scalar
        def _(act):
            st = Steps(act, act_steps)

            def round_unit(u, i=None, per=0):
                if u + (0 if i is None else per) >= UNITS + per * (i is not None):
                    return
                s = u % RING
                if i is None:
                    landed, free = 16 * (u // RING + 1), u - RING + 1
                else:
                    landed, free = i * (16 * per // RING) + 16 * (u // RING + 1), i * per + (u - RING + 1)
                act.wait_ge(raw_landed[s], landed)
                if u >= RING or i is not None:
                    act.wait_ge(w_used, free)
                nc.scalar.activation(w_hi[:, s, :], raw[:, s, :], ACT.Copy).then_inc(w_rounded, 1)

            def rstd_of(n, scale, eps):
                act.wait_ge(stat_ready, n)
                st.seq(nc.scalar.activation(rstd[:], stat[:], ACT.Ln, bias=eps[:], scale=scale))
                nc.scalar.activation(rstd[:], rstd[:], ACT.Exp, scale=-0.5).then_inc(rstd_ready, 1)

            def gate_pairs(phase, func, which):
                u0 = FIRST[phase]
                with act.Fori(0, COUNT[phase] // 4) as i:
                    for j in range(4):
                        if j % 2 == which:
                            act.wait_ge(w_used, i * 4 + (u0 + j + 1))
                            act.wait_ge(bank_free, i * 4 + (u0 + j // 2 * 2 + 2))
                            nc.scalar.activation(act_out[:, j // 2, :], bank[(u0 + j) % RING][:], func
                                                 ).then_inc(gated, 1)
                        round_unit(u0 + j + AHEAD, i, 4)

            def round_units(phase):
                u0 = FIRST[phase]
                n = min(COUNT[phase], UNITS - AHEAD - u0)
                with act.Fori(0, n // RING) as i:
                    for j in range(RING):
                        round_unit(u0 + j + AHEAD, i, RING)
                for u in range(u0 + n // RING * RING, u0 + n):
                    round_unit(u + AHEAD)

            def square_tile(k, m, src, out=None):
                act.wait_ge(x_new, 8 * k + m + 1)
                if m >= 2:
                    act.wait_ge(squares_added, 7 * k + m - 1)
                nc.scalar.activation(act_out[:, m % 2, :], src[:, m, :], ACT.Square).then_inc(tile_squared, 1)

            def mix_squares_units(k, phase):
                u0 = FIRST[phase]
                for j in range(KT):
                    square_tile(k, j, mix)
                    round_unit(u0 + j + AHEAD)

            def mix_squares_ffn(k, phase, tiles):
                u0 = FIRST[phase]
                for j in range(FT // 2):
                    round_unit(u0 + j + AHEAD)
                tiles(0)
                for j in range(FT // 2, FT - 1):
                    round_unit(u0 + j + AHEAD)
                tiles(4)
                round_unit(u0 + FT - 1 + AHEAD)

            def high_parts(k, name, j0, hi):
                for m in range(KT):
                    act.wait_ge(x_new, 8 * k + m + 1)
                    nc.scalar.activation(hi[:, m, :], X[:, m, :], ACT.Copy, scale=pcol(name, j0 + m)
                                         ).then_inc(hi_ready, 1)
                    square_tile(k, m, X)

            def gate_pairs_scaled(phase):
                u0 = FIRST[phase]
                pair0 = 0 if phase == "ffn_in_a" else FT
                with act.Fori(0, COUNT[phase] // 4) as i:
                    for j in range(4):
                        if j % 2 == 0:
                            act.wait_ge(a_scaled, i * 2 + (pair0 + j // 2 + 1))
                            nc.scalar.activation(act_out[:, j // 2, :], act_out[:, j // 2, :], ACT.Silu
                                                 ).then_inc(gated, 1)
                        round_unit(u0 + j + AHEAD, i, 4)

            act.wait_ge(params_landed, 16)
            nc.scalar.activation(silu_c[:], par[:, PCOL["c"]:PCOL["c"] + 8], ACT.Silu).then_inc(silu_c_ready, 1)
            act.wait_ge(inputs_landed, 16)
            for m in range(KT):
                if m >= 2:
                    act.wait_ge(stat_part, m - 1)
                nc.scalar.activation(act_out[:, m % 2, :], X[:, m, :], ACT.Square).then_inc(first_squares, 1)
            for n in range(AHEAD):
                round_unit(n)

            def load_ada(k):
                ada_chunk_used(act, k - ADA_BUFS)
                act.dma_start(ada_w[:, k % ADA_BUFS, :, :], ada[k]).then_inc(ada_landed[k % ADA_BUFS], 16)

            act.wait_ge(consts_ready, 1)
            rstd_of(1, 1.0 / D, eps6)
            gate_pairs("conf_in", ACT.Sigmoid, 1)
            u0 = FIRST["short_in"]
            with act.Fori(0, 2) as i:
                for j in range(12):
                    if j % 3 == 0:
                        act.wait_ge(w_used, i * 12 + (u0 + j + 1))
                        act.wait_ge(bank_free, i * 12 + (u0 + j + 2))
                        nc.scalar.activation(act_out[:, (j // 3) % 2, :], bank[(u0 + j) % RING][:], ACT.Copy
                                             ).then_inc(gated, 1)
                    round_unit(u0 + j + AHEAD, i, 12)
                    for n in taps_beside(j):
                        m = i + 6
                        weight = conv_weight("conv_conf_w", CONF_K, m, n)
                        if n == 0:
                            act.wait_ge(bank_free, u0 + RING)
                            nc.scalar.activation(tile(UC, m), tile(U, m)[:, 0:T], ACT.Identity, scale=weight,
                                                 bias=par[:, bass.ds(m + PCOL["conv_conf_b"], 1)]
                                                 ).then_inc(tap_scaled, 1)
                        else:
                            act.wait_ge(tap_added, i * (POOL_TAPS - 1) + n)
                            nc.scalar.activation(ada_acc[:, (n - 1) % 2, :], tile(U, m)[:, n:n + T], ACT.Copy,
                                                 scale=weight).then_inc(tap_scaled, 1)
            u0 = FIRST["mix_a"]
            for j in range(16):
                load_ada(ADA_FIRST + j)
                if j % 2 == 1:
                    act.wait_ge(w_used, u0 + j + 1)
                    act.wait_ge(bank_free, u0 + j // 2 * 2 + 2)
                    nc.scalar.activation(act_out[:, (j // 2) % 2, :], bank[(u0 + j) % RING][:], ACT.Sigmoid
                                         ).then_inc(gated, 1)
                round_unit(u0 + j + AHEAD)
                if j == 13:
                    rstd_of(3, 1.0 / D, eps5)
            u0 = FIRST["gate_b"]
            for j in range(8):
                act.wait_ge(w_used, u0 + j + 1)
                act.wait_ge(bank_free, u0 + j + RING)
                nc.scalar.activation(gate[:, j, :], bank[(u0 + j) % RING][:], ACT.Sigmoid).then_inc(bank_free, 1)
                round_unit(u0 + j + AHEAD)
                act.wait_ge(ln_scaled, j + 1)
                nc.scalar.activation(UC[:, j, :], UC[:, j, :], ACT.Silu, scale=pcol("conf_ln_g", j),
                                     bias=pcol("conf_ln_b", j)).then_inc(ln_silu, 1)
            round_units("conf_out")
            round_units("w_o")
            rstd_of(4, 1.0 / D, eps6)
            gate_pairs("ffn_in", ACT.Silu, 0)

            def last_tiles(m0):
                for m in range(m0, m0 + 4):
                    act.wait_ge(x_new, m + 1)
                    nc.scalar.activation(x_hi[:, m, :], X[:, m, :], ACT.Copy, scale=joint_gain[:, m:m + 1]
                                         ).then_inc(hi_ready, 1)
                    if m >= 1:
                        act.wait_ge(squares_added, m)
                    nc.scalar.activation(act_out[:, 0, :], X[:, m, :], ACT.Square)
                    nc.scalar.activation(act_out[:, 1, :], X[:, m, :], ACT.Square, scale=pcol("final_norm_g", m)
                                         ).then_inc(tile_squared, 1)

            mix_squares_ffn(0, "ffn_out", last_tiles)
            act.wait_ge(stat_ready, 5)
            st.seq(nc.scalar.activation(act_out[:, 0, :], stat[:], ACT.Ln, bias=eps6[:], scale=1.0 / D))
            nc.scalar.activation(act_out[:, 0, :], act_out[:, 0, :], ACT.Exp, scale=-0.5).then_inc(rstd_ready, 1)
            act.dma_start(small_raw[:], small_w).then_inc(inputs_landed, 16)
            act.dma_start(row[:], rows.partition_broadcast(P).rearrange("p a b -> p (a b)")).then_inc(inputs_landed, 16)
            act.wait_ge(rstd_joined, 1)
            st.seq(nc.scalar.activation(tmp[:], tmp[:], ACT.Ln, bias=eps6[:], scale=1.0 / D))
            nc.scalar.activation(tmp[:], tmp[:], ACT.Exp, scale=-0.5).then_inc(rstd_ready, 1)
            u0 = FIRST["gdn_qkv"]
            with act.Fori(0, 6) as i:
                for j in range(4):
                    round_unit(u0 + j + AHEAD, i, 4)
                    act.wait_ge(silu_in, i * 4 + (j + 1))
                    t = qkv[:, bass.ds(i * 4 + j, 1), :].rearrange("p a t -> p (a t)")
                    nc.scalar.activation(t, t, ACT.Silu).then_inc(silu_out, 1)

            def head_rstd_of(r, scale):
                act.wait_ge(sq_summed, r + 1)
                if r >= 2:
                    act.wait_ge(head_rstd_used, r - 1)
                b = act_out[:, r % 2, :]
                st.seq(nc.scalar.activation(b, bank[4 + r % 2][:], ACT.Ln, bias=eps6[:], scale=scale))
                nc.scalar.activation(b, b, ACT.Exp, scale=-0.5).then_inc(head_rstd, 1)

            u0 = FIRST["gdn_z"]
            act.wait_ge(tok_dve, 1)
            act.dma_start(tri[:], consts[:, 0:2, :]).then_inc(masks_landed, 16)
            for j in range(8):
                round_unit(u0 + j + AHEAD)
                if j == 0:
                    act.wait_ge(tok_dve, 2)
                    nc.scalar.activation(tok[:, 0, :], tok[:, 0, :], ACT.Exp, scale=-1.0)
                    st.seq(nc.scalar.activation(tok[:, 2, :], tok[:, 2, :], ACT.Exp, scale=-1.0))
                    nc.scalar.activation(tok[:, 2, :], tok[:, 2, :], ACT.Ln, bias=ones[:, 0:1])
                    nc.scalar.activation(tok[:, 3, 0:8], row[:, 0:8], ACT.Exp).then_inc(tok_act, 1)
                if j == 2:
                    act.wait_ge(tok_pe, 2)
                    nc.scalar.activation(tok[:, 5, :], bank[6][:, 64:96], ACT.Exp)
                    nc.scalar.activation(tok[:, 6, :], bank[6][:, 96:128], ACT.Exp).then_inc(tok_act, 1)
                if j == 4:
                    act.wait_ge(tok_dve, 4)
                    nc.scalar.activation(tok[:, 7, :], tok[:, 7, :], ACT.Exp).then_inc(tok_act, 1)
                head_rstd_of(2 * j, 1.0)
                head_rstd_of(2 * j + 1, 1.0)
            act.wait_ge(w_used, FIRST["gdn_out"])
            act.dma_start(masks_raw[:], consts[:, 2:, :]).then_inc(masks_landed, 16)
            act.wait_ge(bank_free, FIRST["gdn_out"] + RING)
            nc.scalar.activation(z_gate[:], z_gate[:], ACT.Silu).then_inc(z_ready, 1)

            def chunk_copies(p, c, part):
                for n in range(2):
                    k = p * 8 + c * 2 + n
                    if part == 0:
                        act.wait_ge(new_v, k + 1)
                        nc.scalar.activation(new_v_sb[n], bank[n][:, P:2 * P], ACT.Copy).then_inc(new_v_copied, 1)
                    else:
                        act.wait_ge(chunk_done, k + 1)
                        nc.scalar.activation(qkv[:, 16 + 2 * p + n, c * CH:(c + 1) * CH], bank[n][:, 2 * P:3 * P],
                                             ACT.Copy).then_inc(o_copied, 1)

            for p in range(HEADS // 2 + 1):
                if p < HEADS // 2:
                    for h in (2 * p, 2 * p + 1):
                        act.wait_ge(head_products, 4 * h + 1)
                        if h:
                            act.wait_ge(head_taken, h)
                        nc.scalar.activation(rstd[:], bank[0][:], ACT.Exp).then_inc(decay_row, 1)
                        act.wait_ge(diff_ready, h + 1)
                        nc.scalar.activation(act_out[:, h % 2, :], square[:], ACT.Exp).then_inc(decay_ready, 1)
                for lv in range(LEVELS):
                    if p < HEADS // 2 and lv >= 1:
                        for n in range(2):
                            act.wait_ge(first_half, p * 14 + lv * 2 + n + 1)
                            if lv >= 2 or p >= 1:
                                act.wait_ge(second_half, p * 12 + (lv - 1) * 2 + n - 1)
                            nc.scalar.activation(half[n][:], bank[4 + 2 * n][:], ACT.Copy).then_inc(first_copied, 1)
                    if p >= 1 and lv < NCH:
                        chunk_copies(p - 1, lv, 0)
                        chunk_copies(p - 1, lv, 1)
            for h in range(HEADS):
                head_rstd_of(16 + h, 1.0 / DH)
            mix_squares_units(1, "gdn_out")
            rstd_of(7, 1.0 / D, eps6)
            high_parts(2, "pre_ffn_norm_2", 0, x_hi)
            rstd_of(8, 1.0 / D, eps6)
            gate_pairs_scaled("ffn_in_a")
            mix_squares_ffn(3, "ffn_out_a", lambda m0: [square_tile(3, m, mix) for m in range(m0, m0 + 4)])
            rstd_of(9, 1.0 / D, eps6)
            high_parts(4, "kv_norm_2", 0, x_hi)
            rstd_of(10, 1.0 / D, eps6)
            for m in range(KT):
                nc.scalar.activation(q_hi[:, m, :], X[:, m, :], ACT.Copy, scale=pcol("pre_mix_norm_2", 8 + m)
                                     ).then_inc(hi_ready, 1)
            round_units("fox_k")
            round_units("fox_v")
            act.wait_ge(tok_dve, 5)
            st.seq(nc.scalar.activation(tok[:, 10:12, :], tok[:, 10:12, :], ACT.Exp, scale=-1.0))
            nc.scalar.activation(tok[:, 10:12, :], tok[:, 10:12, :], ACT.Ln, bias=ones[:, 0:1]).then_inc(tok_act, 1)
            act.wait_ge(w_used, FIRST["fox_q"])
            act.wait_ge(tok_pe, 3)
            act.dma_start(masks_raw[:], consts[:, 2:, :]).then_inc(masks_landed, 16)
            round_units("fox_q")

            def copy_prob(s):
                b = s % QB
                act.wait_ge(prob_turned, s + 1)
                if s >= 2:
                    act.wait_ge(pv_done, s - 1)
                nc.scalar.activation(prob_t[s % 2][:, 0:b + 1, :], bank[3 + s % 2][:, 0:(b + 1) * P], ACT.Copy
                                     ).then_inc(prob_copied, 1)

            STEPS = FOX_HEADS * QB
            for s in range(STEPS + 2):
                h, b = s // QB, s % QB
                if s < STEPS:
                    act.wait_ge(scores_taken, s + 1)
                    if s >= 2:
                        act.wait_ge(prob_turned, s - 1)
                    q = softmax[:, s % 2, :]
                    nc.scalar.activation(prob[s % 2][:, 0:(b + 1) * P], score[s % 2][:, 0:(b + 1) * P], ACT.Exp,
                                         scale=-1.0, bias=q[:, 0:1], accum_out=q[:, 1:2]).then_inc(exp_done, 1)
                if s >= 2:
                    copy_prob(s - 2)
            mix_squares_units(5, "fox_o")
            rstd_of(11, 1.0 / D, eps6)
            high_parts(6, "pre_ffn_norm_2", 8, x_hi)
            rstd_of(12, 1.0 / D, eps6)
            gate_pairs_scaled("ffn_in_b")
            mix_squares_ffn(7, "ffn_out_b", lambda m0: [square_tile(7, m, mix) for m in range(m0, m0 + 4)])
            rstd_of(13, 1.0 / D, eps6)

        @block.tensor
        def _(pe):
            def product(acc, s, t, hi, lo, k, start, stop):
                w = bass.ts(t, P)
                nc.tensor.matmul(acc, w_hi[:, s, w], hi[:, k, :], start=start, stop=False)
                nc.tensor.matmul(acc, w_hi[:, s, w], lo[:, k, :], start=False, stop=False)
                return nc.tensor.matmul(acc, w_lo[:, s, w], hi[:, k, :], start=False, stop=stop)

            def unit(u, hi, lo, ready, i=None, per=0):
                s = u % RING
                moved = 0 if i is None else i * per
                pe.wait_ge(w_split, moved + (u + 1))
                pe.wait_ge(bank_free, moved + (u + 1))
                for k in range(KT):
                    if ready is not None:
                        pe.wait_ge(x_ready, ready + k + 1)
                    last = product(bank[s][:], s, k, hi, lo, k, k == 0, k == KT - 1)
                last.then_inc(w_used, 1)

            def units(phase, hi, lo, ready, sums=()):
                u0, done = FIRST[phase], 0
                if ready is not None:
                    done = RING
                    for k in range(KT):
                        pe.wait_ge(x_ready, ready + k + 1)
                        for j in range(RING):
                            u = u0 + j
                            if k == 0:
                                pe.wait_ge(w_split, u + 1)
                                pe.wait_ge(bank_free, u + 1)
                            last = product(bank[u % RING][:], u % RING, k, hi, lo, k, k == 0, k == KT - 1)
                            if k == KT - 1:
                                last.then_inc(w_used, 1)
                                if j == RING - 2:
                                    for n in sums:
                                        sum_over_partitions(n)
                with pe.Fori(0, COUNT[phase] // RING - done // RING) as i:
                    for j in range(RING):
                        unit(u0 + done + j, hi, lo, None, i, RING)

            def small(which):
                for c in range(NCH):
                    for k in range(KT):
                        for t, (x, w) in enumerate(((x_hi, small_hi), (x_hi, small_lo), (x_lo, small_hi))):
                            last = nc.tensor.matmul(bank[6][:, c * 16:(c + 1) * 16], x[:, k, bass.ts(c, P)],
                                                    w[:, which, k, :], start=k == 0 and t == 0,
                                                    stop=k == KT - 1 and t == 2)
                for c in range(NCH):
                    last = nc.tensor.matmul(bank[6][:, 128 + c:129 + c], rstd[0:1, bass.ts(c, P)], ones[0:1, 0:1],
                                            start=True, stop=True)
                return last

            def ffn_out(phase, ready):
                u0 = FIRST[phase]
                for half in range(2):
                    for k2 in range(FT // 2):
                        u = u0 + half * (FT // 2) + k2
                        s = u % RING
                        pe.wait_ge(w_split, u + 1)
                        if k2 == 0:
                            pe.wait_ge(bank_free, u0 + RING)
                        if half == 0:
                            pe.wait_ge(x_ready, ready + 2 * k2 + 2)
                        for m in range(4):
                            for kk in range(2):
                                k = 2 * k2 + kk
                                last = product(bank[4 * half + m][:], s, kk * 4 + m, f_hi, f_lo, k,
                                               k == 0, k == FT - 1)
                        last.then_inc(w_used, 1)

            def sum_over_partitions(n):
                pe.wait_ge(sum_ready, n)
                b, t = (bank[6], square) if n == 5 else (stat, total)
                nc.tensor.matmul(b[:], ones[:], t[:], start=True, stop=True).then_inc(stat_ready, 1)

            def ada_columns(k):
                if k in ADA_ON_PE:
                    pe.wait_ge(ada_landed[k % ADA_BUFS], 16 * (k // ADA_BUFS + 1))
                else:
                    pe.wait_ge(ada_sum_ready, ADA_ON_DVE.index(k) + 1)
                for b in range(ADA_COLS // P):
                    col = ada_ps[:, 2 * k + b:2 * k + b + 1]
                    if k in ADA_ON_PE:
                        for j in range(KT):
                            last = nc.tensor.matmul(col, ada_w[:, k % ADA_BUFS, j, bass.ts(b, P)], silu_c[:, j:j + 1],
                                                    start=j == 0, stop=j == KT - 1)
                    else:
                        for j in range(2):
                            last = nc.tensor.matmul(col, ada_acc[:, ADA_ON_DVE.index(k) % 2, bass.ts(2 * j + b, P)], ones[:, 0:1],
                                                    start=j == 0, stop=j == 1)
                last.then_inc(ada_ps_ready, 1)

            pe.wait_ge(consts_ready, 1)
            pe.wait_ge(silu_c_ready, 1)
            ada_columns(0)
            for m in range(KT):
                pe.wait_ge(first_squares, m + 1)
                last = nc.tensor.matmul(stat[:], ones[:], act_out[:, m % 2, :], start=m == 0, stop=m == KT - 1)
                last.then_inc(stat_part if m < KT - 1 else stat_ready, 1)
            for k in range(1, ADA_FIRST):
                ada_columns(k)
            units("conf_in", x_hi, x_lo, 0)
            units("short_in", x_hi, x_lo, None)
            u0 = FIRST["mix_a"]
            for j in range(16):
                if j % 2 == 0:
                    unit(u0 + j, y_hi, y_lo, 8 if j == 0 else None)
                else:
                    unit(u0 + j, x_hi, x_lo, None)
                if j == 3:
                    sum_over_partitions(1)
                if j == 11:
                    sum_over_partitions(2)
                if j >= 2:
                    ada_columns(ADA_FIRST + j - 2)
            ada_columns(ADA_CHUNKS - 2)
            ada_columns(ADA_CHUNKS - 1)
            units("gate_b", x_hi, x_lo, None)
            units("conf_out", y_hi, y_lo, 16)
            units("w_o", x_hi, x_lo, 24)
            sum_over_partitions(3)
            units("ffn_in", x_hi, x_lo, 32)
            ffn_out("ffn_out", XR["ffn_h"])
            units("gdn_qkv", x_hi, x_lo, XR["gdn_x"], (4, 5))
            u0 = FIRST["gdn_z"]
            pe.wait_ge(tok_dve, 1)
            pe.wait_ge(rstd_joined, 2)
            small(0).then_inc(tok_pe, 1)

            def sum_head(r):
                pe.wait_ge(sq_ready, r + 1)
                if r >= 2:
                    pe.wait_ge(head_rstd, r - 1)
                nc.tensor.matmul(bank[4 + r % 2][:], ones[:], (square, total)[r % 2][:], start=True, stop=True
                                 ).then_inc(sq_summed, 1)

            beta, decay, upper, ident = tok[:, 0, :], tok[:, 4, :], tri[:, 0, :], tri[:, 1, :]
            for j in range(8):
                if j == 2:
                    pe.wait_ge(tok_dve, 3)
                    pe.wait_ge(masks_landed, 16)
                    nc.tensor.matmul(bank[6][:, 64:96], upper, decay, start=True, stop=True)
                    nc.tensor.matmul(bank[6][:, 96:128], ones[:], decay, start=True, stop=True
                                     ).then_inc(tok_pe, 1)
                unit(u0 + j, x_hi, x_lo, None)
                sum_head(2 * j)
                sum_head(2 * j + 1)

            def chunk_part(p, c, part):
                for n in range(2):
                    h, k = 2 * p + n, p * 8 + c * 2 + n
                    slot, cols, b = (p % 2) * 2 + n, slice(c * CH, (c + 1) * CH), bank[n]
                    if part == 0:
                        pe.wait_ge(state_ready, p * 10 + c * 2 + n + 1)
                        nc.tensor.matmul(b[:, 0:P], qkv[:, 8 + h, cols], state[:, n, :], start=True, stop=True
                                         ).then_inc(ks_ready, 1)
                    elif part == 1:
                        pe.wait_ge(rest_ready, k + 1)
                        nc.tensor.matmul(b[:, P:2 * P], inv_t[slot][:, c, :], rest_sb[n], start=True, stop=True
                                         ).then_inc(new_v, 1)
                    else:
                        pe.wait_ge(new_v_copied, k + 1)
                        if k >= 2:
                            pe.wait_ge(o_copied, k - 1)
                        nc.tensor.matmul(b[:, 2 * P:3 * P], state[:, n, :], qkv[:, h, cols], start=True, stop=False)
                        nc.tensor.matmul(b[:, 2 * P:3 * P], new_v_sb[n], attn[slot][:, c, :], start=False, stop=True)
                        nc.tensor.matmul(b[:, 3 * P:4 * P], key_dec[slot][:, c, :], new_v_sb[n], start=True,
                                         stop=True).then_inc(chunk_done, 1)

            for p in range(HEADS // 2 + 1):
                if p < HEADS // 2:
                    for h in (2 * p, 2 * p + 1):
                        if h == 0:
                            pe.wait_ge(bank_free, FIRST["gdn_out"] + RING)
                            pe.wait_ge(tok_dve, 4)
                            pe.wait_ge(head_rstd_used, 16)
                        else:
                            pe.wait_ge(head_taken, h)
                        if h >= 2 and h % 2 == 0:
                            pe.wait_ge(turned_used, 2 * h)
                            pe.wait_ge(o_copied, 0 if p < 2 else 8 * (p - 1))
                            pe.wait_ge(state_ready, 0 if p < 2 else 10 * (p - 1))
                        for c in range(NCH):
                            g = decay[:, c * HEADS + h:c * HEADS + h + 1].broadcast_to([P, P])
                            last = nc.tensor.matmul(bank[0][:, bass.ts(c, P)], g, upper, start=True, stop=True)
                        last.then_inc(head_products, 1)
                        for c in range(NCH):
                            g = beta[:, c * HEADS + h:c * HEADS + h + 1].broadcast_to([P, P])
                            last = nc.tensor.matmul(bank[1][:, bass.ts(c, P)], g, ident, start=True, stop=True)
                        last.then_inc(head_products, 1)
                        for c in range(NCH):
                            kc = qkv[:, 8 + h, bass.ts(c, P)]
                            last = nc.tensor.matmul(bank[2][:, bass.ts(c, P)], kc, kc, start=True, stop=True)
                        last.then_inc(head_products, 1)
                        for c in range(NCH):
                            last = nc.tensor.matmul(bank[3][:, bass.ts(c, P)], qkv[:, 8 + h, bass.ts(c, P)],
                                                    qkv[:, h, bass.ts(c, P)], start=True, stop=True)
                        last.then_inc(head_products, 1)
                for lv in range(LEVELS):
                    if p < HEADS // 2:
                        for n in range(2):
                            pe.wait_ge(level_ready, p * 14 + lv * 2 + n + 1)
                            if lv == 0:
                                pe.wait_ge(head_taken, 2 * p + 2)
                            else:
                                pe.wait_ge(inverse_ready, p * 14 + (lv - 1) * 2 + n + 1)
                            for c in range(NCH):
                                r = ident if lv == 0 else inv[n][:, c, :]
                                last = nc.tensor.matmul(bank[4 + 2 * n][:, bass.ts(c, P)],
                                                        level_a[n][lv % 2][:, c, :], r, start=True, stop=True)
                            last.then_inc(first_half, 1)
                    if p >= 1 and lv < NCH:
                        chunk_part(p - 1, lv, 0)
                    if p < HEADS // 2 and lv in (0, 1):
                        h = 2 * p + lv
                        for w in range(2):
                            if h >= 1:
                                pe.wait_ge(turned_used, 2 * h - 1 + w)
                            for c in range(NCH):
                                last = nc.tensor.transpose(bank[2 + w][:, bass.ts(c, P)],
                                                           qkv[:, 16 - 8 * w + h, bass.ts(c, P)], ident)
                            last.then_inc(turned, 1)
                    if p >= 1 and lv < NCH:
                        chunk_part(p - 1, lv, 1)
                    if p < HEADS // 2 and lv >= 1:
                        slot = (p % 2) * 2
                        for n in range(2):
                            pe.wait_ge(first_copied, p * 12 + (lv - 1) * 2 + n + 1)
                            if lv < LEVELS - 1:
                                for c in range(NCH):
                                    nc.tensor.matmul(bank[4 + 2 * n][:, bass.ts(c, P // 2)], inv_t[slot + n][:, c, :],
                                                     blocks(half[n][:, c:c + 1, :], lv, 0), start=True, stop=True)
                            for c in range(NCH):
                                last = nc.tensor.matmul(bank[5 + 2 * n][:, bass.ts(c, P // 2)], half[n][:, c, :],
                                                        blocks(inv_t[slot + n][:, c:c + 1, :], lv, 1),
                                                        start=True, stop=True)
                            last.then_inc(second_half, 1)
                    if p >= 1 and lv < NCH:
                        chunk_part(p - 1, lv, 2)
            for r in range(16, 24):
                sum_head(r)
            units("gdn_out", og_hi, og_lo, XR["gdn_o"])
            sum_over_partitions(6)
            units("ffn_in_a", x_hi, x_lo, XR["ffn_x_a"], (7,))
            ffn_out("ffn_out_a", XR["ffn_h_a"])
            sum_over_partitions(8)
            units("fox_k", x_hi, x_lo, XR["kv_x"], (9,))
            pe.wait_ge(rstd_ready, 9)
            small(1).then_inc(tok_pe, 1)
            u0 = FIRST["fox_v"]
            for hv in range(2):
                for k2 in range(KT // 2):
                    u = u0 + hv * (KT // 2) + k2
                    s = u % RING
                    pe.wait_ge(w_split, u + 1)
                    if k2 == 0:
                        pe.wait_ge(bank_free, u0 + RING)
                    for t in range(QB):
                        b = bank[4 * hv + t] if 4 * hv + t != 6 else bank[6]
                        if hv == 1 and k2 == 0 and t == 2:
                            pe.wait_ge(tok_dve, 5)
                        for kk in range(2):
                            k = 2 * k2 + kk
                            for i, (x, w) in enumerate(((x_hi, w_hi), (x_hi, w_lo), (x_lo, w_hi))):
                                last = nc.tensor.matmul(b[:], x[:, k, bass.ts(t, P)], w[:, s, bass.ts(kk, T)],
                                                        start=k == 0 and i == 0, stop=k == KT - 1 and i == 2)
                    last.then_inc(w_used, 1)
            pe.wait_ge(x_ready, XR["q_x"] + 8)
            units("fox_q", q_hi, q_lo, None)
            pe.wait_ge(tok_dve, 6)
            pe.wait_ge(v_free, 8)
            for c in range(NCH):
                last = nc.tensor.matmul(bank[7][0:16, bass.ts(c, P)], tok[:, 8:10, :].rearrange(
                    "p a b -> p (a b)")[:, c * 16:(c + 1) * 16], ident, start=True, stop=True)
            last.then_inc(tok_pe, 1)
            pe.wait_ge(masks_ready, 2)
            pe.wait_ge(bank_free, FIRST["fox_o"] + RING)
            STEPS = FOX_HEADS * QB

            def forget_on_partitions(h):
                pe.wait_ge(tok_dve, 7) if h == 0 else pe.wait_ge(forget_copied, h)
                pick = tri[0:16, 1, h:h + 1].broadcast_to([16, P])
                nc.tensor.matmul(bank[7][:], pick, forget_sum[:], start=True, stop=True).then_inc(forget_row, 1)

            forget_on_partitions(0)
            for s in range(STEPS + 3):
                if s < STEPS:
                    h, b = s // QB, s % QB
                    rows_ = slice(h % 2 * FOX_D, (h % 2 + 1) * FOX_D)
                    if s >= 3:
                        pe.wait_ge(scores_taken, s - 2)
                    acc = bank[s % 3]
                    nc.tensor.matmul(acc[:, 0:(b + 1) * P], qf[rows_, h // 2, bass.ts(b, P)],
                                     kf[rows_, h // 2, 0:(b + 1) * P], start=True, stop=False)
                    nc.tensor.matmul(acc[:, bass.ts(b, P)], masks[:, 8, :], masks[:, 9, :], start=False, stop=True
                                     ).then_inc(scores_done, 1)
                    if b == 1 and h + 1 < FOX_HEADS:
                        forget_on_partitions(h + 1)
                if 2 <= s < STEPS + 2:
                    s2 = s - 2
                    pe.wait_ge(prob_ready, s2 + 1)
                    if s2 >= 2:
                        pe.wait_ge(prob_copied, s2 - 1)
                    for kb in range(s2 % QB + 1):
                        last = nc.tensor.transpose(bank[3 + s2 % 2][:, bass.ts(kb, P)],
                                                   prob[s2 % 2][:, bass.ts(kb, P)], ident)
                    last.then_inc(prob_turned, 1)
                if s >= 3:
                    s3 = s - 3
                    h, b = s3 // QB, s3 % QB
                    rows_ = slice(h % 2 * FOX_D, (h % 2 + 1) * FOX_D)
                    pe.wait_ge(prob_copied, s3 + 1)
                    if b == 0 and h % 2 == 0 and h >= 4:
                        pe.wait_ge(x_ready, XR["fox_o"] + h // 2 - 1)
                    for kb in range(b + 1):
                        last = nc.tensor.matmul(bank[5 + h // 2 % 2][rows_, bass.ts(b, P)],
                                                vt[:, kb, h * FOX_D:(h + 1) * FOX_D], prob_t[s3 % 2][:, kb, :],
                                                start=kb == 0, stop=kb == b)
                    last.then_inc(pv_done, 1)
            units("fox_o", q_hi, q_lo, XR["fox_o"])
            sum_over_partitions(10)
            units("ffn_in_b", x_hi, x_lo, XR["ffn_x_b"], (11,))
            ffn_out("ffn_out_b", XR["ffn_h_b"])
            sum_over_partitions(12)

        @block.vector
        def _(dve):
            st = Steps(dve, dve_steps)
            V = nc.vector

            def split(src, hi, lo):
                st.seq(V.tensor_copy(hi, src))
                V.tensor_tensor(lo, src, hi.bitcast(F32), ALU.subtract).then_inc(x_ready, 1)

            def add_square(src, first):
                if first:
                    st.seq(V.tensor_tensor(total[:], src, src, ALU.mult))
                else:
                    st.seq(V.tensor_tensor(square[:], src, src, ALU.mult))
                    st.seq(V.tensor_tensor(total[:], total[:], square[:], ALU.add))

            def conv_taps(src, dst, odd, name, m, taps, bias=None, first=0, counted=True):
                marks = [None, None]
                for k in range(first, taps):
                    n = (k - first) % 2
                    acc, x, w = (dst, odd)[n], src[:, k:k + T], conv_weight(name, taps, m, k)
                    st.after(marks[n])
                    if k == first and bias is not None:
                        ins = V.tensor_scalar(acc, x, w, par[:, bass.ds(m + PCOL[bias], 1)], ALU.mult, ALU.add)
                    elif k < first + 2:
                        ins = V.tensor_scalar(acc, x, w, None, ALU.mult)
                    else:
                        ins = V.scalar_tensor_tensor(acc, x, w, acc, ALU.mult, ALU.add)
                    marks[n] = st.step(ins)
                    yield
                st.after(marks[0])
                st.after(marks[1])
                ins = V.tensor_tensor(dst, dst, odd, ALU.add)
                if counted:
                    st.seq(ins)
                yield ins

            given = []

            def give_back(n):
                V.memset(spare[:, len(given):len(given) + 1], 0.0).then_inc(bank_free, n)
                given.append(n)

            V.memset(eps6[:], 1e-6)
            V.memset(eps5[:], 1e-5).then_inc(bank_free, RING)
            V.memset(U[:, :, 0:CONF_K - 1], 0.0)
            V.memset(prod_pad[:, 0:3], 0.0)
            V.memset(ones[:], 1.0).then_inc(consts_ready, 1)
            dve.wait_ge(consts_ready, 1)

            def ada_chunk(k):
                b, n_th = k % ADA_BUFS, ADA_ON_DVE.index(k)
                chain = (tmp[:, 0:ADA_COLS], tmp[:, ADA_COLS:T],
                         prod_pad[:, 3:3 + ADA_COLS], prod_pad[:, 3 + ADA_COLS:3 + T])
                dve.wait_ge(ada_landed[b], 16 * (k // ADA_BUFS + 1))
                if n_th:
                    dve.wait_ge(ada_sum_ready, n_th)
                marks = [None] * 4
                for j in range(KT):
                    n = j % 4
                    st.after(marks[n])
                    marks[n] = st.step(
                        V.tensor_scalar(chain[n], ada_w[:, b, j, :], silu_c[:, j:j + 1], None, ALU.mult) if j < 4 else
                        V.scalar_tensor_tensor(chain[n], ada_w[:, b, j, :], silu_c[:, j:j + 1], chain[n],
                                               ALU.mult, ALU.add))
                    yield
                for mark in marks:
                    st.after(mark)
                if n_th >= 2:
                    dve.wait_ge(ada_ps_ready, ADA_ON_DVE[n_th - 2] + 1)
                V.tensor_tensor(ada_acc[:, n_th % 2, :], tmp[:], prod_pad[:, 3:], ALU.add).then_inc(ada_sum_ready, 1)
                yield

            dve.wait_ge(inputs_landed, 16)
            dve.wait_ge(params_landed, 16)
            dve.wait_ge(silu_c_ready, 1)
            for k in ADA_ON_DVE:
                if k < ADA_FIRST:
                    for _ in ada_chunk(k):
                        pass
            b_ada = par[:, PCOL["b_ada"]:PCOL["b_ada"] + 48]
            dve.wait_ge(ada_ps_ready, ADA_FIRST)
            st.seq(V.tensor_tensor(mod[:, 0:16], ada_ps[:, 0:16], b_ada[:, 0:16], ALU.add))
            g = par[:, PCOL["norm_mix_g"]:PCOL["norm_mix_g"] + 8]
            st.seq(V.scalar_tensor_tensor(gain[:, 0, :], mod[:, 8:16], 1.0, g, ALU.add, ALU.mult))

            def modulated_input(n, which, shift):
                dve.wait_ge(rstd_ready, n)
                buf, marks, highs = (tmp, square), {}, {}
                for t in range(KT + 2):
                    if t < KT:
                        if t >= 2:
                            dve.wait_ge(x_ready, XSET[which] + t - 1)
                        b = buf[t % 2]
                        marks[t] = st.step(V.scalar_tensor_tensor(b[:], X[:, t, :], gain[:, which, t:t + 1], rstd[:],
                                                                  ALU.mult, ALU.mult))
                    if 1 <= t <= KT:
                        m = t - 1
                        st.after(highs[m])
                        V.tensor_tensor(x_lo[:, m, :], buf[m % 2][:], x_hi[:, m, :].bitcast(F32), ALU.subtract
                                        ).then_inc(x_ready, 1)
                    if t < KT:
                        st.after(marks[t])
                        marks[t] = st.step(V.tensor_scalar(buf[t % 2][:], buf[t % 2][:],
                                                           mod[:, shift + t:shift + t + 1], None, ALU.add))
                        st.after(marks[t])
                        highs[t] = st.step(V.tensor_copy(x_hi[:, t, :], buf[t % 2][:]))

            XSET = [0, 32]
            modulated_input(1, 0, 0)

            u0 = FIRST["conf_in"]
            with st.loop(4, CONF_K + 1) as i:
                taps = conv_taps(tile(U, i), tile(UC, i), square[:], "conv_conf_w", i, CONF_K, "conv_conf_b")
                for j in range(2):
                    dve.wait_ge(gated, i * 2 + (j + 1))
                    V.tensor_tensor(tile(U, i * 2 + j)[:, CONF_K - 1:], bank[(u0 + 2 * j) % RING][:],
                                    act_out[:, j, :], ALU.mult).then_inc(bank_free, 2)
                    if j == 0:
                        dve.wait_ge(bank_free, i * 4 + (u0 + 2 + RING))
                    for _ in range((CONF_K + 1) // 2):
                        next(taps)
            u0 = FIRST["short_in"]

            def long_convolutions(i):
                yield from conv_taps(tile(U, i + 4), tile(UC, i + 4), square[:], "conv_conf_w", i + 4, CONF_K,
                                     "conv_conf_b")
                yield from conv_taps(tile(U, i + 6), total[:], square[:], "conv_conf_w", i + 6, CONF_K,
                                     first=POOL_TAPS)
                dve.wait_ge(tap_added, i * (POOL_TAPS - 1) + (POOL_TAPS + 1))
                st.seq(V.tensor_tensor(tile(UC, i + 6), tile(UC, i + 6), total[:], ALU.add))
                yield

            with st.loop(2, 4 * (SHORT_K + 2) + 2 * CONF_K - POOL_TAPS + 3) as i:
                for r in range(4):
                    m = i * 4 + r
                    cu = u0 + 3 * r
                    if r == 0:
                        fill = long_convolutions(i)

                    def filled(count):
                        for _ in range(count):
                            next(fill, None)
                    dve.wait_ge(gated, i * 4 + (8 + r + 1))
                    dve.wait_ge(w_used, i * 12 + (cu + 2))
                    V.tensor_tensor(prod_pad[:, 3:], bank[(cu + 1) % RING][:], act_out[:, r % 2, :],
                                    ALU.mult).then_inc(bank_free, 2)
                    filled(1)
                    dve.wait_ge(bank_free, i * 12 + (cu + 2 + RING))
                    for _ in conv_taps(prod_pad[:, 4 - SHORT_K:], tmp[:], rstd[:], "conv_short_w", m, SHORT_K):
                        filled(2)
                    dve.wait_ge(w_used, i * 12 + (cu + 3))
                    V.tensor_tensor(tmp[:], tmp[:], bank[(cu + 2) % RING][:], ALU.mult).then_inc(bank_free, 1)
                    filled(1)
                    dve.wait_ge(bank_free, i * 12 + (cu + 3 + RING))
                    high = st.step(V.tensor_copy(tile(y_hi, m), tmp[:]))
                    filled(1)
                    st.after(high)
                    V.tensor_tensor(tile(y_lo, m), tmp[:], tile(y_hi, m).bitcast(F32), ALU.subtract
                                    ).then_inc(x_ready, 1)
                    filled(2)
                    dve.wait_ge(x_ready, i * 4 + (8 + r + 1))
                    if r == 3:
                        for _ in fill:
                            pass
            def layer_norm():
                both, marks = (total, square), [None, None]
                for m in range(2, KT + 1):
                    n = m % 2
                    st.after(marks[n])
                    if m < KT:
                        a = UC[:, m - 2, :] if m < 4 else both[n][:]
                        marks[n] = st.step(V.tensor_tensor(both[n][:], a, UC[:, m, :], ALU.add))
                    else:
                        st.after(marks[1])
                        V.tensor_tensor(total[:], total[:], square[:], ALU.add).then_inc(sum_ready, 1)
                    yield
                dve.wait_ge(stat_ready, 2)
                mean = st.step(V.tensor_scalar(rstd[:], stat[:], 1.0 / D, None, ALU.mult))
                yield
                st.after(mean)
                marks, squared, added = {}, {}, None
                for t in range(KT + 2):
                    if t < KT:
                        marks[t] = st.step(V.tensor_tensor(UC[:, t, :], UC[:, t, :], rstd[:], ALU.subtract))
                        yield
                    if 1 <= t <= KT:
                        m = t - 1
                        st.after(marks[m])
                        st.after(added)
                        squared[m] = st.step(V.tensor_tensor((total if m == 0 else square)[:], UC[:, m, :],
                                                             UC[:, m, :], ALU.mult))
                        yield
                        if m >= 1:
                            st.after(squared[m])
                            ins = V.tensor_tensor(total[:], total[:], square[:], ALU.add)
                            if m == KT - 1:
                                ins.then_inc(sum_ready, 1)
                            else:
                                added = st.step(ins)
                            yield
                dve.wait_ge(rstd_ready, 2)
                for m in range(KT):
                    V.tensor_tensor(UC[:, m, :], UC[:, m, :], rstd[:], ALU.mult).then_inc(ln_scaled, 1)
                    yield

            u0, norm = FIRST["mix_a"], layer_norm()
            for j in range(8):
                dve.wait_ge(gated, 16 + j + 1)
                V.tensor_tensor(mixed[:, j, :], bank[(u0 + 2 * j) % RING][:], act_out[:, j % 2, :], ALU.mult
                                ).then_inc(bank_free, 2)
                for n in range(2):
                    for t, _ in enumerate(ada_chunk(ADA_FIRST + 2 * j + n)):
                        if t % 2 == 1 and (j == 0 and (n, t) != (1, 7) or 2 <= j < 5 or j == 7):
                            next(norm, None)
            for _ in norm:
                pass
            dve.wait_ge(ada_ps_ready, ADA_CHUNKS)
            st.seq(V.tensor_tensor(mod[:, 16:48], ada_ps[:, 16:48], b_ada[:, 16:48], ALU.add))
            st.seq(V.tensor_tensor(joint_gain[:], par[:, PCOL["final_norm_g"]:PCOL["final_norm_g"] + 8],
                                   par[:, PCOL["pre_mix_norm_2"]:PCOL["pre_mix_norm_2"] + 8], ALU.mult))
            g = par[:, PCOL["norm_ffn_g"]:PCOL["norm_ffn_g"] + 8]
            st.seq(V.scalar_tensor_tensor(gain[:, 1, :], mod[:, 32:40], 1.0, g, ALU.add, ALU.mult))
            for m in range(KT):
                dve.wait_ge(ln_silu, m + 1)
                split(UC[:, m, :], y_hi[:, m, :], y_lo[:, m, :])
            dve.wait_ge(bank_free, FIRST["conf_out"] + RING)
            u0 = FIRST["conf_out"]
            for j in range(8):
                dve.wait_ge(w_used, u0 + j + 1)
                V.tensor_tensor(tmp[:], bank[(u0 + j) % RING][:], gate[:, j, :], ALU.mult).then_inc(bank_free, 1)
                dve.wait_ge(bank_free, u0 + j + 1 + RING)
                st.seq(V.tensor_tensor(tmp[:], tmp[:], mixed[:, j, :], ALU.add))
                split(tmp[:], x_hi[:, j, :], x_lo[:, j, :])
                dve.wait_ge(x_ready, 24 + j + 1)

            def add_to_residual(banks, when, scale, freed):
                for j in range(KT):
                    dve.wait_ge(w_used, when(j))
                    ins = V.scalar_tensor_tensor(X[:, j, :], banks[j][:], mod[:, scale + j:scale + j + 1],
                                                 X[:, j, :], ALU.mult, ALU.add)
                    if freed(j):
                        ins.then_inc(bank_free, freed(j)[0])
                        dve.wait_ge(bank_free, freed(j)[1])
                    else:
                        st.seq(ins)
                    if j == 0:
                        st.seq(V.tensor_tensor(total[:], X[:, j, :], X[:, j, :], ALU.mult))
                    else:
                        st.seq(V.tensor_tensor(square[:], X[:, j, :], X[:, j, :], ALU.mult))
                        ins = V.tensor_tensor(total[:], total[:], square[:], ALU.add)
                        st.seq(ins) if j < KT - 1 else ins.then_inc(sum_ready, 1)

            u0 = FIRST["w_o"]
            add_to_residual([bank[(u0 + j) % RING] for j in range(8)], lambda j: u0 + j + 1, 16,
                            lambda j: (1, u0 + j + 1 + RING))
            modulated_input(3, 1, 24)
            def ffn_in(phase, gated0, ready):
                u1 = FIRST[phase]
                with st.loop(FT // 2, 2) as i:
                    for j in range(2):
                        dve.wait_ge(gated, i * 2 + (gated0 + j + 1))
                        dve.wait_ge(w_used, i * 4 + (u1 + 2 * j + 2))
                        V.tensor_tensor(tmp[:], bank[(u1 + 2 * j + 1) % RING][:], act_out[:, j, :], ALU.mult
                                        ).then_inc(bank_free, 2)
                        dve.wait_ge(bank_free, i * 4 + (u1 + 2 * j + 2 + RING))
                        m = i * 2 + j
                        st.seq(V.tensor_copy(tile(f_hi, m), tmp[:]))
                        V.tensor_tensor(tile(f_lo, m), tmp[:], tile(f_hi, m).bitcast(F32), ALU.subtract
                                        ).then_inc(x_ready, 1)
                        dve.wait_ge(x_ready, i * 2 + (ready + j + 1))

            def sum_squares(src, j):
                if j == 0:
                    st.seq(V.tensor_tensor(total[:], src, src, ALU.mult))
                else:
                    st.seq(V.tensor_tensor(square[:], src, src, ALU.mult))
                    ins = V.tensor_tensor(total[:], total[:], square[:], ALU.add)
                    st.seq(ins) if j < KT - 1 else ins.then_inc(sum_ready, 1)

            ffn_in("ffn_in", 24, XR["ffn_h"])
            u2 = FIRST["ffn_out"]
            for j in range(KT):
                dve.wait_ge(w_used, u2 + (FT // 2) * (1 + j // 4))
                V.scalar_tensor_tensor(X[:, j, :], bank[j][:], mod[:, 40 + j:41 + j], X[:, j, :],
                                       ALU.mult, ALU.add).then_inc(x_new, 1)
                if j == KT - 1:
                    dve.wait_ge(x_new, KT)
                    give_back(FT)
                dve.wait_ge(hi_ready, j + 1)
                V.scalar_tensor_tensor(x_lo[:, j, :], X[:, j, :], joint_gain[:, j:j + 1], x_hi[:, j, :].bitcast(F32),
                                       ALU.mult, ALU.subtract).then_inc(x_ready, 1)
                dve.wait_ge(tile_squared, j + 1)
                dve.wait_ge(squares_added, j)
                if j == 0:
                    V.tensor_copy(total[:], act_out[:, 0, :])
                    V.tensor_copy(square[:], act_out[:, 1, :]).then_inc(squares_added, 1)
                elif j < KT - 1:
                    V.tensor_tensor(total[:], total[:], act_out[:, 0, :], ALU.add)
                    V.tensor_tensor(square[:], square[:], act_out[:, 1, :], ALU.add).then_inc(squares_added, 1)
                else:
                    V.tensor_tensor(total[:], total[:], act_out[:, 0, :], ALU.add).then_inc(sum_ready, 1)
                    V.tensor_tensor(square[:], square[:], act_out[:, 1, :], ALU.add).then_inc(sum_ready, 1)

            def ffn_in_scaled(phase, gated0, pair0, ready):
                u1 = FIRST[phase]
                with st.loop(FT // 2, 4) as i:
                    for j in range(2):
                        dve.wait_ge(w_used, i * 4 + (u1 + 2 * j + 1))
                        V.tensor_tensor(act_out[:, j, :], bank[(u1 + 2 * j) % RING][:], rstd[:], ALU.mult
                                        ).then_inc(a_scaled, 1)
                        dve.wait_ge(a_scaled, i * 2 + (pair0 + j + 1))
                        dve.wait_ge(w_used, i * 4 + (u1 + 2 * j + 2))
                        V.tensor_tensor(tmp[:], bank[(u1 + 2 * j + 1) % RING][:], rstd[:], ALU.mult
                                        ).then_inc(bank_free, 2)
                        dve.wait_ge(gated, i * 2 + (gated0 + j + 1))
                        dve.wait_ge(bank_free, i * 4 + (u1 + 2 * j + 2 + RING))
                        st.seq(V.tensor_tensor(tmp[:], tmp[:], act_out[:, j, :], ALU.mult))
                        m = i * 2 + j
                        st.seq(V.tensor_copy(tile(f_hi, m), tmp[:]))
                        V.tensor_tensor(tile(f_lo, m), tmp[:], tile(f_hi, m).bitcast(F32), ALU.subtract
                                        ).then_inc(x_ready, 1)
                        dve.wait_ge(x_ready, i * 2 + (ready + j + 1))

            def add_tile_square(k, m):
                dve.wait_ge(tile_squared, 8 * k + m + 1)
                if m == 0:
                    ins = V.tensor_copy(total[:], act_out[:, 0, :])
                else:
                    dve.wait_ge(squares_added, 7 * k + m)
                    ins = V.tensor_tensor(total[:], total[:], act_out[:, m % 2, :], ALU.add)
                ins.then_inc(squares_added if m < KT - 1 else sum_ready, 1)

            def residual_and_input(n, k, name, j0, in_name, in_j0, ready, high0):
                dve.wait_ge(rstd_ready, n)
                buf, marks = (tmp, square), {}
                for t in range(KT + 2):
                    if t < KT:
                        if t >= 2:
                            dve.wait_ge(x_new, 8 * k + t - 1)
                        marks[t] = st.step(V.scalar_tensor_tensor(buf[t % 2][:], mix[:, t, :], pcol(name, j0 + t),
                                                                  rstd[:], ALU.mult, ALU.mult))
                    if t >= 2:
                        m = t - 2
                        dve.wait_ge(hi_ready, high0 + m + 1)
                        V.scalar_tensor_tensor(x_lo[:, m, :], X[:, m, :], pcol(in_name, in_j0 + m),
                                               x_hi[:, m, :].bitcast(F32), ALU.mult, ALU.subtract
                                               ).then_inc(x_ready, 1)
                    if 1 <= t <= KT:
                        m = t - 1
                        st.after(marks[m])
                        V.tensor_tensor(X[:, m, :], X[:, m, :], buf[m % 2][:], ALU.add).then_inc(x_new, 1)
                    if t >= 2:
                        add_tile_square(k, t - 2)

            def take_mix(k, banks, when, freed):
                for j in range(KT):
                    dve.wait_ge(w_used, when(j))
                    V.tensor_copy(mix[:, j, :], banks[j][:]).then_inc(x_new, 1)
                    if freed(j):
                        give_back(freed(j))
                    if j >= 1:
                        add_tile_square(k, j - 1)
                add_tile_square(k, KT - 1)

            def take_mix_units(k, phase):
                u0 = FIRST[phase]
                take_mix(k, [bank[(u0 + j) % RING] for j in range(8)], lambda j: u0 + j + 1, lambda j: 1)

            def take_mix_ffn(k, phase):
                u2 = FIRST[phase]
                take_mix(k, bank, lambda j: u2 + (FT // 2) * (1 + j // 4), lambda j: FT if j == KT - 1 else 0)

            dve.wait_ge(rstd_ready, 4)
            dve.wait_ge(stat_ready, 6)
            st.seq(V.tensor_tensor(tmp[:], bank[6][:], act_out[:, 0, :], ALU.mult))
            V.tensor_tensor(tmp[:], tmp[:], act_out[:, 0, :], ALU.mult).then_inc(rstd_joined, 1)
            dve.wait_ge(rstd_ready, 5)
            V.tensor_tensor(rstd[:], tmp[:], act_out[:, 0, :], ALU.mult).then_inc(rstd_joined, 1)
            dve.wait_ge(rstd_joined, 2)
            dve.wait_ge(inputs_landed, 48)
            sh = small_hi[:].rearrange("p a k n -> p (a k n)")
            st.seq(V.tensor_copy(sh, small_raw[:]))
            V.tensor_tensor(small_lo[:].rearrange("p a k n -> p (a k n)"), small_raw[:], sh.bitcast(F32),
                            ALU.subtract).then_inc(tok_dve, 1)
            u0 = FIRST["gdn_qkv"]
            with st.loop(6, 4 * 4 + 1) as i:
                st.seq(V.scalar_tensor_tensor(tile(X, i), tile(X, i), par[:, bass.ds(i + PCOL["final_norm_g"], 1)],
                                              act_out[:, 0, :], ALU.mult, ALU.mult))
                for j in range(4):
                    m = i * 4 + j
                    dve.wait_ge(w_used, i * 4 + (u0 + j + 1))
                    V.tensor_tensor(prod_pad[:, 3:], bank[(u0 + j) % RING][:], rstd[:], ALU.mult
                                    ).then_inc(bank_free, 1)
                    dve.wait_ge(bank_free, i * 4 + (u0 + j + 1 + RING))
                    *taps, last = conv_taps(prod_pad, tile(qkv, m), tmp[:], "gdn_conv_2", m, 4, counted=False)
                    last.then_inc(silu_in, 1)
                    dve.wait_ge(silu_in, i * 4 + (j + 1))

            for m in (6, 7):
                st.seq(V.scalar_tensor_tensor(X[:, m, :], X[:, m, :], pcol("final_norm_g", m), act_out[:, 0, :],
                                              ALU.mult, ALU.mult))

            def square_head(r, src):
                if r >= 2:
                    dve.wait_ge(sq_summed, r - 1)
                V.tensor_tensor((square, total)[r % 2][:], src, src, ALU.mult).then_inc(sq_ready, 1)

            u0 = FIRST["gdn_z"]
            dt = row[:, 8:16].unsqueeze(1).broadcast_to([P, NCH, HEADS])

            def byhead(n):
                return tok[:, n, :].rearrange("p (c h) -> p c h", h=HEADS)
            dve.wait_ge(silu_out, 24)
            square_head(0, qkv[:, 0, :])
            for j in range(8):
                if j == 0:
                    dve.wait_ge(tok_pe, 1)
                    ba = bank[6][:, 0:64].rearrange("p (c n) -> p c n", n=16)
                    st.seq(V.tensor_copy(tok[:, 12, 0:4], bank[6][:, 128:132]))
                    rcol = tok[:, 12, 0:4].unsqueeze(2).broadcast_to([P, NCH, HEADS])
                    st.seq(V.tensor_tensor(byhead(0), ba[:, :, 0:8], rcol, ALU.mult))
                    st.seq(V.tensor_tensor(byhead(1), ba[:, :, 8:16], rcol, ALU.mult))
                    st.seq(V.tensor_tensor(byhead(1), byhead(1), dt, ALU.add))
                    V.scalar_tensor_tensor(tok[:, 2, :], tok[:, 1, :], -1.0, tok[:, 1, :], ALU.mult, ALU.max).then_inc(tok_dve, 1)
                if j == 1:
                    dve.wait_ge(tok_act, 1)
                    st.seq(V.tensor_scalar(tok[:, 0, :], tok[:, 0, :], 1.0, None, ALU.add))
                    st.seq(V.reciprocal(tok[:, 0, :], tok[:, 0, :]))
                    st.seq(V.scalar_tensor_tensor(tok[:, 1, :], tok[:, 1, :], 0.0, tok[:, 2, :], ALU.max, ALU.add))
                    ea = tok[:, 3, 0:8].unsqueeze(1).broadcast_to([P, NCH, HEADS])
                    V.scalar_tensor_tensor(byhead(4), byhead(1), -1.0, ea, ALU.mult, ALU.mult).then_inc(tok_dve, 1)
                if j == 3:
                    dve.wait_ge(tok_act, 2)
                    st.seq(V.tensor_copy(tok[:, 8, :], bank[6][:, 64:96]))
                    st.seq(V.scalar_tensor_tensor(tok[:, 9, :], tok[:, 0, :], -1.0, tok[:, 5, :], ALU.mult, ALU.mult))
                    V.tensor_tensor(tok[:, 7, :], bank[6][:, 96:128], tok[:, 8, :], ALU.subtract
                                    ).then_inc(tok_dve, 1)
                dve.wait_ge(w_used, u0 + j + 1)
                V.tensor_tensor(z_gate[:, j, :], bank[(u0 + j) % RING][:], rstd[:], ALU.mult).then_inc(bank_free, 1)
                for r in (2 * j, 2 * j + 1):
                    if r < 15:
                        square_head(r + 1, qkv[:, r + 1, :])
                    dve.wait_ge(head_rstd, r + 1)
                    V.scalar_tensor_tensor(qkv[:, r, :], qkv[:, r, :], DH ** -0.5 if r < HEADS else 1.0,
                                           act_out[:, r % 2, :], ALU.mult, ALU.mult).then_inc(head_rstd_used, 1)
            dve.wait_ge(masks_landed, 32)
            V.tensor_copy(masks[:], masks_raw[:]).then_inc(masks_ready, 1)
            dve.wait_ge(masks_ready, 1)
            dve.wait_ge(tok_act, 3)

            def perhead(n, h):
                return byhead(n)[:, :, h:h + 1].broadcast_to([P, NCH, P])

            def four(b):
                return b[:].rearrange("p (c n) -> p c n", c=NCH)

            def mask4(n):
                return masks[:, n, :].unsqueeze(1).broadcast_to([P, NCH, P])
            ident4 = tri[:, 1, :].unsqueeze(1).broadcast_to([P, NCH, P])

            def chunk_rest(p, c):
                for n in range(2):
                    h, k = 2 * p + n, p * 8 + c * 2 + n
                    dve.wait_ge(ks_ready, k + 1)
                    V.scalar_tensor_tensor(rest_sb[n], bank[n][:, 0:P], tok[:, 9, c * 8 + h:c * 8 + h + 1],
                                           beta_v[(p % 2) * 2 + n][:, c, :], ALU.mult, ALU.add
                                           ).then_inc(rest_ready, 1)

            def chunk_state(p, c):
                for n in range(2):
                    h, k = 2 * p + n, p * 8 + c * 2 + n
                    dve.wait_ge(o_copied, k + 1)
                    V.scalar_tensor_tensor(state[:, n, :], state[:, n, :], tok[:, 6, c * 8 + h:c * 8 + h + 1],
                                           bank[n][:, 3 * P:4 * P], ALU.mult, ALU.add).then_inc(state_ready, 1)

            for p in range(HEADS // 2 + 1):
                if p < HEADS // 2:
                    for n in range(2):
                        h, slot = 2 * p + n, (p % 2) * 2 + n
                        sq4 = square[:].rearrange("p (c n) -> p c n", c=NCH)
                        dec4 = act_out[:, n, :].rearrange("p (c n) -> p c n", c=NCH)
                        dve.wait_ge(decay_row, h + 1)
                        st.seq(V.tensor_tensor(sq4, four(bank[0]), perhead(8, h), ALU.subtract))
                        V.tensor_tensor(sq4, sq4, mask4(0), ALU.add).then_inc(diff_ready, 1)
                        dve.wait_ge(head_products, 4 * h + 4)
                        st.seq(V.tensor_tensor(qkv[:, h, :], qkv[:, h, :], rstd[:], ALU.mult))
                        dve.wait_ge(decay_ready, h + 1)
                        V.tensor_tensor(attn[slot][:], four(bank[3]), dec4, ALU.mult)
                        st.seq(V.tensor_tensor(lower_t[n][:], four(bank[2]), dec4, ALU.mult))
                        V.tensor_tensor(lower_t[n][:], lower_t[n][:], four(bank[1]), ALU.mult).then_inc(head_taken, 1)
                        dve.wait_ge(head_taken, h + 1)
                        V.tensor_tensor(level_a[n][0][:], lower_t[n][:], mask4(1), ALU.mult).then_inc(level_ready, 1)
                if p >= 1:
                    for n in range(2):
                        V.memset(state[:, n, :], 0.0).then_inc(state_ready, 1)
                for lv in range(LEVELS):
                    if p < HEADS // 2 and lv + 1 < LEVELS:
                        for n in range(2):
                            if lv >= 1:
                                dve.wait_ge(first_half, p * 14 + (lv - 1) * 2 + n + 1)
                            V.tensor_tensor(level_a[n][(lv + 1) % 2][:], lower_t[n][:], mask4(2 + lv), ALU.mult
                                            ).then_inc(level_ready, 1)
                    if p >= 1 and lv < NCH:
                        chunk_rest(p - 1, lv)
                    if p < HEADS // 2:
                        for n in range(2):
                            slot = (p % 2) * 2 + n
                            if lv == 0:
                                dve.wait_ge(level_ready, p * 14 + n + 1)
                                st.seq(V.tensor_tensor(inv_t[slot][:], ident4, level_a[n][0][:], ALU.subtract))
                                dve.wait_ge(first_half, p * 14 + n + 1)
                                V.tensor_tensor(inv[n][:], ident4, four(bank[4 + 2 * n]), ALU.subtract
                                                ).then_inc(inverse_ready, 1)
                            else:
                                dve.wait_ge(second_half, p * 12 + (lv - 1) * 2 + n + 1)
                                for t, side in ((inv[n], 0), (inv_t[slot], 1)):
                                    if side == 0 and lv == LEVELS - 1:
                                        continue
                                    t = blocks(t[:], lv, side)
                                    y = bank[4 + 2 * n + side][:, 0:T // 2].rearrange("p (g n) -> p g n", n=2 ** lv)
                                    ins = V.tensor_tensor(t, t, y, ALU.subtract)
                                ins.then_inc(inverse_ready, 1)
                        if lv in (0, 1):
                            h, slot = 2 * p + lv, (p % 2) * 2 + lv
                            dve.wait_ge(turned, 2 * h + 1)
                            V.tensor_tensor(beta_v[slot][:], four(bank[2]), perhead(0, h), ALU.mult
                                            ).then_inc(turned_used, 1)
                            dve.wait_ge(turned, 2 * h + 2)
                            V.tensor_tensor(key_dec[slot][:], four(bank[3]), perhead(7, h), ALU.mult
                                            ).then_inc(turned_used, 1)
                    if p >= 1 and lv < NCH:
                        chunk_state(p - 1, lv)
            dve.wait_ge(o_copied, 32)
            dve.wait_ge(z_ready, 1)
            square_head(16, qkv[:, 16, :])
            for h in range(HEADS):
                if h + 1 < HEADS:
                    square_head(17 + h, qkv[:, 17 + h, :])
                dve.wait_ge(head_rstd, 17 + h)
                V.scalar_tensor_tensor(tmp[:], qkv[:, 16 + h, :], pcol("gdn_out_norm_2", 0), act_out[:, h % 2, :],
                                       ALU.mult, ALU.mult).then_inc(head_rstd_used, 1)
                dve.wait_ge(head_rstd_used, 17 + h)
                st.seq(V.tensor_tensor(tmp[:], tmp[:], z_gate[:, h, :], ALU.mult))
                split(tmp[:], og_hi[:, h, :], og_lo[:, h, :])
                dve.wait_ge(x_ready, XR["gdn_o"] + h + 1)
            take_mix_units(1, "gdn_out")
            residual_and_input(6, 2, "post_mix_norm_2", 0, "pre_ffn_norm_2", 0, XR["ffn_x_a"], 8)
            dve.wait_ge(rstd_ready, 7)
            ffn_in_scaled("ffn_in_a", 24 + FT, 0, XR["ffn_h_a"])
            take_mix_ffn(3, "ffn_out_a")
            residual_and_input(8, 4, "post_ffn_norm_2", 0, "kv_norm_2", 0, XR["kv_x"], 16)
            dve.wait_ge(rstd_ready, 9)
            for m in range(KT):
                dve.wait_ge(hi_ready, 24 + m + 1)
                V.scalar_tensor_tensor(q_lo[:, m, :], X[:, m, :], pcol("pre_mix_norm_2", 8 + m),
                                       q_hi[:, m, :].bitcast(F32), ALU.mult, ALU.subtract).then_inc(x_ready, 1)
            u0 = FIRST["fox_k"]
            for j in range(8):
                dve.wait_ge(w_used, u0 + j + 1)
                V.tensor_tensor(kf[:, j, :], bank[(u0 + j) % RING][:], rstd[:], ALU.mult).then_inc(bank_free, 1)
            soft, part = (tok[:, n:n + 2, :].rearrange("p a b -> p (a b)") for n in (8, 10))
            bf = row[:, 16:32].unsqueeze(1).broadcast_to([P, NCH, 16])
            dve.wait_ge(tok_pe, 3)
            st.seq(V.tensor_copy(tok[:, 12, 0:4], bank[6][:, 128:132]))
            soft3 = soft.rearrange("p (c n) -> p c n", n=16)
            st.seq(V.tensor_tensor(soft3, bank[6][:, 0:64].rearrange("p (c n) -> p c n", n=16),
                                   tok[:, 12, 0:4].unsqueeze(2).broadcast_to([P, NCH, 16]), ALU.mult))
            st.seq(V.tensor_tensor(soft3, soft3, bf, ALU.add))
            V.scalar_tensor_tensor(part, soft, -1.0, soft, ALU.mult, ALU.max).then_inc(tok_dve, 1)
            st.seq(V.tensor_scalar(soft, soft, -1.0, 0.0, ALU.mult, ALU.max))
            dve.wait_ge(tok_act, 4)
            V.tensor_tensor(soft, soft, part, ALU.add).then_inc(tok_dve, 1)
            u0 = FIRST["fox_v"]
            for hv in range(2):
                dve.wait_ge(w_used, u0 + 4 * (hv + 1))
                for t in range(QB):
                    V.tensor_scalar(vt[:, t, bass.ts(hv, T)], bank[4 * hv + t][:], tok[:, 12, t:t + 1], None,
                                    ALU.mult).then_inc(v_free, 1)
            dve.wait_ge(v_free, 8)
            give_back(8)
            u0 = FIRST["fox_q"]
            for j in range(8):
                dve.wait_ge(w_used, u0 + j + 1)
                V.scalar_tensor_tensor(qf[:, j, :], bank[(u0 + j) % RING][:], FOX_D ** -0.5, rstd[:],
                                       ALU.mult, ALU.mult).then_inc(bank_free, 1)
            dve.wait_ge(masks_landed, 48)
            V.tensor_copy(masks[:], masks_raw[:]).then_inc(masks_ready, 1)
            dve.wait_ge(tok_pe, 4)
            st.seq(V.memset(square[0:16, :], 1.0))
            V.tensor_tensor_scan(forget_sum[:], square[0:16, :], bank[7][0:16, :], 0.0, ALU.mult, ALU.add
                                 ).then_inc(tok_dve, 1)
            dve.wait_ge(masks_ready, 2)
            STEPS = FOX_HEADS * QB

            def take_heads(t):
                dve.wait_ge(pv_done, 8 * (t + 1))
                o = bank[5 + t % 2][:]
                st.seq(V.tensor_copy(q_hi[:, t, :], o))
                V.tensor_tensor(q_lo[:, t, :], o, q_hi[:, t, :].bitcast(F32), ALU.subtract).then_inc(x_ready, 1)

            for s in range(STEPS + 1):
                if s < STEPS:
                    h, b = s // QB, s % QB
                    e = (b + 1) * P
                    if b == 0:
                        dve.wait_ge(forget_row, h + 1)
                        V.tensor_copy(forget[h % 2][:], bank[7][:]).then_inc(forget_copied, 1)
                        dve.wait_ge(forget_copied, h + 1)
                    dve.wait_ge(scores_done, s + 1)
                    if s >= 2:
                        dve.wait_ge(exp_done, s - 1)
                    V.tensor_tensor_reduce(out=score[s % 2][:, 0:e], in0=bank[s % 3][:, 0:e],
                                           in1=forget[h % 2][:, 0:e], scale=-1.0, scalar=3e38, op0=ALU.add,
                                           op1=ALU.min, accum_out=softmax[:, s % 2, 0:1]).then_inc(scores_taken, 1)
                if s >= 1:
                    s1 = s - 1
                    h1, e = s1 // QB, (s1 % QB + 1) * P
                    q = softmax[:, s1 % 2, :]
                    dve.wait_ge(exp_done, s1 + 1)
                    st.seq(V.reciprocal(q[:, 2:3], q[:, 1:2]))
                    V.tensor_scalar(prob[s1 % 2][:, 0:e], prob[s1 % 2][:, 0:e], q[:, 2:3], None, ALU.mult
                                    ).then_inc(prob_ready, 1)
                if s >= 12 and (s - 12) % 8 == 0:
                    take_heads((s - 12) // 8)
            take_heads(7)
            take_mix_units(5, "fox_o")
            residual_and_input(10, 6, "post_mix_norm_2", 8, "pre_ffn_norm_2", 8, XR["ffn_x_b"], 32)
            dve.wait_ge(rstd_ready, 11)
            ffn_in_scaled("ffn_in_b", 24 + 2 * FT, FT, XR["ffn_h_b"])
            take_mix_ffn(7, "ffn_out_b")
            dve.wait_ge(rstd_ready, 12)
            buf, marks = (tmp, square), {}
            for t in range(KT + 1):
                if t < KT:
                    if t >= 2:
                        dve.wait_ge(out_ready, t - 1)
                    marks[t] = st.step(V.scalar_tensor_tensor(buf[t % 2][:], mix[:, t, :],
                                                              pcol("post_ffn_norm_2", 8 + t), rstd[:],
                                                              ALU.mult, ALU.mult))
                if t >= 1:
                    st.after(marks[t - 1])
                    V.tensor_tensor(X[:, t - 1, :], X[:, t - 1, :], buf[(t - 1) % 2][:], ALU.add
                                    ).then_inc(out_ready, 1)


def unit_tiles(w):
    return w.reshape(KT, P, -1, P).transpose(2, 1, 0, 3).reshape(-1, P, UNIT)


def ffn_out_units(w):
    return w.reshape(FT // 2, 2, P, 2, 4, P).transpose(3, 0, 2, 1, 4, 5).reshape(-1, P, UNIT)


def paired(*parts):
    return np.stack(parts, axis=1).reshape(-1, P, UNIT)


def columns(v, name):
    v = v.reshape(-1, v.shape[-1] // P, P)
    v = v.transpose(2, 1, 0) if "conv_" in name and not name.endswith("_b") or name == "gdn_conv_2" \
        else v.transpose(2, 0, 1)
    return v.reshape(P, -1)


def constant_tiles():
    a, b = np.arange(P)[:, None], np.arange(P)[None, :]
    tiles = [a <= b, a == b, np.where(a <= b, 0.0, -1e30)]
    for lv in range(LEVELS):
        n = 2 ** lv
        tiles.append((a // (2 * n) == b // (2 * n)) & (a // n % 2 == 0) & (b // n % 2 == 1))
    tiles += [a == b, np.where(a >= b, 0.0, -1e30)]
    return np.ascontiguousarray(np.stack([t.astype(np.float32) for t in tiles]).transpose(1, 0, 2))


def kernel(**inputs):
    import concourse.bacc as _bacc
    from concourse.bass_utils import run_bass_kernel_spmd as _run

    a = {k: np.asarray(v) for k, v in inputs.items()}
    w_in = unit_tiles(a["w_in"][0])
    b_u, c_u, v_u, vc_u, gl_u, ga_u, gb_u = (w_in[8 * n:8 * n + 8] for n in range(7))
    ffn = unit_tiles(a["w_ffn_in"][0])
    gdn = a["gdn_w_in_2"][0]
    ffn_2 = []
    for n in range(2):
        f = unit_tiles(a["w_ffn_in_2"][n])
        ffn_2.append((paired(f[:FT], f[FT:]), ffn_out_units(a["w_ffn_out_2"][n])))
    weights = np.concatenate([
        paired(vc_u, gl_u), paired(c_u, v_u, b_u), paired(unit_tiles(a["w_short_out"][0]), ga_u), gb_u,
        unit_tiles(a["w_conf_out"][0]), unit_tiles(a["w_o"][0]), paired(ffn[:FT], ffn[FT:]),
        ffn_out_units(a["w_ffn_out"][0]),
        unit_tiles(gdn[:, :4096]), unit_tiles(a["gdn_w_out_2"][0]), *ffn_2[0],
        unit_tiles(a["w_kv_2"][:, :1024]),
        a["w_kv_2"][:, 1024:2048].reshape(4, 2, P, 2, T).transpose(3, 0, 2, 1, 4).reshape(-1, P, UNIT),
        unit_tiles(a["fox_w_q_2"][0]), unit_tiles(a["fox_w_o_2"][0]), *ffn_2[1]])
    small = np.stack([gdn[:, 4096:], a["w_kv_2"][:, 2048:]]).reshape(2, KT, P, 16).transpose(2, 0, 1, 3)
    rows = np.concatenate([a["gdn_a_log_2"].ravel(), a["gdn_dt_bias_2"].ravel(), a["b_forget_2"]]).reshape(1, 32)
    params = np.concatenate([columns(a[name], name) for name, _ in PARAMS], axis=1)
    ada = np.ascontiguousarray(a["w_ada"][0].reshape(KT, P, ADA_CHUNKS, ADA_COLS).transpose(2, 1, 0, 3))
    arrays = {"x_t": np.ascontiguousarray(a["x"][0].T), "params": np.ascontiguousarray(params),
              "weights": np.ascontiguousarray(weights), "ada": ada,
              "small_w": np.ascontiguousarray(small.reshape(P, -1)), "rows": rows, "consts": constant_tiles()}
    nc = _bacc.Bacc("TRN2", target_bir_lowering=False, num_devices=1)
    args = [nc.dram_tensor(n, v.shape, F32, kind="ExternalInput").ap() for n, v in arrays.items()]
    out = nc.dram_tensor("out_t", (D, T), F32, kind="ExternalOutput").ap()
    program(nc, *args, out)
    r = _run(nc, [arrays], core_ids=[0])
    return r.results[0]["out_t"].T.reshape(1, T, D)
```

```python
from contextlib import ExitStack, contextmanager

import concourse.bass as bass
import numpy as np
from concourse import mybir

F32 = mybir.dt.float32
F32R = mybir.dt.float32r
BF16 = mybir.dt.bfloat16
ACT = mybir.ActivationFunctionType
ALU = mybir.AluOpType

P = 128
D = 1024
T = 512
KT = D // P
DFF = 2816
FT = DFF // P
RING = 4
AHEAD = RING
UNIT = 8 * P
SHORT_K, CONF_K = 3, 31
POOL_TAPS = 15
ADA_COLS = 256
ADA_BUFS = 3
ADA_CHUNKS = 6 * D // ADA_COLS
ADA_FIRST = 2 * D // ADA_COLS
ADA_ON_PE = (0, 2, 4, 6)
ADA_ON_DVE = [k for k in range(ADA_CHUNKS) if k not in ADA_ON_PE]

PARAMS = [("norm_mix_g", 8), ("norm_ffn_g", 8), ("final_norm_g", 8), ("conv_conf_b", 8), ("conf_ln_g", 8),
          ("conf_ln_b", 8), ("c", 8), ("b_ada", 48), ("conv_short_w", 8 * SHORT_K), ("conv_conf_w", 8 * CONF_K),
          ("pre_mix_norm_2", 16), ("post_mix_norm_2", 16), ("pre_ffn_norm_2", 16), ("post_ffn_norm_2", 16),
          ("kv_norm_2", 8), ("gdn_conv_2", 24 * 4), ("gdn_out_norm_2", 1), ("b_forget_2", 1)]
PCOL, _n = {}, 0
for _name, _w in PARAMS:
    PCOL[_name] = _n
    _n += _w
NPARAM = _n

PHASES = [("conf_in", 16), ("short_in", 24), ("mix_a", 16), ("gate_b", 8), ("conf_out", 8), ("w_o", 8),
          ("ffn_in", 2 * FT), ("ffn_out", FT),
          ("gdn_qkv", 24), ("gdn_ba", 1), ("gdn_z", 8), ("gdn_out", 8), ("ffn_in_a", 2 * FT), ("ffn_out_a", FT),
          ("fox_k", 8), ("fox_f", 1), ("fox_v", 8), ("fox_q", 8), ("fox_o", 8), ("ffn_in_b", 2 * FT), ("ffn_out_b", FT)]
FIRST, _n = {}, 0
for _name, _w in PHASES:
    FIRST[_name] = _n
    _n += _w
UNITS = _n
COUNT = dict(PHASES)

INPUTS = [("h1", 8), ("short", 8), ("conf", 8), ("mixed", 8), ("ffn_x", 8), ("ffn_h", FT),
          ("gdn_x", 8), ("gdn_o", 8), ("ffn_x_a", 8), ("ffn_h_a", FT),
          ("kv_x", 8), ("q_x", 8), ("fox_o", 8), ("ffn_x_b", 8), ("ffn_h_b", FT)]
XR, _n = {}, 0
for _name, _w in INPUTS:
    XR[_name] = _n
    _n += _w

HEADS, DH = 8, 128
CH = 128
NCH = T // CH
LEVELS = 7
FOX_HEADS, FOX_D = 16, 64
QB = T // P
NCONST = 2 + 3 + LEVELS


LN_EXP = "natural_log_exp_and_others"
BIG_BYTES = 91072


class Steps:

    def __init__(self, eng, sem):
        self.eng, self.sem, self.n, self.i, self.per = eng, sem, 0, None, 0

    @contextmanager
    def loop(self, count, per):
        start = self.n
        with self.eng.Fori(0, count) as i:
            self.i, self.per = i, per
            yield i
            assert self.n - start == per, (self.n - start, per)
        self.i, self.n = None, start + count * per

    def value(self):
        return self.n if self.i is None else self.n + self.i * self.per

    def step(self, ins):
        ins.then_inc(self.sem, 1)
        self.n += 1
        return self.value()

    def after(self, mark):
        if mark is not None:
            self.eng.wait_ge(self.sem, mark)

    def wait(self):
        self.eng.wait_ge(self.sem, self.value())

    def seq(self, ins):
        self.step(ins)
        self.wait()


def program(nc, xT, params, weights, ada, rows, consts, out):
    ctx = ExitStack()
    with ctx:
        def at(name, where, shape, dt=F32):
            return nc.alloc_sbuf_tensor_at(name, shape, dt, offset=where)

        place = [-(-nc.sbuf_base // 32) * 32]

        def sb(name, shape, dt=F32):
            t = at(name, place[0], shape, dt)
            place[0] += -(-int(np.prod(shape[1:])) * 4 // 32) * 32
            return t

        raw = sb("raw", [P, RING, UNIT])
        w_hi = sb("w_hi", [P, RING, UNIT], F32R)
        w_lo = sb("w_lo", [P, RING, UNIT], F32R)
        X = sb("X", [P, KT, T])
        XB = place[0]
        x_hi = sb("x_hi", [P, KT, T], F32R)
        x_lo = sb("x_lo", [P, KT, T], F32R)
        par = sb("par", [P, NPARAM])
        mod = sb("mod", [P, 48])
        gain = sb("gain", [P, 2, KT])
        silu_c = sb("silu_c", [P, KT])
        ones = sb("ones", [P, P])
        eps6 = sb("eps6", [P, 1])
        eps5 = sb("eps5", [P, 1])
        spare = sb("spare", [P, 24])
        joint_gain = sb("joint_gain", [P, KT])
        total = sb("total", [P, T])
        square = sb("square", [P, T])
        rstd = sb("rstd", [P, T])
        act_out = sb("act_out", [P, 2, T])
        tmp = sb("tmp", [P, T])
        prod_pad = sb("prod_pad", [P, 3 + T])
        ada_acc = at("ada_acc", place[0], [P, 2, 2 * ADA_COLS])
        place[0] += 4 * ADA_COLS
        tri = at("tri", place[0] - 4 * ADA_COLS, [P, 2, P])
        place[0] += 8 * ADA_COLS
        row = sb("row", [P, 16])
        tok = sb("tok", [P, 16, NCH * HEADS])
        BIG = place[0]
        assert BIG + BIG_BYTES <= nc.sbuf_usable_end, (BIG, nc.sbuf_usable_end)
        f_hi = at("f_hi", BIG, [P, FT, T], F32R)
        f_lo = at("f_lo", BIG + FT * T * 4, [P, FT, T], F32R)
        held = at("held", BIG + (2 * FT - 4) * T * 4, [P, 4, T])
        U = at("U", BIG, [P, KT, CONF_K - 1 + T])
        UC = at("UC", BIG + 17344, [P, KT, T])
        y_hi = at("y_hi", BIG + 33728, [P, KT, T], F32R)
        y_lo = at("y_lo", BIG + 50112, [P, KT, T], F32R)
        ada_w = at("ada_w", BIG + 66496, [P, ADA_BUFS, KT, ADA_COLS])
        gate = at("gate", BIG + 66496, [P, KT, T])
        mixed = U[:, :, 0:T]
        qkv = at("qkv", BIG, [P, 3 * HEADS, T])
        z_gate = at("z_gate", BIG + 49152, [P, HEADS, T])
        og_hi = at("og_hi", BIG, [P, KT, T], F32R)
        og_lo = at("og_lo", BIG + 16384, [P, KT, T], F32R)
        inv_t = [at(f"inv_t{n}", BIG + 65536 + 2048 * n, [P, NCH, CH]) for n in range(4)]
        attn = [at(f"attn{n}", BIG + 73728 + 2048 * n, [P, NCH, CH]) for n in range(4)]
        beta_v = [at(f"beta_v{n}", BIG + 81920 + 2048 * n, [P, NCH, DH]) for n in range(4)]
        inv = [at(f"inv{n}", XB + 2048 * n, [P, NCH, CH]) for n in range(2)]
        half = [at(f"half{n}", XB + 4096 + 2048 * n, [P, NCH, CH]) for n in range(2)]
        level_a = [[at(f"level_a{n}{b}", XB + 8192 + 4096 * n + 2048 * b, [P, NCH, CH]) for b in range(2)]
                   for n in range(2)]
        lower_t = [at(f"lower_t{n}", XB + 16384 + 2048 * n, [P, NCH, CH]) for n in range(2)]
        state = at("state", XB + 20480, [P, 2, DH])
        masks = at("masks", XB + 21504, [P, NCONST - 2, P], BF16)
        masks_raw = at("masks_raw", XB + 8192, [P, NCONST - 2, P])
        key_dec = [at(f"key_dec{n}", XB + 24576 + 2048 * n, [P, NCH, DH]) for n in range(4)]
        new_v_sb = [tmp[:, n * P:(n + 1) * P] for n in range(2)]
        rest_sb = [tmp[:, (2 + n) * P:(3 + n) * P] for n in range(2)]
        mix = at("mix", XB, [P, KT, T])
        kf = at("kf", BIG, [P, KT, T])
        vt = at("vt", BIG + 16384, [P, QB, D])
        qf = at("qf", BIG + 32768, [P, KT, T])
        q_hi = at("q_hi", BIG + 49152, [P, KT, T], F32R)
        q_lo = at("q_lo", BIG + 65536, [P, KT, T], F32R)
        score = [at(f"score{n}", XB + 2048 * n, [P, T]) for n in range(2)]
        prob = [at(f"prob{n}", XB + 4096 + 2048 * n, [P, T]) for n in range(2)]
        prob_t = [at(f"prob_t{n}", XB + 8192 + 2048 * n, [P, QB, P]) for n in range(2)]
        forget = [at(f"forget{n}", XB + 12288 + 2048 * n, [P, T]) for n in range(2)]
        forget_sum = at("forget_sum", XB + 16384, [16, T])
        softmax = at("softmax", XB + 18432, [P, 4, 4])

        def pcol(name, j):
            return par[:, PCOL[name] + j:PCOL[name] + j + 1]

        bank = [ctx.enter_context(nc.psum_tensor(f"bank{b}", [P, T], F32)) for b in range(8)]
        stat = bank[7]
        ada_ps = bank[6]

        def sem(name):
            return ctx.enter_context(nc.semaphore(name))

        raw_landed = [sem(f"raw_landed{s}") for s in range(RING)]
        w_rounded = sem("w_rounded")
        pool_steps = sem("pool_steps")
        tap_scaled = sem("tap_scaled")
        tap_added = sem("tap_added")
        w_split = sem("w_split")
        w_used = sem("w_used")
        tail_done = sem("tail_done")
        bank_free = sem("bank_free")
        x_ready = sem("x_ready")
        gated = sem("gated")
        inputs_landed = sem("inputs_landed")
        params_landed = sem("params_landed")
        consts_ready = sem("consts_ready")
        sum_ready = sem("sum_ready")
        stat_ready = sem("stat_ready")
        rstd_ready = sem("rstd_ready")
        silu_c_ready = sem("silu_c_ready")
        ada_landed = [sem(f"ada_landed{s}") for s in range(ADA_BUFS)]
        ada_sum_ready = sem("ada_sum_ready")
        ada_ps_ready = sem("ada_ps_ready")
        ln_scaled = sem("ln_scaled")
        ln_silu = sem("ln_silu")
        act_steps = sem("act_steps")
        dve_steps = sem("dve_steps")
        first_squares = sem("first_squares")
        stat_part = sem("stat_part")
        x_new = sem("x_new")
        hi_ready = sem("hi_ready")
        tile_squared = sem("tile_squared")
        squares_added = sem("squares_added")
        rstd_joined = sem("rstd_joined")
        a_scaled = sem("a_scaled")
        silu_in = sem("silu_in")
        silu_out = sem("silu_out")
        sq_ready = sem("sq_ready")
        sq_summed = sem("sq_summed")
        head_rstd = sem("head_rstd")
        head_rstd_used = sem("head_rstd_used")
        tok_pe = sem("tok_pe")
        tok_act = sem("tok_act")
        tok_dve = sem("tok_dve")
        masks_landed = sem("masks_landed")
        masks_ready = sem("masks_ready")
        z_ready = sem("z_ready")
        head_products = sem("head_products")
        decay_row = sem("decay_row")
        diff_ready = sem("diff_ready")
        decay_ready = sem("decay_ready")
        head_taken = sem("head_taken")
        turned = sem("turned")
        turned_used = sem("turned_used")
        level_ready = sem("level_ready")
        first_half = sem("first_half")
        first_copied = sem("first_copied")
        second_half = sem("second_half")
        inverse_ready = sem("inverse_ready")
        ks_ready = sem("ks_ready")
        rest_ready = sem("rest_ready")
        new_v = sem("new_v")
        new_v_copied = sem("new_v_copied")
        chunk_done = sem("chunk_done")
        state_ready = sem("state_ready")
        o_copied = sem("o_copied")
        forget_row = sem("forget_row")
        forget_copied = sem("forget_copied")
        scores_done = sem("scores_done")
        scores_taken = sem("scores_taken")
        exp_done = sem("exp_done")
        prob_ready = sem("prob_ready")
        prob_turned = sem("prob_turned")
        prob_copied = sem("prob_copied")
        pv_done = sem("pv_done")
        v_free = sem("v_free")
        out_ready = sem("out_ready")
        out_stored = sem("out_stored")

        block = ctx.enter_context(nc.Block())

        def ada_chunk_used(eng, k):
            if k in ADA_ON_PE:
                eng.wait_ge(ada_ps_ready, k + 1)
            else:
                eng.wait_ge(ada_sum_ready, ADA_ON_DVE.index(k) + 1)

        def tile(t, m):
            return t[:, bass.ds(m, 1), :].rearrange("p a t -> p (a t)") if not isinstance(m, int) else t[:, m, :]

        def conv_weight(name, taps, m, k):
            w = par[:, PCOL[name]:PCOL[name] + dict(PARAMS)[name]].rearrange("p (m k) -> p m k", k=taps)
            return w[:, bass.ds(m, 1), k:k + 1].rearrange("p a b -> p (a b)")

        def blocks(t, lv, odd):
            return t.rearrange("p c (g two n) -> p (c g) two n", two=2, n=2 ** lv)[:, :, odd, :]

        outs = (prod_pad[:, 3:], rstd[:])

        def taps_beside(j):
            return [n for n in range(POOL_TAPS) if n * 12 // POOL_TAPS == j]

        @block.sync
        def _(sp):
            def load(s, u, wait):
                if wait is not None:
                    sp.wait_ge(w_split, wait)
                sp.dma_start(raw[:, s, :], weights[bass.ds(u, 1), :, :].rearrange("a p n -> (a p) n")
                             ).then_inc(raw_landed[s], 16)

            def load_ada(k):
                if k >= ADA_BUFS:
                    ada_chunk_used(sp, k - ADA_BUFS)
                sp.dma_start(ada_w[:, k % ADA_BUFS, :, :], ada[k]).then_inc(ada_landed[k % ADA_BUFS], 16)

            sp.dma_start(par[:], params).then_inc(params_landed, 16)
            for k in range(2):
                load_ada(k)
            sp.dma_start(X[:], xT.rearrange("(k p) t -> p k t", p=P)).then_inc(inputs_landed, 16)
            for k in range(2, ADA_FIRST):
                load_ada(k)
                if 3 <= k < 3 + RING:
                    load(k - 3, k - 3, None)
            with sp.Fori(0, UNITS // RING - 1) as i:
                for s in range(RING):
                    load(s, i * RING + (RING + s), i * RING + (s + 1))
            for u in range(UNITS // RING * RING, UNITS):
                load(u % RING, u, u - RING + 1)
            for n in range(4):
                sp.wait_ge(out_ready, 2 * n + 2)
                sp.dma_start(out.rearrange("(k p) t -> p k t", p=P)[:, 2 * n:2 * n + 2, :], X[:, 2 * n:2 * n + 2, :]
                             ).then_inc(out_stored, 16)
            sp.wait_ge(out_stored, 64)

        @block.gpsimd
        def _(pool):
            def low(s, u1):
                pool.wait_ge(w_rounded, u1)
                nc.gpsimd.tensor_tensor(w_lo[:, s, :], raw[:, s, :], w_hi[:, s, :].bitcast(F32),
                                        ALU.subtract).then_inc(w_split, 1)

            def lows(start, count):
                with pool.Fori(0, count // RING) as i:
                    for s in range(RING):
                        low((start + s) % RING, i * RING + (start + s + 1))
                for u in range(start + count // RING * RING, start + count):
                    low(u % RING, u + 1)

            nc.gpsimd.memset(spare[:, 23:24], 0.0).then_inc(tap_added, 2)
            start = FIRST["short_in"] + AHEAD
            lows(0, start)
            for i in range(2):
                for j in range(12):
                    u = start + 12 * i + j
                    low(u % RING, u + 1)
                    for n in taps_beside(j):
                        if n:
                            pool.wait_ge(tap_scaled, i * POOL_TAPS + n + 1)
                            pool.wait_ge(tap_added, i * (POOL_TAPS - 1) + n + 1)
                            nc.gpsimd.tensor_tensor(UC[:, 6 + i, :], UC[:, 6 + i, :], ada_acc[:, (n - 1) % 2, :],
                                                    ALU.add).then_inc(tap_added, 1)
            start += 24
            lows(start, FIRST["gdn_out"] + RING - start)
            pool.wait_ge(z_ready, 1)
            for h in range(HEADS - 2):
                pool.wait_ge(head_rstd_used, 17 + h)
                o = outs[h % 2]
                nc.gpsimd.tensor_tensor(o, o, z_gate[:, h, :], ALU.mult).then_inc(pool_steps, 1)
                pool.wait_ge(pool_steps, 2 * h + 1)
                nc.gpsimd.tensor_copy(og_hi[:, h, :], o).then_inc(pool_steps, 1)
                pool.wait_ge(pool_steps, 2 * h + 2)
                nc.gpsimd.tensor_tensor(og_lo[:, h, :], o, og_hi[:, h, :].bitcast(F32), ALU.subtract
                                        ).then_inc(x_ready, 1)
            start = FIRST["gdn_out"] + RING
            lows(start, UNITS - start)

        @block.scalar
        def _(act):
            st = Steps(act, act_steps)

            def round_unit(u, i=None, per=0):
                if u + (0 if i is None else per) >= UNITS + per * (i is not None):
                    return
                s = u % RING
                if i is None:
                    landed, free = 16 * (u // RING + 1), u - RING + 1
                else:
                    landed, free = i * (16 * per // RING) + 16 * (u // RING + 1), i * per + (u - RING + 1)
                act.wait_ge(raw_landed[s], landed)
                if u >= RING or i is not None:
                    act.wait_ge(w_used, free)
                nc.scalar.activation(w_hi[:, s, :], raw[:, s, :], ACT.Copy).then_inc(w_rounded, 1)

            def tables(name):
                nc.scalar.preload_act_table_set(name)

            def rstd_of(n, scale, eps, load=True):
                if load:
                    tables(LN_EXP)
                act.wait_ge(stat_ready, n)
                st.seq(nc.scalar.activation(rstd[:], stat[:], ACT.Ln, bias=eps[:], scale=scale))
                nc.scalar.activation(rstd[:], rstd[:], ACT.Exp, scale=-0.5).then_inc(rstd_ready, 1)

            def gate_pairs(phase, func, which):
                u0 = FIRST[phase]
                with act.Fori(0, COUNT[phase] // 4) as i:
                    for j in range(4):
                        if j % 2 == which:
                            act.wait_ge(w_used, i * 4 + (u0 + j + 1))
                            act.wait_ge(bank_free, i * 4 + (u0 + j // 2 * 2 + 2))
                            nc.scalar.activation(act_out[:, j // 2, :], bank[(u0 + j) % RING][:], func
                                                 ).then_inc(gated, 1)
                        round_unit(u0 + j + AHEAD, i, 4)

            def round_units(phase):
                u0 = FIRST[phase]
                n = min(COUNT[phase], UNITS - AHEAD - u0)
                with act.Fori(0, n // RING) as i:
                    for j in range(RING):
                        round_unit(u0 + j + AHEAD, i, RING)
                for u in range(u0 + n // RING * RING, u0 + n):
                    round_unit(u + AHEAD)

            def square_tile(k, m, src, out=None):
                act.wait_ge(x_new, 8 * k + m + 1)
                if m >= 2:
                    act.wait_ge(squares_added, 7 * k + m - 1)
                nc.scalar.activation(act_out[:, m % 2, :], src[:, m, :], ACT.Square).then_inc(tile_squared, 1)

            def mix_squares_units(k, phase):
                u0 = FIRST[phase]
                tables(LN_EXP)
                for j in range(KT):
                    square_tile(k, j, mix)
                    round_unit(u0 + j + AHEAD)

            def mix_squares_ffn(k, phase, tiles):
                u0 = FIRST[phase]
                for j in range(FT // 2):
                    round_unit(u0 + j + AHEAD)
                tiles(0)
                for j in range(FT // 2, FT - 2):
                    round_unit(u0 + j + AHEAD)
                tables(LN_EXP)
                tiles(4)
                round_unit(u0 + FT - 2 + AHEAD)
                round_unit(u0 + FT - 1 + AHEAD)

            def high_parts(k, name, j0, hi):
                for m in range(KT):
                    act.wait_ge(x_new, 8 * k + m + 1)
                    nc.scalar.activation(hi[:, m, :], X[:, m, :], ACT.Copy, scale=pcol(name, j0 + m)
                                         ).then_inc(hi_ready, 1)
                    square_tile(k, m, X)

            def round_first(phase):
                for j in range(RING):
                    round_unit(FIRST[phase] + j + AHEAD)

            def gate_pairs_scaled(phase, n):
                u0 = FIRST[phase]
                pair0 = 0 if phase == "ffn_in_a" else FT

                def silu(i, j):
                    act.wait_ge(a_scaled, i * 2 + (pair0 + j + 1))
                    nc.scalar.activation(act_out[:, j, :], act_out[:, j, :], ACT.Silu).then_inc(gated, 1)

                round_first(phase)
                rstd_of(n, 1.0 / D, eps6, load=False)
                silu(0, 0)
                silu(0, 1)
                with act.Fori(0, COUNT[phase] // 4 - 1) as i:
                    for j in range(4):
                        if j % 2 == 0:
                            silu(i + 1, j // 2)
                        round_unit(u0 + RING + j + AHEAD, i, 4)

            act.wait_ge(params_landed, 16)
            nc.scalar.activation(silu_c[:], par[:, PCOL["c"]:PCOL["c"] + 8], ACT.Silu).then_inc(silu_c_ready, 1)
            act.wait_ge(inputs_landed, 16)
            for m in range(KT):
                if m >= 2:
                    act.wait_ge(stat_part, m - 1)
                nc.scalar.activation(act_out[:, m % 2, :], X[:, m, :], ACT.Square).then_inc(first_squares, 1)
            for n in range(AHEAD):
                round_unit(n)

            def load_ada(k):
                ada_chunk_used(act, k - ADA_BUFS)
                act.dma_start(ada_w[:, k % ADA_BUFS, :, :], ada[k]).then_inc(ada_landed[k % ADA_BUFS], 16)

            act.wait_ge(consts_ready, 1)
            rstd_of(1, 1.0 / D, eps6)
            gate_pairs("conf_in", ACT.Sigmoid, 1)
            u0 = FIRST["short_in"]
            with act.Fori(0, 2) as i:
                for j in range(12):
                    if j % 3 == 0:
                        act.wait_ge(w_used, i * 12 + (u0 + j + 1))
                        act.wait_ge(bank_free, i * 12 + (u0 + j + 2))
                        nc.scalar.activation(act_out[:, (j // 3) % 2, :], bank[(u0 + j) % RING][:], ACT.Copy
                                             ).then_inc(gated, 1)
                    round_unit(u0 + j + AHEAD, i, 12)
                    for n in taps_beside(j):
                        m = i + 6
                        weight = conv_weight("conv_conf_w", CONF_K, m, n)
                        if n == 0:
                            act.wait_ge(bank_free, u0 + RING)
                            nc.scalar.activation(tile(UC, m), tile(U, m)[:, 0:T], ACT.Identity, scale=weight,
                                                 bias=par[:, bass.ds(m + PCOL["conv_conf_b"], 1)]
                                                 ).then_inc(tap_scaled, 1)
                        else:
                            act.wait_ge(tap_added, i * (POOL_TAPS - 1) + n)
                            nc.scalar.activation(ada_acc[:, (n - 1) % 2, :], tile(U, m)[:, n:n + T], ACT.Copy,
                                                 scale=weight).then_inc(tap_scaled, 1)
            u0 = FIRST["mix_a"]
            for j in range(16):
                load_ada(ADA_FIRST + j)
                if j % 2 == 1:
                    act.wait_ge(w_used, u0 + j + 1)
                    act.wait_ge(bank_free, u0 + j // 2 * 2 + 2)
                    nc.scalar.activation(act_out[:, (j // 2) % 2, :], bank[(u0 + j) % RING][:], ACT.Sigmoid
                                         ).then_inc(gated, 1)
                round_unit(u0 + j + AHEAD)
                if j == 13:
                    rstd_of(3, 1.0 / D, eps5)
            u0 = FIRST["gate_b"]
            act.wait_ge(ada_sum_ready, len(ADA_ON_DVE))
            for j in range(8):
                act.wait_ge(w_used, u0 + j + 1)
                act.wait_ge(bank_free, u0 + j + RING)
                nc.scalar.activation(gate[:, j, :], bank[(u0 + j) % RING][:], ACT.Sigmoid).then_inc(bank_free, 1)
                round_unit(u0 + j + AHEAD)
                act.wait_ge(ln_scaled, j + 1)
                nc.scalar.activation(UC[:, j, :], UC[:, j, :], ACT.Silu, scale=pcol("conf_ln_g", j),
                                     bias=pcol("conf_ln_b", j)).then_inc(ln_silu, 1)
            round_units("conf_out")
            round_units("w_o")
            rstd_of(4, 1.0 / D, eps6)
            gate_pairs("ffn_in", ACT.Silu, 0)

            def last_tiles(m0):
                for m in range(m0, m0 + 4):
                    act.wait_ge(x_new, m + 1)
                    nc.scalar.activation(x_hi[:, m, :], X[:, m, :], ACT.Copy, scale=joint_gain[:, m:m + 1]
                                         ).then_inc(hi_ready, 1)
                    if m >= 1:
                        act.wait_ge(squares_added, m)
                    nc.scalar.activation(act_out[:, 0, :], X[:, m, :], ACT.Square)
                    nc.scalar.activation(act_out[:, 1, :], X[:, m, :], ACT.Square, scale=pcol("final_norm_g", m)
                                         ).then_inc(tile_squared, 1)

            mix_squares_ffn(0, "ffn_out", last_tiles)
            round_first("gdn_qkv")
            act.wait_ge(stat_ready, 5)
            st.seq(nc.scalar.activation(act_out[:, 0, :], stat[:], ACT.Ln, bias=eps6[:], scale=1.0 / D))
            nc.scalar.activation(act_out[:, 0, :], act_out[:, 0, :], ACT.Exp, scale=-0.5).then_inc(rstd_ready, 1)
            act.dma_start(tri[:], consts[:, 0:2, :]).then_inc(masks_landed, 16)
            act.dma_start(row[:], rows.partition_broadcast(P).rearrange("p a b -> p (a b)")).then_inc(inputs_landed, 16)
            act.wait_ge(rstd_joined, 1)
            st.seq(nc.scalar.activation(tmp[:], tmp[:], ACT.Ln, bias=eps6[:], scale=1.0 / D))
            nc.scalar.activation(tmp[:], tmp[:], ACT.Exp, scale=-0.5).then_inc(rstd_ready, 1)
            u0 = FIRST["gdn_qkv"]

            def silu_qkv(m):
                act.wait_ge(silu_in, m + 1)
                t = tile(qkv, m)
                nc.scalar.activation(t, t, ACT.Silu).then_inc(silu_out, 1)

            for j in range(4):
                silu_qkv(j)
            with act.Fori(0, 5) as i:
                for j in range(4):
                    round_unit(u0 + RING + j + AHEAD, i, 4)
                    silu_qkv(i * 4 + (j + 4))

            def head_rstd_of(r, scale):
                act.wait_ge(sq_summed, r + 1)
                if r >= 2:
                    act.wait_ge(head_rstd_used, r - 1)
                b = act_out[:, r % 2, :]
                st.seq(nc.scalar.activation(b, bank[4 + r % 2][:], ACT.Ln, bias=eps6[:], scale=scale))
                nc.scalar.activation(b, b, ACT.Exp, scale=-0.5).then_inc(head_rstd, 1)

            tables(LN_EXP)
            round_unit(FIRST["gdn_ba"] + AHEAD)
            u0 = FIRST["gdn_z"]
            for j in range(8):
                round_unit(u0 + j + AHEAD)
                if j == 0:
                    act.wait_ge(tok_dve, 1)
                    nc.scalar.activation(tok[:, 0, :], tok[:, 0, :], ACT.Exp, scale=-1.0)
                    st.seq(nc.scalar.activation(tok[:, 2, :], tok[:, 2, :], ACT.Exp, scale=-1.0))
                    nc.scalar.activation(tok[:, 2, :], tok[:, 2, :], ACT.Ln, bias=ones[:, 0:1])
                    nc.scalar.activation(tok[:, 3, 0:8], row[:, 0:8], ACT.Exp).then_inc(tok_act, 1)
                if j == 3:
                    act.wait_ge(tok_pe, 2)
                    nc.scalar.activation(tok[:, 5, :], bank[6][:, 64:96], ACT.Exp)
                    nc.scalar.activation(tok[:, 6, :], bank[6][:, 96:128], ACT.Exp).then_inc(tok_act, 1)
                if j == 5:
                    act.wait_ge(tok_dve, 3)
                    nc.scalar.activation(tok[:, 7, :], tok[:, 7, :], ACT.Exp).then_inc(tok_act, 1)
                head_rstd_of(2 * j, 1.0)
                head_rstd_of(2 * j + 1, 1.0)
            act.wait_ge(w_used, FIRST["gdn_out"])
            act.dma_start(masks_raw[:], consts[:, 2:, :]).then_inc(masks_landed, 16)
            act.wait_ge(bank_free, FIRST["gdn_out"] + RING)
            nc.scalar.activation(z_gate[:], z_gate[:], ACT.Silu).then_inc(z_ready, 1)

            def chunk_copies(p, c, part):
                for n in range(2):
                    k = p * 8 + c * 2 + n
                    if part == 0:
                        act.wait_ge(new_v, k + 1)
                        nc.scalar.activation(new_v_sb[n], bank[n][:, P:2 * P], ACT.Copy).then_inc(new_v_copied, 1)
                    else:
                        act.wait_ge(chunk_done, k + 1)
                        nc.scalar.activation(qkv[:, 16 + 2 * p + n, c * CH:(c + 1) * CH], bank[n][:, 2 * P:3 * P],
                                             ACT.Copy).then_inc(o_copied, 1)

            def head_decays(h):
                act.wait_ge(head_products, 4 * h + 1)
                if h:
                    act.wait_ge(head_taken, h)
                nc.scalar.activation(rstd[:], bank[0][:], ACT.Exp).then_inc(decay_row, 1)
                act.wait_ge(diff_ready, h + 1)
                nc.scalar.activation(act_out[:, h % 2, :], square[:], ACT.Exp).then_inc(decay_ready, 1)

            tables(LN_EXP)
            head_decays(0)
            head_decays(1)
            for p in range(HEADS // 2 + 1):
                for lv in range(LEVELS):
                    if p < HEADS // 2 and lv >= 1:
                        for n in range(2):
                            act.wait_ge(first_half, p * 14 + lv * 2 + n + 1)
                            if lv >= 2 or p >= 1:
                                act.wait_ge(second_half, p * 12 + (lv - 1) * 2 + n - 1)
                            nc.scalar.activation(half[n][:], bank[4 + 2 * n][:], ACT.Copy).then_inc(first_copied, 1)
                    if p + 1 < HEADS // 2 and lv == LEVELS - 3:
                        head_decays(2 * p + 2)
                    if p + 1 < HEADS // 2 and lv == LEVELS - 2:
                        head_decays(2 * p + 3)
                    if p >= 1 and lv < NCH:
                        chunk_copies(p - 1, lv, 0)
                        chunk_copies(p - 1, lv, 1)
                    if p == HEADS // 2 and lv < HEADS // 2 - 1:
                        head_rstd_of(16 + 2 * lv, 1.0 / DH)
                        head_rstd_of(17 + 2 * lv, 1.0 / DH)
            for h in (HEADS - 2, HEADS - 1):
                head_rstd_of(16 + h, 1.0 / DH)
            mix_squares_units(1, "gdn_out")
            rstd_of(7, 1.0 / D, eps6, load=False)
            high_parts(2, "pre_ffn_norm_2", 0, x_hi)
            gate_pairs_scaled("ffn_in_a", 8)
            mix_squares_ffn(3, "ffn_out_a", lambda m0: [square_tile(3, m, mix) for m in range(m0, m0 + 4)])
            rstd_of(9, 1.0 / D, eps6, load=False)
            high_parts(4, "kv_norm_2", 0, x_hi)
            round_first("fox_k")
            rstd_of(10, 1.0 / D, eps6, load=False)
            for m in range(KT):
                nc.scalar.activation(q_hi[:, m, :], X[:, m, :], ACT.Copy, scale=pcol("pre_mix_norm_2", 8 + m)
                                     ).then_inc(hi_ready, 1)
            for j in range(RING, 8):
                round_unit(FIRST["fox_k"] + j + AHEAD)
            round_unit(FIRST["fox_f"] + AHEAD)
            for j in range(2):
                round_unit(FIRST["fox_v"] + j + AHEAD)
            act.wait_ge(tok_dve, 4)
            f = square[0:16, :]
            st.seq(nc.scalar.activation(f, f, ACT.Exp, scale=-1.0))
            nc.scalar.activation(f, f, ACT.Ln, bias=ones[0:16, 0:1]).then_inc(tok_act, 1)
            for j in range(2, 8):
                round_unit(FIRST["fox_v"] + j + AHEAD)
            act.wait_ge(w_used, FIRST["fox_q"])
            act.wait_ge(tok_pe, 3)
            act.dma_start(masks_raw[:], consts[:, 2:, :]).then_inc(masks_landed, 16)
            round_units("fox_q")

            def copy_prob(s):
                b = s % QB
                act.wait_ge(prob_turned, s + 1)
                if s >= 2:
                    act.wait_ge(pv_done, s - 1)
                nc.scalar.activation(prob_t[s % 2][:, 0:b + 1, :], bank[3 + s % 2][:, 0:(b + 1) * P], ACT.Copy
                                     ).then_inc(prob_copied, 1)

            STEPS = FOX_HEADS * QB
            for s in range(STEPS + 2):
                h, b = s // QB, s % QB
                if s < STEPS:
                    act.wait_ge(scores_taken, s + 1)
                    if s >= 2:
                        act.wait_ge(prob_turned, s - 1)
                    q = softmax[:, s % 2, :]
                    nc.scalar.activation(prob[s % 2][:, 0:(b + 1) * P], score[s % 2][:, 0:(b + 1) * P], ACT.Exp,
                                         scale=-1.0, bias=q[:, 0:1], accum_out=q[:, 1:2]).then_inc(exp_done, 1)
                if s >= 2:
                    copy_prob(s - 2)
            mix_squares_units(5, "fox_o")
            rstd_of(11, 1.0 / D, eps6, load=False)
            high_parts(6, "pre_ffn_norm_2", 8, x_hi)
            gate_pairs_scaled("ffn_in_b", 12)
            mix_squares_ffn(7, "ffn_out_b", lambda m0: [square_tile(7, m, mix) for m in range(m0, m0 + 4)])
            rstd_of(13, 1.0 / D, eps6, load=False)

        @block.tensor
        def _(pe):
            def product(acc, s, t, hi, lo, k, start, stop):
                w = bass.ts(t, P)
                nc.tensor.matmul(acc, w_hi[:, s, w], hi[:, k, :], start=start, stop=False)
                nc.tensor.matmul(acc, w_hi[:, s, w], lo[:, k, :], start=False, stop=False)
                return nc.tensor.matmul(acc, w_lo[:, s, w], hi[:, k, :], start=False, stop=stop)

            def unit(u, hi, lo, ready, i=None, per=0):
                s = u % RING
                moved = 0 if i is None else i * per
                pe.wait_ge(w_split, moved + (u + 1))
                pe.wait_ge(bank_free, moved + (u + 1))
                for k in range(KT):
                    if ready is not None:
                        pe.wait_ge(x_ready, ready + k + 1)
                    last = product(bank[s][:], s, k, hi, lo, k, k == 0, k == KT - 1)
                last.then_inc(w_used, 1)

            def units(phase, hi, lo, ready, sums=()):
                u0, done = FIRST[phase], 0
                if ready is not None:
                    done = RING
                    for k in range(KT):
                        pe.wait_ge(x_ready, ready + k + 1)
                        for j in range(RING):
                            u = u0 + j
                            if k == 0:
                                pe.wait_ge(w_split, u + 1)
                                pe.wait_ge(bank_free, u + 1)
                            last = product(bank[u % RING][:], u % RING, k, hi, lo, k, k == 0, k == KT - 1)
                            if k == KT - 1:
                                last.then_inc(w_used, 1)
                    for n in sums:
                        sum_over_partitions(n)
                with pe.Fori(0, COUNT[phase] // RING - done // RING) as i:
                    for j in range(RING):
                        unit(u0 + done + j, hi, lo, None, i, RING)

            def ffn_out(phase, ready):
                u0 = FIRST[phase]
                for half in range(2):
                    for k2 in range(FT // 2 - 2 * half):
                        u = u0 + half * (FT // 2) + k2
                        s = u % RING
                        pe.wait_ge(w_split, u + 1)
                        if k2 == 0:
                            pe.wait_ge(bank_free, u0 + RING)
                        if half == 0:
                            pe.wait_ge(x_ready, ready + 2 * k2 + 2)
                        for m in range(4):
                            for kk in range(2):
                                k = 2 * k2 + kk
                                last = product(bank[4 * half + m][:], s, kk * 4 + m, f_hi, f_lo, k,
                                               k == 0, k == FT - 1)
                        last.then_inc(w_used, 1)
                for u in (u0 + FT - 2, u0 + FT - 1):
                    pe.wait_ge(w_split, u + 1)
                for m in range(4):
                    for u in (u0 + FT - 2, u0 + FT - 1):
                        for kk in range(2):
                            k = 2 * (u - u0 - FT // 2) + kk
                            last = product(bank[4 + m][:], u % RING, kk * 4 + m, f_hi, f_lo, k, False, k == FT - 1)
                        if m == 3:
                            last.then_inc(w_used, 1)
                    if m < 3:
                        last.then_inc(tail_done, 1)

            def sum_over_partitions(n):
                pe.wait_ge(sum_ready, n)
                b, t = (bank[6], square) if n == 5 else (stat, total)
                nc.tensor.matmul(b[:], ones[:], t[:], start=True, stop=True).then_inc(stat_ready, 1)

            def ada_columns(k):
                if k in ADA_ON_PE:
                    pe.wait_ge(ada_landed[k % ADA_BUFS], 16 * (k // ADA_BUFS + 1))
                else:
                    pe.wait_ge(ada_sum_ready, ADA_ON_DVE.index(k) + 1)
                for b in range(ADA_COLS // P):
                    col = ada_ps[:, 2 * k + b:2 * k + b + 1]
                    if k in ADA_ON_PE:
                        for j in range(KT):
                            last = nc.tensor.matmul(col, ada_w[:, k % ADA_BUFS, j, bass.ts(b, P)], silu_c[:, j:j + 1],
                                                    start=j == 0, stop=j == KT - 1)
                    else:
                        last = nc.tensor.matmul(col, ada_acc[:, ADA_ON_DVE.index(k) % 2, bass.ts(b, P)], ones[:, 0:1],
                                                start=True, stop=True)
                last.then_inc(ada_ps_ready, 1)

            pe.wait_ge(consts_ready, 1)
            pe.wait_ge(silu_c_ready, 1)
            ada_columns(0)
            for m in range(KT):
                pe.wait_ge(first_squares, m + 1)
                last = nc.tensor.matmul(stat[:], ones[:], act_out[:, m % 2, :], start=m == 0, stop=m == KT - 1)
                last.then_inc(stat_part if m < KT - 1 else stat_ready, 1)
            for k in range(1, ADA_FIRST):
                ada_columns(k)
            units("conf_in", x_hi, x_lo, 0)
            units("short_in", x_hi, x_lo, None)
            u0 = FIRST["mix_a"]
            for j in range(16):
                if j % 2 == 0:
                    unit(u0 + j, y_hi, y_lo, 8 if j == 0 else None)
                else:
                    unit(u0 + j, x_hi, x_lo, None)
                if j == 3:
                    sum_over_partitions(1)
                if j == 11:
                    sum_over_partitions(2)
                if j >= 2:
                    ada_columns(ADA_FIRST + j - 2)
            units("gate_b", x_hi, x_lo, None)
            ada_columns(ADA_CHUNKS - 2)
            ada_columns(ADA_CHUNKS - 1)
            units("conf_out", y_hi, y_lo, 16)
            units("w_o", x_hi, x_lo, 24)
            sum_over_partitions(3)
            units("ffn_in", x_hi, x_lo, 32)
            ffn_out("ffn_out", XR["ffn_h"])
            units("gdn_qkv", x_hi, x_lo, XR["gdn_x"], (4, 5))
            unit(FIRST["gdn_ba"], x_hi, x_lo, None)
            u0 = FIRST["gdn_z"]

            def sum_head(r):
                pe.wait_ge(sq_ready, r + 1)
                if r >= 2:
                    pe.wait_ge(head_rstd, r - 1)
                nc.tensor.matmul(bank[4 + r % 2][:], ones[:], (square, total)[r % 2][:], start=True, stop=True
                                 ).then_inc(sq_summed, 1)

            beta, decay, upper, ident = tok[:, 0, :], tok[:, 4, :], tri[:, 0, :], tri[:, 1, :]
            for j in range(8):
                if j == 3:
                    pe.wait_ge(tok_dve, 2)
                    nc.tensor.matmul(bank[6][:, 64:96], upper, decay, start=True, stop=True)
                    nc.tensor.matmul(bank[6][:, 96:128], ones[:], decay, start=True, stop=True
                                     ).then_inc(tok_pe, 1)
                unit(u0 + j, x_hi, x_lo, None)
                if j == 0:
                    pe.wait_ge(bank_free, u0 + RING)
                    pe.wait_ge(masks_landed, 16)
                    for c in range(NCH):
                        last = nc.tensor.matmul(bank[6][:, c * 16:(c + 1) * 16], tmp[0:16, bass.ts(c, P)],
                                                ident[0:16, 0:16], start=True, stop=True)
                    last.then_inc(tok_pe, 1)
                sum_head(2 * j)
                sum_head(2 * j + 1)

            def chunk_part(p, c, part):
                for n in range(2):
                    h, k = 2 * p + n, p * 8 + c * 2 + n
                    slot, cols, b = (p % 2) * 2 + n, slice(c * CH, (c + 1) * CH), bank[n]
                    if part == 0:
                        pe.wait_ge(state_ready, p * 10 + c * 2 + n + 1)
                        nc.tensor.matmul(b[:, 0:P], qkv[:, 8 + h, cols], state[:, n, :], start=True, stop=True
                                         ).then_inc(ks_ready, 1)
                    elif part == 1:
                        pe.wait_ge(rest_ready, k + 1)
                        nc.tensor.matmul(b[:, P:2 * P], inv_t[slot][:, c, :], rest_sb[n], start=True, stop=True
                                         ).then_inc(new_v, 1)
                    else:
                        pe.wait_ge(new_v_copied, k + 1)
                        if k >= 2:
                            pe.wait_ge(o_copied, k - 1)
                        nc.tensor.matmul(b[:, 2 * P:3 * P], state[:, n, :], qkv[:, h, cols], start=True, stop=False)
                        nc.tensor.matmul(b[:, 2 * P:3 * P], new_v_sb[n], attn[slot][:, c, :], start=False, stop=True)
                        nc.tensor.matmul(b[:, 3 * P:4 * P], key_dec[slot][:, c, :], new_v_sb[n], start=True,
                                         stop=True).then_inc(chunk_done, 1)

            def products_of(h):
                p = h // 2
                if h == 0:
                    pe.wait_ge(bank_free, FIRST["gdn_out"] + RING)
                    pe.wait_ge(tok_dve, 3)
                    pe.wait_ge(head_rstd_used, 16)
                else:
                    pe.wait_ge(head_taken, h)
                if h >= 2 and h % 2 == 0:
                    pe.wait_ge(turned_used, 2 * h)
                    if p >= 2:
                        pe.wait_ge(o_copied, 8 * (p - 1))
                        pe.wait_ge(state_ready, 10 * (p - 1))
                for c in range(NCH):
                    g = decay[:, c * HEADS + h:c * HEADS + h + 1].broadcast_to([P, P])
                    last = nc.tensor.matmul(bank[0][:, bass.ts(c, P)], g, upper, start=True, stop=True)
                last.then_inc(head_products, 1)
                for c in range(NCH):
                    g = beta[:, c * HEADS + h:c * HEADS + h + 1].broadcast_to([P, P])
                    last = nc.tensor.matmul(bank[1][:, bass.ts(c, P)], g, ident, start=True, stop=True)
                last.then_inc(head_products, 1)
                for c in range(NCH):
                    kc = qkv[:, 8 + h, bass.ts(c, P)]
                    last = nc.tensor.matmul(bank[2][:, bass.ts(c, P)], kc, kc, start=True, stop=True)
                last.then_inc(head_products, 1)
                for c in range(NCH):
                    last = nc.tensor.matmul(bank[3][:, bass.ts(c, P)], qkv[:, 8 + h, bass.ts(c, P)],
                                            qkv[:, h, bass.ts(c, P)], start=True, stop=True)
                last.then_inc(head_products, 1)

            products_of(0)
            products_of(1)
            for p in range(HEADS // 2 + 1):
                for lv in range(LEVELS):
                    if p < HEADS // 2:
                        for n in range(2):
                            pe.wait_ge(level_ready, p * 14 + lv * 2 + n + 1)
                            if lv == 0:
                                pe.wait_ge(head_taken, 2 * p + 2)
                            else:
                                pe.wait_ge(inverse_ready, p * 14 + (lv - 1) * 2 + n + 1)
                            for c in range(NCH):
                                r = ident if lv == 0 else inv[n][:, c, :]
                                last = nc.tensor.matmul(bank[4 + 2 * n][:, bass.ts(c, P)],
                                                        level_a[n][(p + lv) % 2][:, c, :], r, start=True, stop=True)
                            last.then_inc(first_half, 1)
                        if p + 1 < HEADS // 2 and lv == LEVELS - 3:
                            products_of(2 * p + 2)
                    if p >= 1 and lv < NCH:
                        chunk_part(p - 1, lv, 0)
                    if p == HEADS // 2 and lv < HEADS // 2 - 1:
                        sum_head(16 + 2 * lv)
                    if p < HEADS // 2 and lv in (0, 1):
                        h = 2 * p + lv
                        for w in range(2):
                            if h >= 1:
                                pe.wait_ge(turned_used, 2 * h - 1 + w)
                            for c in range(NCH):
                                last = nc.tensor.transpose(bank[2 + w][:, bass.ts(c, P)],
                                                           qkv[:, 16 - 8 * w + h, bass.ts(c, P)], ident)
                            last.then_inc(turned, 1)
                    if p >= 1 and lv < NCH:
                        chunk_part(p - 1, lv, 1)
                    if p == HEADS // 2 and lv < HEADS // 2 - 1:
                        sum_head(17 + 2 * lv)
                    if p < HEADS // 2 and lv >= 1:
                        slot = (p % 2) * 2
                        for n in range(2):
                            pe.wait_ge(first_copied, p * 12 + (lv - 1) * 2 + n + 1)
                            if lv < LEVELS - 1:
                                for c in range(NCH):
                                    nc.tensor.matmul(bank[4 + 2 * n][:, bass.ts(c, P // 2)], inv_t[slot + n][:, c, :],
                                                     blocks(half[n][:, c:c + 1, :], lv, 0), start=True, stop=True)
                            for c in range(NCH):
                                last = nc.tensor.matmul(bank[5 + 2 * n][:, bass.ts(c, P // 2)], half[n][:, c, :],
                                                        blocks(inv_t[slot + n][:, c:c + 1, :], lv, 1),
                                                        start=True, stop=True)
                            last.then_inc(second_half, 1)
                    if p + 1 < HEADS // 2 and lv == LEVELS - 2:
                        products_of(2 * p + 3)
                    if p >= 1 and lv < NCH:
                        chunk_part(p - 1, lv, 2)
            for r in (22, 23):
                sum_head(r)
            units("gdn_out", og_hi, og_lo, XR["gdn_o"])
            sum_over_partitions(6)
            units("ffn_in_a", x_hi, x_lo, XR["ffn_x_a"], (7,))
            ffn_out("ffn_out_a", XR["ffn_h_a"])
            sum_over_partitions(8)
            units("fox_k", x_hi, x_lo, XR["kv_x"], (9,))
            pe.wait_ge(rstd_ready, 9)
            unit(FIRST["fox_f"], x_hi, x_lo, None)
            for c in range(NCH):
                last = nc.tensor.matmul(bank[6][:, c:c + 1], rstd[0:1, bass.ts(c, P)], ones[0:1, 0:1],
                                        start=True, stop=True)
            last.then_inc(tok_pe, 1)
            u0 = FIRST["fox_v"]
            for hv in range(2):
                for k2 in range(KT // 2):
                    u = u0 + hv * (KT // 2) + k2
                    s = u % RING
                    pe.wait_ge(w_split, u + 1)
                    if k2 == 0:
                        pe.wait_ge(bank_free, u0 + RING)
                    for t in range(QB):
                        b = bank[4 * hv + t] if 4 * hv + t != 6 else bank[6]
                        if hv == 1 and k2 == 0 and t == 2:
                            pe.wait_ge(tok_dve, 4)
                        for kk in range(2):
                            k = 2 * k2 + kk
                            for i, (x, w) in enumerate(((x_hi, w_hi), (x_hi, w_lo), (x_lo, w_hi))):
                                last = nc.tensor.matmul(b[:], x[:, k, bass.ts(t, P)], w[:, s, bass.ts(kk, T)],
                                                        start=k == 0 and i == 0, stop=k == KT - 1 and i == 2)
                    last.then_inc(w_used, 1)
            pe.wait_ge(x_ready, XR["q_x"] + 8)
            units("fox_q", q_hi, q_lo, None)
            pe.wait_ge(v_free, 8)
            pe.wait_ge(masks_ready, 2)
            pe.wait_ge(bank_free, FIRST["fox_o"] + RING)
            STEPS = FOX_HEADS * QB

            def forget_on_partitions(h):
                pe.wait_ge(tok_dve, 6) if h == 0 else pe.wait_ge(forget_copied, h)
                pick = tri[0:16, 1, h:h + 1].broadcast_to([16, P])
                nc.tensor.matmul(bank[7][:], pick, forget_sum[:], start=True, stop=True).then_inc(forget_row, 1)

            forget_on_partitions(0)
            for s in range(STEPS + 3):
                if s < STEPS:
                    h, b = s // QB, s % QB
                    rows_ = slice(h % 2 * FOX_D, (h % 2 + 1) * FOX_D)
                    if s >= 3:
                        pe.wait_ge(scores_taken, s - 2)
                    acc = bank[s % 3]
                    nc.tensor.matmul(acc[:, 0:(b + 1) * P], qf[rows_, h // 2, bass.ts(b, P)],
                                     kf[rows_, h // 2, 0:(b + 1) * P], start=True, stop=False)
                    nc.tensor.matmul(acc[:, bass.ts(b, P)], masks[:, 8, :], masks[:, 9, :], start=False, stop=True
                                     ).then_inc(scores_done, 1)
                    if b == 1 and h + 1 < FOX_HEADS:
                        forget_on_partitions(h + 1)
                if 2 <= s < STEPS + 2:
                    s2 = s - 2
                    pe.wait_ge(prob_ready, s2 + 1)
                    if s2 >= 2:
                        pe.wait_ge(prob_copied, s2 - 1)
                    for kb in range(s2 % QB + 1):
                        last = nc.tensor.transpose(bank[3 + s2 % 2][:, bass.ts(kb, P)],
                                                   prob[s2 % 2][:, bass.ts(kb, P)], ident)
                    last.then_inc(prob_turned, 1)
                if s >= 3:
                    s3 = s - 3
                    h, b = s3 // QB, s3 % QB
                    rows_ = slice(h % 2 * FOX_D, (h % 2 + 1) * FOX_D)
                    pe.wait_ge(prob_copied, s3 + 1)
                    if b == 0 and h % 2 == 0 and h >= 4:
                        pe.wait_ge(x_ready, XR["fox_o"] + h // 2 - 1)
                    for kb in range(b + 1):
                        last = nc.tensor.matmul(bank[5 + h // 2 % 2][rows_, bass.ts(b, P)],
                                                vt[:, kb, h * FOX_D:(h + 1) * FOX_D], prob_t[s3 % 2][:, kb, :],
                                                start=kb == 0, stop=kb == b)
                    last.then_inc(pv_done, 1)
            units("fox_o", q_hi, q_lo, XR["fox_o"])
            sum_over_partitions(10)
            units("ffn_in_b", x_hi, x_lo, XR["ffn_x_b"], (11,))
            ffn_out("ffn_out_b", XR["ffn_h_b"])
            sum_over_partitions(12)

        @block.vector
        def _(dve):
            st = Steps(dve, dve_steps)
            V = nc.vector

            def split(src, hi, lo):
                st.seq(V.tensor_copy(hi, src))
                V.tensor_tensor(lo, src, hi.bitcast(F32), ALU.subtract).then_inc(x_ready, 1)

            def conv_taps(src, dst, odd, name, m, taps, bias=None, first=0, counted=True):
                marks = [None, None]
                for k in range(first, taps):
                    n = (k - first) % 2
                    acc, x, w = (dst, odd)[n], src[:, k:k + T], conv_weight(name, taps, m, k)
                    st.after(marks[n])
                    if k == first and bias is not None:
                        ins = V.tensor_scalar(acc, x, w, par[:, bass.ds(m + PCOL[bias], 1)], ALU.mult, ALU.add)
                    elif k < first + 2:
                        ins = V.tensor_scalar(acc, x, w, None, ALU.mult)
                    else:
                        ins = V.scalar_tensor_tensor(acc, x, w, acc, ALU.mult, ALU.add)
                    marks[n] = st.step(ins)
                    yield
                st.after(marks[0])
                st.after(marks[1])
                ins = V.tensor_tensor(dst, dst, odd, ALU.add)
                if counted:
                    st.seq(ins)
                yield ins

            given = []

            def give_back(n):
                V.memset(spare[:, len(given):len(given) + 1], 0.0).then_inc(bank_free, n)
                given.append(n)

            V.memset(eps6[:], 1e-6)
            V.memset(eps5[:], 1e-5).then_inc(bank_free, RING)
            V.memset(U[:, :, 0:CONF_K - 1], 0.0)
            V.memset(prod_pad[:, 0:3], 0.0)
            V.memset(ones[:], 1.0).then_inc(consts_ready, 1)
            dve.wait_ge(consts_ready, 1)

            def ada_chunk(k):
                b, n_th = k % ADA_BUFS, ADA_ON_DVE.index(k)
                chain = (tmp[:, 0:ADA_COLS], tmp[:, ADA_COLS:T],
                         prod_pad[:, 3:3 + ADA_COLS], prod_pad[:, 3 + ADA_COLS:3 + T])
                dve.wait_ge(ada_landed[b], 16 * (k // ADA_BUFS + 1))
                if n_th:
                    dve.wait_ge(ada_sum_ready, n_th)
                marks = [None] * 4
                for j in range(KT):
                    n = j % 4
                    st.after(marks[n])
                    marks[n] = st.step(
                        V.tensor_scalar(chain[n], ada_w[:, b, j, :], silu_c[:, j:j + 1], None, ALU.mult) if j < 4 else
                        V.scalar_tensor_tensor(chain[n], ada_w[:, b, j, :], silu_c[:, j:j + 1], chain[n],
                                               ALU.mult, ALU.add))
                    yield
                for mark in marks:
                    st.after(mark)
                if n_th >= 2:
                    dve.wait_ge(ada_ps_ready, ADA_ON_DVE[n_th - 2] + 1)
                acc = ada_acc[:, n_th % 2, :]
                mark = st.step(V.tensor_tensor(acc, tmp[:], prod_pad[:, 3:], ALU.add))
                yield
                st.after(mark)
                V.tensor_tensor(acc[:, 0:ADA_COLS], acc[:, 0:ADA_COLS], acc[:, ADA_COLS:], ALU.add
                                ).then_inc(ada_sum_ready, 1)
                yield

            dve.wait_ge(inputs_landed, 16)
            dve.wait_ge(params_landed, 16)
            dve.wait_ge(silu_c_ready, 1)
            for k in ADA_ON_DVE:
                if k < ADA_FIRST:
                    for _ in ada_chunk(k):
                        pass
            b_ada = par[:, PCOL["b_ada"]:PCOL["b_ada"] + 48]
            dve.wait_ge(ada_ps_ready, ADA_FIRST)
            st.seq(V.tensor_tensor(mod[:, 0:16], ada_ps[:, 0:16], b_ada[:, 0:16], ALU.add))
            g = par[:, PCOL["norm_mix_g"]:PCOL["norm_mix_g"] + 8]
            st.seq(V.scalar_tensor_tensor(gain[:, 0, :], mod[:, 8:16], 1.0, g, ALU.add, ALU.mult))

            def modulated_input(n, which, shift):
                dve.wait_ge(rstd_ready, n)
                buf, marks, highs = (tmp, square), {}, {}
                for t in range(KT + 2):
                    if t < KT:
                        if t >= 2:
                            dve.wait_ge(x_ready, XSET[which] + t - 1)
                        b = buf[t % 2]
                        marks[t] = st.step(V.scalar_tensor_tensor(b[:], X[:, t, :], gain[:, which, t:t + 1], rstd[:],
                                                                  ALU.mult, ALU.mult))
                    if 1 <= t <= KT:
                        m = t - 1
                        st.after(highs[m])
                        V.tensor_tensor(x_lo[:, m, :], buf[m % 2][:], x_hi[:, m, :].bitcast(F32), ALU.subtract
                                        ).then_inc(x_ready, 1)
                    if t < KT:
                        st.after(marks[t])
                        marks[t] = st.step(V.tensor_scalar(buf[t % 2][:], buf[t % 2][:],
                                                           mod[:, shift + t:shift + t + 1], None, ALU.add))
                        st.after(marks[t])
                        highs[t] = st.step(V.tensor_copy(x_hi[:, t, :], buf[t % 2][:]))

            XSET = [0, 32]
            modulated_input(1, 0, 0)

            u0 = FIRST["conf_in"]
            with st.loop(4, CONF_K + 1) as i:
                taps = conv_taps(tile(U, i), tile(UC, i), square[:], "conv_conf_w", i, CONF_K, "conv_conf_b")
                for j in range(2):
                    dve.wait_ge(gated, i * 2 + (j + 1))
                    V.tensor_tensor(tile(U, i * 2 + j)[:, CONF_K - 1:], bank[(u0 + 2 * j) % RING][:],
                                    act_out[:, j, :], ALU.mult).then_inc(bank_free, 2)
                    if j == 0:
                        dve.wait_ge(bank_free, i * 4 + (u0 + 2 + RING))
                    for _ in range((CONF_K + 1) // 2):
                        next(taps)
            u0 = FIRST["short_in"]

            def long_convolutions(i):
                yield from conv_taps(tile(U, i + 4), tile(UC, i + 4), square[:], "conv_conf_w", i + 4, CONF_K,
                                     "conv_conf_b")
                yield from conv_taps(tile(U, i + 6), total[:], square[:], "conv_conf_w", i + 6, CONF_K,
                                     first=POOL_TAPS)
                dve.wait_ge(tap_added, i * (POOL_TAPS - 1) + (POOL_TAPS + 1))
                st.seq(V.tensor_tensor(tile(UC, i + 6), tile(UC, i + 6), total[:], ALU.add))
                yield

            with st.loop(2, 4 * (SHORT_K + 2) + 2 * CONF_K - POOL_TAPS + 3) as i:
                for r in range(4):
                    m = i * 4 + r
                    cu = u0 + 3 * r
                    if r == 0:
                        fill = long_convolutions(i)

                    def filled(count):
                        for _ in range(count):
                            next(fill, None)
                    dve.wait_ge(gated, i * 4 + (8 + r + 1))
                    dve.wait_ge(w_used, i * 12 + (cu + 2))
                    V.tensor_tensor(prod_pad[:, 3:], bank[(cu + 1) % RING][:], act_out[:, r % 2, :],
                                    ALU.mult).then_inc(bank_free, 2)
                    filled(1)
                    dve.wait_ge(bank_free, i * 12 + (cu + 2 + RING))
                    for _ in conv_taps(prod_pad[:, 4 - SHORT_K:], tmp[:], rstd[:], "conv_short_w", m, SHORT_K):
                        filled(2)
                    dve.wait_ge(w_used, i * 12 + (cu + 3))
                    V.tensor_tensor(tmp[:], tmp[:], bank[(cu + 2) % RING][:], ALU.mult).then_inc(bank_free, 1)
                    filled(1)
                    dve.wait_ge(bank_free, i * 12 + (cu + 3 + RING))
                    high = st.step(V.tensor_copy(tile(y_hi, m), tmp[:]))
                    filled(1)
                    st.after(high)
                    V.tensor_tensor(tile(y_lo, m), tmp[:], tile(y_hi, m).bitcast(F32), ALU.subtract
                                    ).then_inc(x_ready, 1)
                    filled(2)
                    dve.wait_ge(x_ready, i * 4 + (8 + r + 1))
                    if r == 3:
                        for _ in fill:
                            pass
            def layer_norm():
                both, marks = (total, square), [None, None]
                for m in range(2, KT + 1):
                    n = m % 2
                    st.after(marks[n])
                    if m < KT:
                        a = UC[:, m - 2, :] if m < 4 else both[n][:]
                        marks[n] = st.step(V.tensor_tensor(both[n][:], a, UC[:, m, :], ALU.add))
                    else:
                        st.after(marks[1])
                        V.tensor_tensor(total[:], total[:], square[:], ALU.add).then_inc(sum_ready, 1)
                    yield
                dve.wait_ge(stat_ready, 2)
                mean = st.step(V.tensor_scalar(rstd[:], stat[:], 1.0 / D, None, ALU.mult))
                yield
                st.after(mean)
                marks, squared, added = {}, {}, None
                for t in range(KT + 2):
                    if t < KT:
                        marks[t] = st.step(V.tensor_tensor(UC[:, t, :], UC[:, t, :], rstd[:], ALU.subtract))
                        yield
                    if 1 <= t <= KT:
                        m = t - 1
                        st.after(marks[m])
                        st.after(added)
                        squared[m] = st.step(V.tensor_tensor((total if m == 0 else square)[:], UC[:, m, :],
                                                             UC[:, m, :], ALU.mult))
                        yield
                        if m >= 1:
                            st.after(squared[m])
                            ins = V.tensor_tensor(total[:], total[:], square[:], ALU.add)
                            if m == KT - 1:
                                ins.then_inc(sum_ready, 1)
                            else:
                                added = st.step(ins)
                            yield
                dve.wait_ge(rstd_ready, 2)
                for m in range(KT):
                    V.tensor_tensor(UC[:, m, :], UC[:, m, :], rstd[:], ALU.mult).then_inc(ln_scaled, 1)
                    yield

            u0, norm = FIRST["mix_a"], layer_norm()
            for j in range(8):
                dve.wait_ge(gated, 16 + j + 1)
                V.tensor_tensor(mixed[:, j, :], bank[(u0 + 2 * j) % RING][:], act_out[:, j % 2, :], ALU.mult
                                ).then_inc(bank_free, 2)
                for n in range(2):
                    for t, _ in enumerate(ada_chunk(ADA_FIRST + 2 * j + n)):
                        if t % 2 == 1 and t < KT and (j == 0 and (n, t) != (1, 7) or 2 <= j < 5 or j == 7):
                            next(norm, None)
            for _ in norm:
                pass
            for m in range(KT):
                dve.wait_ge(ln_silu, m + 1)
                split(UC[:, m, :], y_hi[:, m, :], y_lo[:, m, :])
            dve.wait_ge(ada_ps_ready, ADA_CHUNKS)
            st.seq(V.tensor_tensor(mod[:, 16:48], ada_ps[:, 16:48], b_ada[:, 16:48], ALU.add))
            st.seq(V.tensor_tensor(joint_gain[:], par[:, PCOL["final_norm_g"]:PCOL["final_norm_g"] + 8],
                                   par[:, PCOL["pre_mix_norm_2"]:PCOL["pre_mix_norm_2"] + 8], ALU.mult))
            g = par[:, PCOL["norm_ffn_g"]:PCOL["norm_ffn_g"] + 8]
            st.seq(V.scalar_tensor_tensor(gain[:, 1, :], mod[:, 32:40], 1.0, g, ALU.add, ALU.mult))
            dve.wait_ge(bank_free, FIRST["conf_out"] + RING)
            u0 = FIRST["conf_out"]
            for j in range(8):
                dve.wait_ge(w_used, u0 + j + 1)
                V.tensor_tensor(tmp[:], bank[(u0 + j) % RING][:], gate[:, j, :], ALU.mult).then_inc(bank_free, 1)
                dve.wait_ge(bank_free, u0 + j + 1 + RING)
                st.seq(V.tensor_tensor(tmp[:], tmp[:], mixed[:, j, :], ALU.add))
                split(tmp[:], x_hi[:, j, :], x_lo[:, j, :])
                dve.wait_ge(x_ready, 24 + j + 1)

            def add_to_residual(banks, when, scale, freed):
                for j in range(KT):
                    dve.wait_ge(w_used, when(j))
                    ins = V.scalar_tensor_tensor(X[:, j, :], banks[j][:], mod[:, scale + j:scale + j + 1],
                                                 X[:, j, :], ALU.mult, ALU.add)
                    if freed(j):
                        ins.then_inc(bank_free, freed(j)[0])
                        dve.wait_ge(bank_free, freed(j)[1])
                    else:
                        st.seq(ins)
                    if j == 0:
                        st.seq(V.tensor_tensor(total[:], X[:, j, :], X[:, j, :], ALU.mult))
                    else:
                        st.seq(V.tensor_tensor(square[:], X[:, j, :], X[:, j, :], ALU.mult))
                        ins = V.tensor_tensor(total[:], total[:], square[:], ALU.add)
                        st.seq(ins) if j < KT - 1 else ins.then_inc(sum_ready, 1)

            u0 = FIRST["w_o"]
            add_to_residual([bank[(u0 + j) % RING] for j in range(8)], lambda j: u0 + j + 1, 16,
                            lambda j: (1, u0 + j + 1 + RING))
            modulated_input(3, 1, 24)
            def ffn_in(phase, gated0, ready):
                u1 = FIRST[phase]
                with st.loop(FT // 2, 2) as i:
                    for j in range(2):
                        dve.wait_ge(gated, i * 2 + (gated0 + j + 1))
                        dve.wait_ge(w_used, i * 4 + (u1 + 2 * j + 2))
                        V.tensor_tensor(tmp[:], bank[(u1 + 2 * j + 1) % RING][:], act_out[:, j, :], ALU.mult
                                        ).then_inc(bank_free, 2)
                        dve.wait_ge(bank_free, i * 4 + (u1 + 2 * j + 2 + RING))
                        m = i * 2 + j
                        st.seq(V.tensor_copy(tile(f_hi, m), tmp[:]))
                        V.tensor_tensor(tile(f_lo, m), tmp[:], tile(f_hi, m).bitcast(F32), ALU.subtract
                                        ).then_inc(x_ready, 1)
                        dve.wait_ge(x_ready, i * 2 + (ready + j + 1))

            def wait_ffn_tile(n, u2, j):
                if j < 4:
                    dve.wait_ge(w_used, u2 + FT // 2)
                elif j < KT - 1:
                    dve.wait_ge(tail_done, 3 * n + j - 3)
                else:
                    dve.wait_ge(w_used, u2 + FT)

            ffn_in("ffn_in", 24, XR["ffn_h"])
            u2 = FIRST["ffn_out"]
            for j in range(KT):
                wait_ffn_tile(0, u2, j)
                V.scalar_tensor_tensor(X[:, j, :], bank[j][:], mod[:, 40 + j:41 + j], X[:, j, :],
                                       ALU.mult, ALU.add).then_inc(x_new, 1)
                if j == KT - 1:
                    dve.wait_ge(x_new, KT)
                    give_back(FT)
                dve.wait_ge(hi_ready, j + 1)
                V.scalar_tensor_tensor(x_lo[:, j, :], X[:, j, :], joint_gain[:, j:j + 1], x_hi[:, j, :].bitcast(F32),
                                       ALU.mult, ALU.subtract).then_inc(x_ready, 1)
                dve.wait_ge(tile_squared, j + 1)
                if j:
                    dve.wait_ge(squares_added, j)
                if j == 0:
                    V.tensor_copy(total[:], act_out[:, 0, :])
                    V.tensor_copy(square[:], act_out[:, 1, :]).then_inc(squares_added, 1)
                elif j < KT - 1:
                    V.tensor_tensor(total[:], total[:], act_out[:, 0, :], ALU.add)
                    V.tensor_tensor(square[:], square[:], act_out[:, 1, :], ALU.add).then_inc(squares_added, 1)
                else:
                    V.tensor_tensor(total[:], total[:], act_out[:, 0, :], ALU.add).then_inc(sum_ready, 1)
                    V.tensor_tensor(square[:], square[:], act_out[:, 1, :], ALU.add).then_inc(sum_ready, 1)

            def ffn_in_scaled(phase, n_rstd, gated0, pair0, ready):
                u1 = FIRST[phase]

                def pairs(i, taken):
                    for j in range(2):
                        a, b = (held[:, 2 * j + n, :] if taken else bank[(u1 + 2 * j + n) % RING][:] for n in range(2))
                        if not taken:
                            dve.wait_ge(w_used, i * 4 + (u1 + 2 * j + 1))
                        V.tensor_tensor(act_out[:, j, :], a, rstd[:], ALU.mult).then_inc(a_scaled, 1)
                        dve.wait_ge(a_scaled, i * 2 + (pair0 + j + 1))
                        if taken:
                            st.seq(V.tensor_tensor(tmp[:], b, rstd[:], ALU.mult))
                        else:
                            dve.wait_ge(w_used, i * 4 + (u1 + 2 * j + 2))
                            V.tensor_tensor(tmp[:], b, rstd[:], ALU.mult).then_inc(bank_free, 2)
                            dve.wait_ge(bank_free, i * 4 + (u1 + 2 * j + 2 + RING))
                        dve.wait_ge(gated, i * 2 + (gated0 + j + 1))
                        st.seq(V.tensor_tensor(tmp[:], tmp[:], act_out[:, j, :], ALU.mult))
                        m = i * 2 + j
                        st.seq(V.tensor_copy(tile(f_hi, m), tmp[:]))
                        V.tensor_tensor(tile(f_lo, m), tmp[:], tile(f_hi, m).bitcast(F32), ALU.subtract
                                        ).then_inc(x_ready, 1)
                        dve.wait_ge(x_ready, i * 2 + (ready + j + 1))

                take_raw(phase, [held[:, j, :] for j in range(RING)])
                dve.wait_ge(rstd_ready, n_rstd)
                pairs(0, True)
                with st.loop(FT // 2 - 1, 4) as i:
                    pairs(i + 1, False)

            def add_tile_square(k, m):
                dve.wait_ge(tile_squared, 8 * k + m + 1)
                if m == 0:
                    ins = V.tensor_copy(total[:], act_out[:, 0, :])
                else:
                    dve.wait_ge(squares_added, 7 * k + m)
                    ins = V.tensor_tensor(total[:], total[:], act_out[:, m % 2, :], ALU.add)
                ins.then_inc(squares_added if m < KT - 1 else sum_ready, 1)

            def residual_and_input(n, k, name, j0, in_name, in_j0, ready, high0):
                dve.wait_ge(rstd_ready, n)
                buf, marks = (tmp, square), {}
                for t in range(KT + 2):
                    if 1 <= t <= KT:
                        m = t - 1
                        st.after(marks[m])
                        V.tensor_tensor(X[:, m, :], X[:, m, :], buf[m % 2][:], ALU.add).then_inc(x_new, 1)
                    if t < KT:
                        if t >= 2:
                            dve.wait_ge(x_new, 8 * k + t - 1)
                        marks[t] = st.step(V.scalar_tensor_tensor(buf[t % 2][:], mix[:, t, :], pcol(name, j0 + t),
                                                                  rstd[:], ALU.mult, ALU.mult))
                    if 1 <= t <= KT:
                        dve.wait_ge(hi_ready, high0 + m + 1)
                        V.scalar_tensor_tensor(x_lo[:, m, :], X[:, m, :], pcol(in_name, in_j0 + m),
                                               x_hi[:, m, :].bitcast(F32), ALU.mult, ALU.subtract
                                               ).then_inc(x_ready, 1)
                    if t >= 2:
                        add_tile_square(k, t - 2)

            def take_mix(k, banks, wait_for, freed):
                for j in range(KT):
                    wait_for(j)
                    V.tensor_copy(mix[:, j, :], banks[j][:]).then_inc(x_new, 1)
                    if freed(j):
                        give_back(freed(j))
                    if j >= 1:
                        add_tile_square(k, j - 1)
                add_tile_square(k, KT - 1)

            def take_mix_units(k, phase):
                u0 = FIRST[phase]
                take_mix(k, [bank[(u0 + j) % RING] for j in range(8)], lambda j: dve.wait_ge(w_used, u0 + j + 1), lambda j: 1)

            def take_mix_ffn(k, phase):
                u2 = FIRST[phase]
                take_mix(k, bank, lambda j: wait_ffn_tile(k // 4 + 1, u2, j), lambda j: FT if j == KT - 1 else 0)

            def take_raw(phase, where):
                for j, t in enumerate(where):
                    dve.wait_ge(w_used, FIRST[phase] + j + 1)
                    V.tensor_copy(t, bank[(FIRST[phase] + j) % RING][:]).then_inc(bank_free, 1)
                dve.wait_ge(bank_free, FIRST[phase] + 2 * RING)

            take_raw("gdn_qkv", [qkv[:, j, :] for j in range(RING)])
            dve.wait_ge(rstd_ready, 4)
            dve.wait_ge(stat_ready, 6)
            st.seq(V.tensor_tensor(tmp[:], bank[6][:], act_out[:, 0, :], ALU.mult))
            V.tensor_tensor(tmp[:], tmp[:], act_out[:, 0, :], ALU.mult).then_inc(rstd_joined, 1)
            dve.wait_ge(rstd_ready, 5)
            V.tensor_tensor(rstd[:], tmp[:], act_out[:, 0, :], ALU.mult).then_inc(rstd_joined, 1)
            dve.wait_ge(rstd_joined, 2)
            u0 = FIRST["gdn_qkv"]

            def qkv_round(i, taken):
                st.seq(V.scalar_tensor_tensor(tile(X, i), tile(X, i), par[:, bass.ds(i + PCOL["final_norm_g"], 1)],
                                              act_out[:, 0, :], ALU.mult, ALU.mult))
                for j in range(4):
                    m = i * 4 + j
                    if taken:
                        st.seq(V.tensor_tensor(prod_pad[:, 3:], tile(qkv, m), rstd[:], ALU.mult))
                    else:
                        dve.wait_ge(w_used, i * 4 + (u0 + j + 1))
                        V.tensor_tensor(prod_pad[:, 3:], bank[(u0 + j) % RING][:], rstd[:], ALU.mult
                                        ).then_inc(bank_free, 1)
                        dve.wait_ge(bank_free, i * 4 + (u0 + j + 1 + RING))
                    *taps, last = conv_taps(prod_pad, tile(qkv, m), tmp[:], "gdn_conv_2", m, 4, counted=False)
                    last.then_inc(silu_in, 1)
                    dve.wait_ge(silu_in, i * 4 + (j + 1))

            qkv_round(0, True)
            with st.loop(5, 4 * 4 + 1) as i:
                qkv_round(i + 1, False)

            for m in (6, 7):
                st.seq(V.scalar_tensor_tensor(X[:, m, :], X[:, m, :], pcol("final_norm_g", m), act_out[:, 0, :],
                                              ALU.mult, ALU.mult))

            def square_head(r, src):
                if r >= 2:
                    dve.wait_ge(sq_summed, r - 1)
                V.tensor_tensor((square, total)[r % 2][:], src, src, ALU.mult).then_inc(sq_ready, 1)

            u0 = FIRST["gdn_z"]
            dt = row[:, 8:16].unsqueeze(1).broadcast_to([P, NCH, HEADS])

            def byhead(n):
                return tok[:, n, :].rearrange("p (c h) -> p c h", h=HEADS)
            dve.wait_ge(w_used, FIRST["gdn_ba"] + 1)
            V.tensor_tensor(tmp[0:16, :], bank[FIRST["gdn_ba"] % RING][0:16, :], rstd[0:16, :], ALU.mult
                            ).then_inc(bank_free, 1)
            dve.wait_ge(inputs_landed, 32)
            dve.wait_ge(silu_out, 24)
            square_head(0, qkv[:, 0, :])
            for j in range(8):
                if j == 0:
                    dve.wait_ge(tok_pe, 1)
                    ba = bank[6][:, 0:64].rearrange("p (c n) -> p c n", n=16)
                    st.step(V.tensor_copy(byhead(0), ba[:, :, 0:8]))
                    st.seq(V.tensor_tensor(byhead(1), ba[:, :, 8:16], dt, ALU.add))
                    V.scalar_tensor_tensor(tok[:, 2, :], tok[:, 1, :], -1.0, tok[:, 1, :], ALU.mult, ALU.max).then_inc(tok_dve, 1)
                if j == 1:
                    dve.wait_ge(tok_act, 1)
                    st.seq(V.tensor_scalar(tok[:, 0, :], tok[:, 0, :], 1.0, None, ALU.add))
                    st.seq(V.reciprocal(tok[:, 0, :], tok[:, 0, :]))
                    st.seq(V.scalar_tensor_tensor(tok[:, 1, :], tok[:, 1, :], 0.0, tok[:, 2, :], ALU.max, ALU.add))
                    ea = tok[:, 3, 0:8].unsqueeze(1).broadcast_to([P, NCH, HEADS])
                    V.scalar_tensor_tensor(byhead(4), byhead(1), -1.0, ea, ALU.mult, ALU.mult).then_inc(tok_dve, 1)
                if j == 4:
                    dve.wait_ge(tok_act, 2)
                    st.seq(V.tensor_copy(tok[:, 8, :], bank[6][:, 64:96]))
                    st.seq(V.scalar_tensor_tensor(tok[:, 9, :], tok[:, 0, :], -1.0, tok[:, 5, :], ALU.mult, ALU.mult))
                    V.tensor_tensor(tok[:, 7, :], bank[6][:, 96:128], tok[:, 8, :], ALU.subtract
                                    ).then_inc(tok_dve, 1)
                dve.wait_ge(w_used, u0 + j + 1)
                V.tensor_tensor(z_gate[:, j, :], bank[(u0 + j) % RING][:], rstd[:], ALU.mult).then_inc(bank_free, 1)
                for r in (2 * j, 2 * j + 1):
                    if r < 15:
                        square_head(r + 1, qkv[:, r + 1, :])
                    dve.wait_ge(head_rstd, r + 1)
                    V.scalar_tensor_tensor(qkv[:, r, :], qkv[:, r, :], DH ** -0.5 if r < HEADS else 1.0,
                                           act_out[:, r % 2, :], ALU.mult, ALU.mult).then_inc(head_rstd_used, 1)
            dve.wait_ge(masks_landed, 32)
            V.tensor_copy(masks[:], masks_raw[:]).then_inc(masks_ready, 1)
            dve.wait_ge(masks_ready, 1)
            dve.wait_ge(tok_act, 3)

            def perhead(n, h):
                return byhead(n)[:, :, h:h + 1].broadcast_to([P, NCH, P])

            def four(b):
                return b[:].rearrange("p (c n) -> p c n", c=NCH)

            def mask4(n):
                return masks[:, n, :].unsqueeze(1).broadcast_to([P, NCH, P])
            ident4 = tri[:, 1, :].unsqueeze(1).broadcast_to([P, NCH, P])

            def chunk_rest(p, c):
                for n in range(2):
                    h, k = 2 * p + n, p * 8 + c * 2 + n
                    dve.wait_ge(ks_ready, k + 1)
                    V.scalar_tensor_tensor(rest_sb[n], bank[n][:, 0:P], tok[:, 9, c * 8 + h:c * 8 + h + 1],
                                           beta_v[(p % 2) * 2 + n][:, c, :], ALU.mult, ALU.add
                                           ).then_inc(rest_ready, 1)

            def chunk_state(p, c):
                for n in range(2):
                    h, k = 2 * p + n, p * 8 + c * 2 + n
                    dve.wait_ge(o_copied, k + 1)
                    V.scalar_tensor_tensor(state[:, n, :], state[:, n, :], tok[:, 6, c * 8 + h:c * 8 + h + 1],
                                           bank[n][:, 3 * P:4 * P], ALU.mult, ALU.add).then_inc(state_ready, 1)

            sq4 = square[:].rearrange("p (c n) -> p c n", c=NCH)

            def differences(h):
                dve.wait_ge(decay_row, h + 1)
                if h:
                    dve.wait_ge(decay_ready, h)
                st.seq(V.tensor_tensor(sq4, four(bank[0]), perhead(8, h), ALU.subtract))
                V.tensor_tensor(sq4, sq4, mask4(0), ALU.add).then_inc(diff_ready, 1)

            def take_products(h):
                p, n, slot = h // 2, h % 2, h % 4
                dec4 = act_out[:, n, :].rearrange("p (c n) -> p c n", c=NCH)
                dve.wait_ge(head_products, 4 * h + 4)
                st.seq(V.tensor_tensor(qkv[:, h, :], qkv[:, h, :], rstd[:], ALU.mult))
                dve.wait_ge(decay_ready, h + 1)
                V.tensor_tensor(attn[slot][:], four(bank[3]), dec4, ALU.mult)
                if p:
                    dve.wait_ge(level_ready, p * 14)
                    dve.wait_ge(first_half, p * 14 - 4 + n + 1)
                st.seq(V.tensor_tensor(lower_t[n][:], four(bank[2]), dec4, ALU.mult))
                V.tensor_tensor(lower_t[n][:], lower_t[n][:], four(bank[1]), ALU.mult).then_inc(head_taken, 1)
                dve.wait_ge(head_taken, h + 1)
                V.tensor_tensor(level_a[n][p % 2][:], lower_t[n][:], mask4(1), ALU.mult).then_inc(level_ready, 1)

            def scale_output(h):
                dve.wait_ge(head_rstd, 17 + h)
                if h >= 2:
                    dve.wait_ge(x_ready, XR["gdn_o"] + h - 1)
                V.scalar_tensor_tensor(outs[h % 2], qkv[:, 16 + h, :], pcol("gdn_out_norm_2", 0), act_out[:, h % 2, :],
                                       ALU.mult, ALU.mult).then_inc(head_rstd_used, 1)

            def gate_output(h):
                dve.wait_ge(z_ready, 1)
                dve.wait_ge(head_rstd_used, 17 + h)
                st.seq(V.tensor_tensor(outs[h % 2], outs[h % 2], z_gate[:, h, :], ALU.mult))
                split(outs[h % 2], og_hi[:, h, :], og_lo[:, h, :])

            for h in range(2):
                differences(h)
                take_products(h)
            for p in range(HEADS // 2 + 1):
                if p >= 1:
                    for n in range(2):
                        V.memset(state[:, n, :], 0.0).then_inc(state_ready, 1)
                for lv in range(LEVELS):
                    if p < HEADS // 2 and lv + 1 < LEVELS:
                        for n in range(2):
                            if lv >= 1 or p >= 1:
                                dve.wait_ge(first_half, p * 14 + (lv - 1) * 2 + n + 1)
                            V.tensor_tensor(level_a[n][(p + lv + 1) % 2][:], lower_t[n][:], mask4(2 + lv), ALU.mult
                                            ).then_inc(level_ready, 1)
                    if p + 1 < HEADS // 2:
                        if lv == LEVELS - 3:
                            differences(2 * p + 2)
                        if lv >= LEVELS - 2:
                            take_products(2 * p + 2 + lv - (LEVELS - 2))
                    if p >= 1 and lv < NCH:
                        chunk_rest(p - 1, lv)
                    if p == HEADS // 2:
                        if 1 <= lv < HEADS // 2:
                            scale_output(2 * lv - 2)
                            scale_output(2 * lv - 1)
                        if lv < HEADS // 2 - 1:
                            for h in (2 * lv, 2 * lv + 1):
                                dve.wait_ge(o_copied, 8 * (HEADS // 2 - 1))
                                square_head(16 + h, qkv[:, 16 + h, :])
                    if p < HEADS // 2:
                        for n in range(2):
                            slot = (p % 2) * 2 + n
                            if lv == 0:
                                dve.wait_ge(level_ready, p * 14 + n + 1)
                                st.seq(V.tensor_tensor(inv_t[slot][:], ident4, level_a[n][p % 2][:], ALU.subtract))
                                dve.wait_ge(first_half, p * 14 + n + 1)
                                V.tensor_tensor(inv[n][:], ident4, four(bank[4 + 2 * n]), ALU.subtract
                                                ).then_inc(inverse_ready, 1)
                            else:
                                dve.wait_ge(second_half, p * 12 + (lv - 1) * 2 + n + 1)
                                for t, side in ((inv[n], 0), (inv_t[slot], 1)):
                                    if side == 0 and lv == LEVELS - 1:
                                        continue
                                    t = blocks(t[:], lv, side)
                                    y = bank[4 + 2 * n + side][:, 0:T // 2].rearrange("p (g n) -> p g n", n=2 ** lv)
                                    ins = V.tensor_tensor(t, t, y, ALU.subtract)
                                ins.then_inc(inverse_ready, 1)
                        if p + 1 < HEADS // 2 and lv == LEVELS - 2:
                            differences(2 * p + 3)
                        if lv in (0, 1):
                            h, slot = 2 * p + lv, (p % 2) * 2 + lv
                            dve.wait_ge(turned, 2 * h + 1)
                            V.tensor_tensor(beta_v[slot][:], four(bank[2]), perhead(0, h), ALU.mult
                                            ).then_inc(turned_used, 1)
                            dve.wait_ge(turned, 2 * h + 2)
                            V.tensor_tensor(key_dec[slot][:], four(bank[3]), perhead(7, h), ALU.mult
                                            ).then_inc(turned_used, 1)
                    if p >= 1 and lv < NCH:
                        chunk_state(p - 1, lv)
            dve.wait_ge(o_copied, 8 * (HEADS // 2))
            for h in (HEADS - 2, HEADS - 1):
                square_head(16 + h, qkv[:, 16 + h, :])
            for h in (HEADS - 2, HEADS - 1):
                scale_output(h)
            dve.wait_ge(x_ready, XR["gdn_o"] + HEADS - 2)
            for h in (HEADS - 2, HEADS - 1):
                gate_output(h)
            take_mix_units(1, "gdn_out")
            residual_and_input(6, 2, "post_mix_norm_2", 0, "pre_ffn_norm_2", 0, XR["ffn_x_a"], 8)
            ffn_in_scaled("ffn_in_a", 7, 24 + FT, 0, XR["ffn_h_a"])
            take_mix_ffn(3, "ffn_out_a")
            residual_and_input(8, 4, "post_ffn_norm_2", 0, "kv_norm_2", 0, XR["kv_x"], 16)
            take_raw("fox_k", [kf[:, j, :] for j in range(RING)])
            dve.wait_ge(rstd_ready, 9)
            for j in range(RING):
                st.step(V.tensor_tensor(kf[:, j, :], kf[:, j, :], rstd[:], ALU.mult))
            for m in range(KT):
                dve.wait_ge(hi_ready, 24 + m + 1)
                V.scalar_tensor_tensor(q_lo[:, m, :], X[:, m, :], pcol("pre_mix_norm_2", 8 + m),
                                       q_hi[:, m, :].bitcast(F32), ALU.mult, ALU.subtract).then_inc(x_ready, 1)
            u0 = FIRST["fox_k"]
            for j in range(RING, 8):
                dve.wait_ge(w_used, u0 + j + 1)
                V.tensor_tensor(kf[:, j, :], bank[(u0 + j) % RING][:], rstd[:], ALU.mult).then_inc(bank_free, 1)
            f, part = tmp[0:16, :], square[0:16, :]
            dve.wait_ge(w_used, FIRST["fox_f"] + 1)
            V.tensor_tensor(f, bank[FIRST["fox_f"] % RING][0:16, :], rstd[0:16, :], ALU.mult).then_inc(bank_free, 1)
            dve.wait_ge(bank_free, FIRST["fox_v"] + RING)
            st.seq(V.tensor_scalar(f, f, par[0:16, PCOL["b_forget_2"]:PCOL["b_forget_2"] + 1], None, ALU.add))
            dve.wait_ge(tok_pe, 3)
            V.tensor_copy(tok[:, 12, 0:4], bank[6][:, 0:4])
            V.scalar_tensor_tensor(part, f, -1.0, f, ALU.mult, ALU.max).then_inc(tok_dve, 1)
            dve.wait_ge(tok_dve, 4)
            st.seq(V.tensor_scalar(f, f, -1.0, 0.0, ALU.mult, ALU.max))
            dve.wait_ge(tok_act, 4)
            V.tensor_tensor(f, f, part, ALU.add).then_inc(tok_dve, 1)
            u0 = FIRST["fox_v"]
            for hv in range(2):
                dve.wait_ge(w_used, u0 + 4 * (hv + 1))
                for t in range(QB):
                    V.tensor_scalar(vt[:, t, bass.ts(hv, T)], bank[4 * hv + t][:], tok[:, 12, t:t + 1], None,
                                    ALU.mult).then_inc(v_free, 1)
                if hv == 0:
                    dve.wait_ge(v_free, 4)
                    give_back(8)
            u0 = FIRST["fox_q"]
            for j in range(8):
                dve.wait_ge(w_used, u0 + j + 1)
                V.scalar_tensor_tensor(qf[:, j, :], bank[(u0 + j) % RING][:], FOX_D ** -0.5, rstd[:],
                                       ALU.mult, ALU.mult).then_inc(bank_free, 1)
            dve.wait_ge(masks_landed, 48)
            V.tensor_copy(masks[:], masks_raw[:]).then_inc(masks_ready, 1)
            dve.wait_ge(tok_dve, 5)
            st.seq(V.memset(square[0:16, :], 1.0))
            V.tensor_tensor_scan(forget_sum[:], square[0:16, :], tmp[0:16, :], 0.0, ALU.mult, ALU.add
                                 ).then_inc(tok_dve, 1)
            dve.wait_ge(masks_ready, 2)
            STEPS = FOX_HEADS * QB

            def take_heads(t):
                dve.wait_ge(pv_done, 8 * (t + 1))
                o = bank[5 + t % 2][:]
                st.seq(V.tensor_copy(q_hi[:, t, :], o))
                V.tensor_tensor(q_lo[:, t, :], o, q_hi[:, t, :].bitcast(F32), ALU.subtract).then_inc(x_ready, 1)

            for s in range(STEPS + 1):
                if s < STEPS:
                    h, b = s // QB, s % QB
                    e = (b + 1) * P
                    if b == 0:
                        dve.wait_ge(forget_row, h + 1)
                        V.tensor_copy(forget[h % 2][:], bank[7][:]).then_inc(forget_copied, 1)
                        dve.wait_ge(forget_copied, h + 1)
                    dve.wait_ge(scores_done, s + 1)
                    if s >= 2:
                        dve.wait_ge(exp_done, s - 1)
                    V.tensor_tensor_reduce(out=score[s % 2][:, 0:e], in0=bank[s % 3][:, 0:e],
                                           in1=forget[h % 2][:, 0:e], scale=-1.0, scalar=3e38, op0=ALU.add,
                                           op1=ALU.min, accum_out=softmax[:, s % 2, 0:1]).then_inc(scores_taken, 1)
                if s >= 1:
                    s1 = s - 1
                    h1, e = s1 // QB, (s1 % QB + 1) * P
                    q = softmax[:, s1 % 2, :]
                    dve.wait_ge(exp_done, s1 + 1)
                    st.seq(V.reciprocal(q[:, 2:3], q[:, 1:2]))
                    V.tensor_scalar(prob[s1 % 2][:, 0:e], prob[s1 % 2][:, 0:e], q[:, 2:3], None, ALU.mult
                                    ).then_inc(prob_ready, 1)
                if s >= 12 and (s - 12) % 8 == 0:
                    take_heads((s - 12) // 8)
            take_heads(7)
            take_mix_units(5, "fox_o")
            residual_and_input(10, 6, "post_mix_norm_2", 8, "pre_ffn_norm_2", 8, XR["ffn_x_b"], 32)
            ffn_in_scaled("ffn_in_b", 11, 24 + 2 * FT, FT, XR["ffn_h_b"])
            take_mix_ffn(7, "ffn_out_b")
            dve.wait_ge(rstd_ready, 12)
            buf, marks = (tmp, square), {}
            for t in range(KT + 1):
                if t < KT:
                    if t >= 2:
                        dve.wait_ge(out_ready, t - 1)
                    marks[t] = st.step(V.scalar_tensor_tensor(buf[t % 2][:], mix[:, t, :],
                                                              pcol("post_ffn_norm_2", 8 + t), rstd[:],
                                                              ALU.mult, ALU.mult))
                if t >= 1:
                    st.after(marks[t - 1])
                    V.tensor_tensor(X[:, t - 1, :], X[:, t - 1, :], buf[(t - 1) % 2][:], ALU.add
                                    ).then_inc(out_ready, 1)


def unit_tiles(w):
    return w.reshape(KT, P, -1, P).transpose(2, 1, 0, 3).reshape(-1, P, UNIT)


def narrow_unit(w):
    return unit_tiles(np.pad(w, ((0, 0), (0, P - w.shape[1]))))


def ffn_out_units(w):
    return w.reshape(FT // 2, 2, P, 2, 4, P).transpose(3, 0, 2, 1, 4, 5).reshape(-1, P, UNIT)


def paired(*parts):
    return np.stack(parts, axis=1).reshape(-1, P, UNIT)


def columns(v, name):
    v = v.reshape(-1, v.shape[-1] // P, P)
    v = v.transpose(2, 1, 0) if "conv_" in name and not name.endswith("_b") or name == "gdn_conv_2" \
        else v.transpose(2, 0, 1)
    return v.reshape(P, -1)


def constant_tiles():
    a, b = np.arange(P)[:, None], np.arange(P)[None, :]
    tiles = [a <= b, a == b, np.where(a <= b, 0.0, -1e30)]
    for lv in range(LEVELS):
        n = 2 ** lv
        tiles.append((a // (2 * n) == b // (2 * n)) & (a // n % 2 == 0) & (b // n % 2 == 1))
    tiles += [a == b, np.where(a >= b, 0.0, -1e30)]
    return np.ascontiguousarray(np.stack([t.astype(np.float32) for t in tiles]).transpose(1, 0, 2))


def kernel(**inputs):
    import concourse.bacc as _bacc
    from concourse.bass_utils import run_bass_kernel_spmd as _run

    a = {k: np.asarray(v) for k, v in inputs.items()}
    w_in = unit_tiles(a["w_in"][0])
    b_u, c_u, v_u, vc_u, gl_u, ga_u, gb_u = (w_in[8 * n:8 * n + 8] for n in range(7))
    ffn = unit_tiles(a["w_ffn_in"][0])
    gdn = a["gdn_w_in_2"][0]
    ffn_2 = []
    for n in range(2):
        f = unit_tiles(a["w_ffn_in_2"][n])
        ffn_2.append((paired(f[:FT], f[FT:]), ffn_out_units(a["w_ffn_out_2"][n])))
    weights = np.concatenate([
        paired(vc_u, gl_u), paired(c_u, v_u, b_u), paired(unit_tiles(a["w_short_out"][0]), ga_u), gb_u,
        unit_tiles(a["w_conf_out"][0]), unit_tiles(a["w_o"][0]), paired(ffn[:FT], ffn[FT:]),
        ffn_out_units(a["w_ffn_out"][0]),
        unit_tiles(gdn[:, :3072]), narrow_unit(gdn[:, 4096:]), unit_tiles(gdn[:, 3072:4096]),
        unit_tiles(a["gdn_w_out_2"][0]), *ffn_2[0],
        unit_tiles(a["w_kv_2"][:, :1024]), narrow_unit(a["w_kv_2"][:, 2048:]),
        a["w_kv_2"][:, 1024:2048].reshape(4, 2, P, 2, T).transpose(3, 0, 2, 1, 4).reshape(-1, P, UNIT),
        unit_tiles(a["fox_w_q_2"][0]), unit_tiles(a["fox_w_o_2"][0]), *ffn_2[1]])
    rows = np.concatenate([a["gdn_a_log_2"].ravel(), a["gdn_dt_bias_2"].ravel()]).reshape(1, 16)
    a["b_forget_2"] = np.pad(a["b_forget_2"], (0, P - FOX_HEADS))
    params = np.concatenate([columns(a[name], name) for name, _ in PARAMS], axis=1)
    ada = np.ascontiguousarray(a["w_ada"][0].reshape(KT, P, ADA_CHUNKS, ADA_COLS).transpose(2, 1, 0, 3))
    arrays = {"x_t": np.ascontiguousarray(a["x"][0].T), "params": np.ascontiguousarray(params),
              "weights": np.ascontiguousarray(weights), "ada": ada,
              "rows": rows, "consts": constant_tiles()}
    nc = _bacc.Bacc("TRN2", target_bir_lowering=False, num_devices=1)
    args = [nc.dram_tensor(n, v.shape, F32, kind="ExternalInput").ap() for n, v in arrays.items()]
    out = nc.dram_tensor("out_t", (D, T), F32, kind="ExternalOutput").ap()
    program(nc, *args, out)
    r = _run(nc, [arrays], core_ids=[0])
    return r.results[0]["out_t"].T.reshape(1, T, D)
```
